# Optimizing a Trainium2 kernel written in Bass

```python
import math
import jax
import jax.numpy as jnp
from jax import lax
import numpy as np

D_MODEL = 1024
BATCH = 1
SEQ = 1024
DEPTH = 1

GRID_W = 64
CTX_LEN = 256
N_BRANCH = 4
CONF_D = 512
CONF_K = 31
SSD_D = 768
SSD_HEADS = 12
SSD_HEAD_DIM = 64
SSD_GROUPS = 4
SSD_HPG = SSD_HEADS // SSD_GROUPS
SSD_STATE = 128
SSD_CONV_K = 3
SSD_CHUNK = 128
SSD_BC = SSD_GROUPS * SSD_STATE
SSD_XBC = SSD_D + 2 * SSD_BC
SSD_PROJ = SSD_D + SSD_XBC + 2 * SSD_HEADS
HY_D = 512
HY_ORDER = 2
HY_SHORT_K = 3
HY_EMB = 33
HY_BANDS = (HY_EMB - 1) // 2
HY_HID = 64
HY_N_FILT = HY_ORDER * 2 * HY_D
HY_MIN_DECAY = math.log(1e-2) / 1.5
HY_MAX_DECAY = math.log(1e-2) / 0.3
SC_D = 512
SC_K = 3
OFF_A = 0
OFF_B = OFF_A + 2 * CONF_D
OFF_C = OFF_B + SSD_PROJ
OFF_D = OFF_C + 3 * HY_D
OFF_G = OFF_D + 3 * SC_D
PROJ_TOTAL = OFF_G + N_BRANCH * D_MODEL
MOE_GROUPS = 4
MOE_EPG = 8
MOE_EXPERTS = MOE_GROUPS * MOE_EPG
MOE_TOP_K = 2
MOE_FF = 512
MOE_BLOCK = 128
DN_ALPHA = (2 * DEPTH) ** 0.25
DN_BETA = (8 * DEPTH) ** -0.25
LN_EPS = 1e-5
F32 = jnp.float32

kernel_name = "hybrid_conv_ssd_hyena_moe_diffusion_block"

def layer_norm(x, g, b):
    xf = x.astype(F32)
    mu = jnp.mean(xf, -1, keepdims=True)
    var = jnp.mean(jnp.square(xf - mu), -1, keepdims=True)
    return ((xf - mu) * lax.rsqrt(var + LN_EPS) * g.astype(F32) + b.astype(F32)).astype(x.dtype)

def rms_norm(x, g):
    xf = x.astype(F32)
    return (xf * lax.rsqrt(jnp.mean(jnp.square(xf), -1, keepdims=True) + LN_EPS) * g.astype(F32)).astype(x.dtype)

def modulate(h, shift, scale):
    return h * (1 + scale) + shift

def dwconv_seq(x, w):
    k = w.shape[0]
    return lax.conv_general_dilated(x, w[:, None, :].astype(x.dtype), window_strides=(1,), padding=((k // 2, k // 2),), dimension_numbers=("NWC", "WIO", "NWC"), feature_group_count=x.shape[-1])

def dwconv_grid_cols(x, w, rows):
    bsz, n, ch = x.shape
    k = w.shape[0]
    y = lax.conv_general_dilated(x.reshape(bsz, rows, GRID_W, ch), w[:, None, None, :].astype(x.dtype), window_strides=(1, 1), padding=((k // 2, k // 2), (0, 0)), dimension_numbers=("NHWC", "HWIO", "NHWC"), feature_group_count=ch)
    return y.reshape(bsz, n, ch)

def conformer_branch(p_a, lp, rows):
    val, gate = jnp.split(p_a, 2, axis=-1)
    v = val * jax.nn.sigmoid(gate)
    v = dwconv_seq(v, lp["conf_dw_w"]) if rows is None else dwconv_grid_cols(v, lp["conf_dw_w"], rows)
    v = layer_norm(v + lp["conf_dw_b"], lp["conf_ln_g"], lp["conf_ln_b"])
    return jax.nn.silu(v)

def ssd_prepare(p_b, lp):
    bsz, n = p_b.shape[:2]
    z = p_b[..., :SSD_D]
    xbc = jax.nn.silu(dwconv_seq(p_b[..., SSD_D:SSD_D + SSD_XBC], lp["ssd_conv_w"]) + lp["ssd_conv_b"])
    xs = xbc[..., :SSD_D].reshape(bsz, n, SSD_GROUPS, SSD_HPG, SSD_HEAD_DIM)
    b_in = xbc[..., SSD_D:SSD_D + SSD_BC].reshape(bsz, n, SSD_GROUPS, SSD_STATE)
    c_out = xbc[..., SSD_D + SSD_BC:].reshape(bsz, n, SSD_GROUPS, SSD_STATE)
    dt_raw = p_b[..., SSD_D + SSD_XBC:].astype(F32).reshape(bsz, n, 2, SSD_HEADS)
    dt = jax.nn.softplus(dt_raw + lp["ssd_dt_bias"].astype(F32))
    a_rate = -jnp.exp(lp["ssd_a_log"].astype(F32))
    return z, xs, b_in, c_out, dt, a_rate

def _ssd_direction(xs, b_in, c_out, dt, a_rate, d):
    bsz, n = xs.shape[:2]
    dt_d = dt[:, :, d].reshape(bsz, n, SSD_GROUPS, SSD_HPG)
    log_decay = dt_d * a_rate[d].reshape(SSD_GROUPS, SSD_HPG)
    xdt = xs * dt_d[..., None].astype(xs.dtype)
    if d == 1:
        xdt, log_decay, b_in, c_out = (jnp.flip(t, axis=1) for t in (xdt, log_decay, b_in, c_out))
    return xdt, log_decay, b_in, c_out

def _ssd_blocks(xdt, log_decay, b_in):
    bsz, n = xdt.shape[:2]
    nc = n // SSD_CHUNK
    xc = xdt.reshape(bsz, nc, SSD_CHUNK, SSD_GROUPS, SSD_HPG, SSD_HEAD_DIM)
    a_cum = jnp.cumsum(log_decay.reshape(bsz, nc, SSD_CHUNK, SSD_GROUPS, SSD_HPG), axis=2).transpose(0, 3, 4, 1, 2)
    bc = b_in.reshape(bsz, nc, SSD_CHUNK, SSD_GROUPS, SSD_STATE)
    return xc, a_cum, bc

def _ssd_chunk_states(xc, a_cum, bc, init):
    decay_to_end = jnp.exp(a_cum[..., -1:] - a_cum)
    chunk_states = jnp.einsum("bclgn,bgecl,bclgep->cbgepn", bc.astype(F32), decay_to_end, xc.astype(F32))
    chunk_decay = jnp.moveaxis(jnp.exp(a_cum[..., -1]), -1, 0)[..., None, None]

    def step(h, inp):
        dec, s = inp
        return dec * h + s, h

    final, h_in = lax.scan(step, init, (chunk_decay, chunk_states))
    return h_in, final

def ssd_scan(xdt, log_decay, b_in, c_out, init):
    xc, a_cum, bc = _ssd_blocks(xdt, log_decay, b_in)
    cc = c_out.reshape(bc.shape).astype(F32)
    h_in, final = _ssd_chunk_states(xc, a_cum, bc, init)
    lower = jnp.tril(jnp.ones((SSD_CHUNK, SSD_CHUNK), dtype=bool))
    decay_in = jnp.exp(jnp.where(lower, a_cum[..., :, None] - a_cum[..., None, :], -jnp.inf))
    cb = jnp.einsum("bclgn,bcsgn->bgcls", cc, bc.astype(F32))
    y_diag = jnp.einsum("bgcls,bgecls,bcsgep->bclgep", cb, decay_in, xc.astype(F32))
    y_off = jnp.einsum("bclgn,cbgepn,bgecl->bclgep", cc, h_in, jnp.exp(a_cum))
    return (y_diag + y_off).reshape(xdt.shape).astype(xdt.dtype), final

def ssd_branch(p_b, init, lp):
    z, xs, b_in, c_out, dt, a_rate = ssd_prepare(p_b, lp)
    y = xs * lp["ssd_d"].reshape(SSD_GROUPS, SSD_HPG, 1).astype(xs.dtype)
    finals = []
    for d in range(2):
        xdt, log_decay, b_d, c_d = _ssd_direction(xs, b_in, c_out, dt, a_rate, d)
        y_d, f_d = ssd_scan(xdt, log_decay, b_d, c_d, init[d])
        y = y + (jnp.flip(y_d, axis=1) if d == 1 else y_d)
        finals.append(f_d)
    y = y.reshape(z.shape)
    return rms_norm(y * jax.nn.silu(z), lp["ssd_norm_g"]), jnp.stack(finals)

def ssd_context_states(p_b, init, lp):
    _, xs, b_in, c_out, dt, a_rate = ssd_prepare(p_b, lp)
    finals = []
    for d in range(2):
        xdt, log_decay, b_d, _ = _ssd_direction(xs, b_in, c_out, dt, a_rate, d)
        xc, a_cum, bc = _ssd_blocks(xdt, log_decay, b_d)
        finals.append(_ssd_chunk_states(xc, a_cum, bc, init[d])[1])
    return jnp.stack(finals)

def hyena_filters(n, lp):
    t01 = jnp.linspace(0.0, 1.0, n, dtype=F32)[:, None]
    omega = (2.0 * math.pi / n) * jnp.arange(n, dtype=F32)[:, None]
    bands = jnp.linspace(1e-4, HY_BANDS - 1, HY_BANDS, dtype=F32)
    feat = jnp.concatenate([t01, jnp.cos(bands * omega), -jnp.sin(bands * omega)], axis=-1)
    hid = jnp.sin(lp["hy_freq"][0].astype(F32) * (feat @ lp["hy_w1"].astype(F32) + lp["hy_b1"].astype(F32)))
    hid = jnp.sin(lp["hy_freq"][1].astype(F32) * (hid @ lp["hy_w2"].astype(F32) + lp["hy_b2"].astype(F32)))
    deltas = jnp.abs(jnp.linspace(HY_MIN_DECAY, HY_MAX_DECAY, HY_N_FILT, dtype=F32))
    filt = (hid @ lp["hy_w3"].astype(F32)) * jnp.exp(-t01 * deltas)
    filt = filt.reshape(n, HY_ORDER, 2, HY_D)
    fwd, bwd = filt[:, :, 0], filt[:, :, 1]
    k2 = jnp.concatenate([fwd, jnp.zeros((1, HY_ORDER, HY_D), F32), jnp.flip(bwd[1:], axis=0)], axis=0)
    return k2 / jnp.sum(jnp.abs(k2), axis=0, keepdims=True)

def fft_conv(z, k2):
    n = z.shape[1]
    zf = jnp.fft.rfft(z, n=2 * n, axis=1)
    kf = jnp.fft.rfft(k2, axis=0)
    return jnp.fft.irfft(zf * kf[None], n=2 * n, axis=1)[:, :n]

def hyena_branch(p_c, lp):
    q = dwconv_seq(p_c, lp["hy_short_w"]) + lp["hy_short_b"]
    v, x1, x2 = jnp.split(q, 3, axis=-1)
    k2 = hyena_filters(p_c.shape[1], lp)
    z = v.astype(F32)
    for o, gate in enumerate((x1, x2)):
        z = gate.astype(F32) * (fft_conv(z, k2[:, o]) + lp["hy_bias"][o].astype(F32) * z)
    return z.astype(p_c.dtype)

def short_conv_branch(p_d, lp):
    bg, cg, xv = jnp.split(p_d, 3, axis=-1)
    return bg * dwconv_seq(cg * xv, lp["sc_conv_w"])

def token_mixer(u, ssd_init, lp, rows):
    p = u @ lp["w_in"]
    y_a = conformer_branch(p[..., OFF_A:OFF_B], lp, rows)
    y_b, ssd_final = ssd_branch(p[..., OFF_B:OFF_C], ssd_init, lp)
    y_c = hyena_branch(p[..., OFF_C:OFF_D], lp)
    y_d = short_conv_branch(p[..., OFF_D:OFF_G], lp)
    gates = jax.nn.sigmoid(p[..., OFF_G:]).reshape(*u.shape[:-1], N_BRANCH, D_MODEL)
    merged = (gates[..., 0, :] * (y_a @ lp["w_branch_a"]) + gates[..., 1, :] * (y_b @ lp["w_branch_b"])
              + gates[..., 2, :] * (y_c @ lp["w_branch_c"]) + gates[..., 3, :] * (y_d @ lp["w_branch_d"]))
    return merged @ lp["w_out"], ssd_final

def moe_ffn(u, lp):
    shp = u.shape
    tok = u.reshape(-1, D_MODEL)
    n_tok = tok.shape[0]
    g_logits = (tok @ lp["rt_group_w"] + lp["rt_group_b"]).astype(F32)
    g_sel = jnp.argmax(g_logits, axis=-1).astype(jnp.int32)
    g_prob = jnp.take_along_axis(jax.nn.softmax(g_logits, axis=-1), g_sel[:, None], axis=-1)
    e_logits = (tok @ lp["rt_expert_w"] + lp["rt_expert_b"]).astype(F32).reshape(n_tok, MOE_GROUPS, MOE_EPG)
    e_logits = jnp.take_along_axis(e_logits, g_sel[:, None, None], axis=1)[:, 0]
    top_v, top_i = lax.top_k(e_logits, MOE_TOP_K)
    weights = jax.nn.softmax(top_v, axis=-1) * g_prob
    expert = g_sel[:, None] * MOE_EPG + top_i.astype(jnp.int32)
    n_assign = n_tok * MOE_TOP_K
    flat_e = expert.reshape(n_assign)
    order = jnp.argsort(flat_e)
    sorted_e = flat_e[order]
    counts = jnp.bincount(flat_e, length=MOE_EXPERTS)
    padded = (counts + MOE_BLOCK - 1) // MOE_BLOCK * MOE_BLOCK
    pad_end = jnp.cumsum(padded)
    pad_start = pad_end - padded
    start = jnp.cumsum(counts) - counts
    dest = pad_start[sorted_e] + jnp.arange(n_assign, dtype=jnp.int32) - start[sorted_e]
    n_blocks = (n_assign + MOE_EXPERTS * (MOE_BLOCK - 1) + MOE_BLOCK - 1) // MOE_BLOCK
    n_rows = n_blocks * MOE_BLOCK
    row_tok = jnp.full((n_rows,), n_tok, jnp.int32).at[dest].set((order // MOE_TOP_K).astype(jnp.int32))
    row_w = jnp.zeros((n_rows,), F32).at[dest].set(weights.reshape(n_assign)[order])
    block_e = jnp.minimum(jnp.searchsorted(pad_end, jnp.arange(n_blocks, dtype=jnp.int32) * MOE_BLOCK, side="right"), MOE_EXPERTS - 1)
    tok_pad = jnp.concatenate([tok, jnp.zeros((1, D_MODEL), tok.dtype)], axis=0)
    xin = tok_pad[row_tok].reshape(n_blocks, MOE_BLOCK, D_MODEL)

    def expert_block(args):
        xb, e = args
        hid = jax.nn.silu(xb @ lp["ex_w_gate"][e]) * (xb @ lp["ex_w_up"][e])
        return hid @ lp["ex_w_down"][e]

    y = lax.map(expert_block, (xin, block_e)).reshape(n_rows, D_MODEL)
    out = jnp.zeros((n_tok + 1, D_MODEL), F32).at[row_tok].add(y * row_w[:, None])
    return out[:n_tok].astype(u.dtype).reshape(shp)

def setup_inputs(seed: int = 0) -> dict:
    key = jax.random.key(seed)
    ks = iter(jax.random.split(key, 64))

    def nrm(shape, scale):
        return scale * jax.random.normal(next(ks), shape, F32)

    L = DEPTH
    dt0 = jnp.exp(jax.random.uniform(next(ks), (L, 2, SSD_HEADS), F32, math.log(1e-3), math.log(1e-1)))
    a0 = jax.random.uniform(next(ks), (L, 2, SSD_HEADS), F32, 1.0, 16.0)
    return {
        "x": nrm((BATCH, SEQ, D_MODEL), 1.0),
        "c": nrm((BATCH, D_MODEL), 1.0),
        "ctx": nrm((BATCH, CTX_LEN, D_MODEL), 1.0),
        "c_ctx": nrm((D_MODEL,), 1.0),
        "w_mod": nrm((L, D_MODEL, 6 * D_MODEL), D_MODEL ** -0.5),
        "b_mod": nrm((L, 6 * D_MODEL), 0.01),
        "ln_g": 1.0 + nrm((L, 2, D_MODEL), 0.01),
        "ln_b": nrm((L, 2, D_MODEL), 0.01),
        "w_in": nrm((L, D_MODEL, PROJ_TOTAL), D_MODEL ** -0.5),
        "conf_dw_w": nrm((L, CONF_K, CONF_D), CONF_K ** -0.5),
        "conf_dw_b": nrm((L, CONF_D), 0.01),
        "conf_ln_g": 1.0 + nrm((L, CONF_D), 0.01),
        "conf_ln_b": nrm((L, CONF_D), 0.01),
        "ssd_conv_w": nrm((L, SSD_CONV_K, SSD_XBC), SSD_CONV_K ** -0.5),
        "ssd_conv_b": nrm((L, SSD_XBC), 0.01),
        "ssd_a_log": jnp.log(a0),
        "ssd_dt_bias": dt0 + jnp.log(-jnp.expm1(-dt0)),
        "ssd_d": 1.0 + nrm((L, SSD_HEADS), 0.01),
        "ssd_norm_g": 1.0 + nrm((L, SSD_D), 0.01),
        "hy_short_w": nrm((L, HY_SHORT_K, 3 * HY_D), HY_SHORT_K ** -0.5),
        "hy_short_b": nrm((L, 3 * HY_D), 0.01),
        "hy_w1": nrm((L, HY_EMB, HY_HID), HY_EMB ** -0.5),
        "hy_b1": nrm((L, HY_HID), 0.1),
        "hy_w2": nrm((L, HY_HID, HY_HID), HY_HID ** -0.5),
        "hy_b2": nrm((L, HY_HID), 0.1),
        "hy_freq": 1.0 + nrm((L, 2, HY_HID), 0.01),
        "hy_w3": nrm((L, HY_HID, HY_N_FILT), HY_HID ** -0.5),
        "hy_bias": nrm((L, HY_ORDER, HY_D), 0.1),
        "sc_conv_w": nrm((L, SC_K, SC_D), SC_K ** -0.5),
        "w_branch_a": nrm((L, CONF_D, D_MODEL), CONF_D ** -0.5),
        "w_branch_b": nrm((L, SSD_D, D_MODEL), SSD_D ** -0.5),
        "w_branch_c": nrm((L, HY_D, D_MODEL), HY_D ** -0.5),
        "w_branch_d": nrm((L, SC_D, D_MODEL), SC_D ** -0.5),
        "w_out": nrm((L, D_MODEL, D_MODEL), DN_BETA * D_MODEL ** -0.5),
        "rt_group_w": nrm((L, D_MODEL, MOE_GROUPS), D_MODEL ** -0.5),
        "rt_group_b": nrm((L, MOE_GROUPS), 0.01),
        "rt_expert_w": nrm((L, D_MODEL, MOE_EXPERTS), D_MODEL ** -0.5),
        "rt_expert_b": nrm((L, MOE_EXPERTS), 0.01),
        "ex_w_gate": nrm((L, MOE_EXPERTS, D_MODEL, MOE_FF), D_MODEL ** -0.5),
        "ex_w_up": nrm((L, MOE_EXPERTS, D_MODEL, MOE_FF), D_MODEL ** -0.5),
        "ex_w_down": nrm((L, MOE_EXPERTS, MOE_FF, D_MODEL), DN_BETA * MOE_FF ** -0.5),
    }

def reference(x, c, ctx, c_ctx, w_mod, b_mod, ln_g, ln_b, w_in, conf_dw_w, conf_dw_b, conf_ln_g, conf_ln_b,
              ssd_conv_w, ssd_conv_b, ssd_a_log, ssd_dt_bias, ssd_d, ssd_norm_g, hy_short_w, hy_short_b,
              hy_w1, hy_b1, hy_w2, hy_b2, hy_freq, hy_w3, hy_bias, sc_conv_w, w_branch_a, w_branch_b,
              w_branch_c, w_branch_d, w_out, rt_group_w, rt_group_b, rt_expert_w, rt_expert_b,
              ex_w_gate, ex_w_up, ex_w_down):
    bsz, n_lat, _ = x.shape
    rows = n_lat // GRID_W
    ssd_zero = jnp.zeros((2, bsz, SSD_GROUPS, SSD_HPG, SSD_HEAD_DIM, SSD_STATE), F32)
    h_lat, h_ctx = x, ctx
    for l in range(DEPTH):
        lp = dict(w_in=w_in[l], conf_dw_w=conf_dw_w[l], conf_dw_b=conf_dw_b[l], conf_ln_g=conf_ln_g[l],
                  conf_ln_b=conf_ln_b[l], ssd_conv_w=ssd_conv_w[l], ssd_conv_b=ssd_conv_b[l],
                  ssd_a_log=ssd_a_log[l], ssd_dt_bias=ssd_dt_bias[l], ssd_d=ssd_d[l], ssd_norm_g=ssd_norm_g[l],
                  hy_short_w=hy_short_w[l], hy_short_b=hy_short_b[l], hy_w1=hy_w1[l], hy_b1=hy_b1[l],
                  hy_w2=hy_w2[l], hy_b2=hy_b2[l], hy_freq=hy_freq[l], hy_w3=hy_w3[l], hy_bias=hy_bias[l],
                  sc_conv_w=sc_conv_w[l], w_branch_a=w_branch_a[l], w_branch_b=w_branch_b[l],
                  w_branch_c=w_branch_c[l], w_branch_d=w_branch_d[l], w_out=w_out[l],
                  rt_group_w=rt_group_w[l], rt_group_b=rt_group_b[l], rt_expert_w=rt_expert_w[l],
                  rt_expert_b=rt_expert_b[l], ex_w_gate=ex_w_gate[l], ex_w_up=ex_w_up[l], ex_w_down=ex_w_down[l])
        last = l == DEPTH - 1
        mod_lat = jnp.split((jax.nn.silu(c) @ w_mod[l] + b_mod[l])[:, None, :], 6, axis=-1)
        mod_ctx = jnp.split(jax.nn.silu(c_ctx) @ w_mod[l] + b_mod[l], 6, axis=-1)
        u_ctx = modulate(h_ctx, mod_ctx[0], mod_ctx[1])
        if last:
            ctx_states = ssd_context_states(u_ctx @ w_in[l][:, OFF_B:OFF_C], ssd_zero, lp)
        else:
            mix_ctx, ctx_states = token_mixer(u_ctx, ssd_zero, lp, None)
        mix_lat, _ = token_mixer(modulate(h_lat, mod_lat[0], mod_lat[1]), ctx_states, lp, rows)
        h_lat = layer_norm(DN_ALPHA * h_lat + mod_lat[2] * mix_lat, ln_g[l, 0], ln_b[l, 0])
        ffn_lat = moe_ffn(modulate(h_lat, mod_lat[3], mod_lat[4]), lp)
        h_lat = layer_norm(DN_ALPHA * h_lat + mod_lat[5] * ffn_lat, ln_g[l, 1], ln_b[l, 1])
        if not last:
            h_ctx = layer_norm(DN_ALPHA * h_ctx + mod_ctx[2] * mix_ctx, ln_g[l, 0], ln_b[l, 0])
            ffn_ctx = moe_ffn(modulate(h_ctx, mod_ctx[3], mod_ctx[4]), lp)
            h_ctx = layer_norm(DN_ALPHA * h_ctx + mod_ctx[5] * ffn_ctx, ln_g[l, 1], ln_b[l, 1])
    return h_lat


_drawn_inputs = setup_inputs


def setup_inputs(seed=0):
    import zlib

    import numpy as np

    out = dict(_drawn_inputs(seed))
    spreads = {}
    factors = {'ctx': 8.0,
     'c_ctx': 3.8,
     'b_mod': 3.238,
     'ln_g': 3.042,
     'ln_b': 3.162,
     'conf_dw_b': 8.0,
     'conf_ln_g': 196.683,
     'conf_ln_b': 200.0,
     'ssd_conv_b': 26.193,
     'ssd_d': 200.0,
     'ssd_norm_g': 183.671,
     'hy_short_w': 3.755,
     'hy_short_b': 8.0,
     'hy_w1': 3.097,
     'hy_b1': 8.0,
     'hy_w2': 4.821,
     'hy_b2': 7.01,
     'hy_freq': 8.0,
     'hy_w3': 4.753,
     'hy_bias': 6.592,
     'w_branch_c': 3.595,
     'rt_group_b': 7.708,
     'rt_expert_b': 6.199}
    for name, (base, spread) in spreads.items():
        noise = np.random.default_rng([zlib.crc32(name.encode()), seed]).standard_normal(out[name].shape)
        drawn = base * np.exp(spread * noise) if base else spread * noise
        out[name] = jnp.asarray(drawn.astype(out[name].dtype))
    for name, factor in factors.items():
        out[name] = (out[name] * factor).astype(out[name].dtype)
    return out
```

```python
import math
from contextlib import ExitStack, contextmanager

import numpy as np

import concourse.bass as bass
from concourse import mybir

F32 = mybir.dt.float32
I32 = mybir.dt.int32
ALU = mybir.AluOpType
ACT = mybir.ActivationFunctionType
AX = mybir.AxisListType

P = 128
D = 1024
T = 1024
KT = D // P
TT = T // P
CTX = 256
GRID_W = 64
CONF_D = 512
CONF_K = 31
SSD_D = 768
HEADS = 12
GROUPS = 4
HPG = HEADS // GROUPS
HD = SSD_D // HEADS
CHUNKS = T // P
CTX_CHUNKS = CTX // P
HY_D = 512
HY_EMB = 33
HY_HID = 64
SC_D = 512
MOE_GROUPS = 4
MOE_EPG = 8
EXPERTS = MOE_GROUPS * MOE_EPG
FF = 512
ALPHA = 2.0 ** 0.25
EPS = 1e-5
BLOCKS = (2 * T + EXPERTS * (P - 1)) // P
SLOTS = BLOCKS + 1
RING = 4
HALVES = ((0, 512), (512, 1024))
BIG = 1e30

OFF_B = 2 * CONF_D
OFF_XBC = OFF_B + SSD_D
OFF_DT = OFF_XBC + SSD_D + 2 * GROUPS * P
OFF_C = OFF_DT + 2 * HEADS
OFF_D = OFF_C + 3 * HY_D
OFF_G = OFF_D + 3 * SC_D

TWO_PI_1 = 6.28125
TWO_PI_2 = float((np.float32(2 * math.pi - TWO_PI_1).view(np.uint32) & np.uint32(0xFFFFF000)).view(np.float32))
TWO_PI_3 = 2 * math.pi - TWO_PI_1 - TWO_PI_2
ROUND = 1.5 * 2.0 ** 23

COLS = {
    "b_mod": 48, "hy_b1": 1, "hy_b2": 1, "hy_f1": 1, "hy_f2": 1,
    "ssd_conv_w": 42, "ssd_conv_b": 14, "ssd_norm_g": 6,
    "hy_short_w": 36, "hy_short_b": 12,
    "conf_dw_w": 124, "conf_dw_b": 4, "conf_ln_g": 4, "conf_ln_b": 4, "sc_conv_w": 12,
}
ROWS = {
    "dt_bias": 24, "a_log": 24, "ssd_d": 12, "hy_bias": 1024, "rt_b": 36,
    "ln_g1": D, "ln_b1": D, "ln_g2": D, "ln_b2": D,
}
CONSTS = {
    "ident": P, "upto": P, "from": P, "before": P, "iota": 64, "sign": 1, "weight": TT,
    "weight_s": TT, "t01": TT, "not_first": TT,
}


def places(sizes):
    at, out = 0, {}
    for name, n in sizes.items():
        out[name] = (at, at + n)
        at += n
    return out, at


COL_AT, N_COLS = places(COLS)
ROW_AT, N_ROWS = places(ROWS)
CONST_AT, N_CONSTS = places(CONSTS)


def shape_constants():
    q = np.arange(P)
    c = np.zeros((P, N_CONSTS), np.float32)

    def put(name, v):
        c[:, CONST_AT[name][0]:CONST_AT[name][1]] = v

    put("ident", np.eye(P))
    put("upto", q[:, None] <= q[None, :])
    put("from", q[:, None] >= q[None, :])
    put("before", q[:, None] < q[None, :])
    put("iota", np.arange(64)[None, :])
    put("sign", ((-1.0) ** q)[:, None])
    weight = np.full((P, TT), 2.0 / (2 * T))
    weight[0, 0] = 1.0 / (2 * T)
    put("weight", weight)
    not_first = np.ones((P, TT))
    not_first[0, 0] = 0.0
    put("not_first", not_first)
    put("weight_s", weight * not_first)
    t01 = np.linspace(0.0, 1.0, T, dtype=np.float32)
    put("t01", t01.reshape(TT, P).T)

    bands_n = (HY_EMB - 1) // 2
    omega = np.float32(2.0 * math.pi / T) * np.arange(T, dtype=np.float32)[:, None]
    bands = np.linspace(1e-4, bands_n - 1, bands_n, dtype=np.float32)
    phase = (bands * omega).astype(np.float32)
    feat = np.concatenate([t01[:, None], np.cos(phase), -np.sin(phase)], axis=-1).astype(np.float32)
    deltas = np.abs(np.linspace(math.log(1e-2) / 1.5, math.log(1e-2) / 0.3, 4 * HY_D, dtype=np.float32))

    k = np.arange(T, dtype=np.int64)
    angle = (np.outer(k, k) % (2 * T)) * (2.0 * math.pi / (2 * T))
    cos, sin = np.cos(angle), np.sin(angle)
    forward, inverse = sin.copy(), sin.copy()
    forward[:, 0] = (-1.0) ** k
    inverse[0, :] = (-1.0) ** k

    def pair(sine):
        return np.stack([as_items(cos.astype(np.float32)), as_items(sine.astype(np.float32))], axis=1)

    return {
        "consts": c, "featT": np.ascontiguousarray(feat.T), "neg_deltas": -deltas[None, :],
        "zeros": np.zeros((P, 4 * D), np.float32),
        "dft": pair(forward).reshape(2 * TT, P, KT * P), "idft": pair(inverse).reshape(2 * TT, P, KT * P),
    }


def as_items(w):
    kt, n = w.shape[0] // P, w.shape[1] // P
    return np.ascontiguousarray(w.reshape(kt, P, n, P).transpose(2, 1, 0, 3)).reshape(n, P, kt * P)


def as_cols(v):
    v = np.asarray(v)
    v = v.reshape(-1, v.shape[-1] // P, P)
    return v.transpose(2, 1, 0).reshape(P, -1)


class Chain:

    def __init__(self, eng, sem):
        self.eng, self.sem, self.start, self.steps = eng, sem, 0, 0

    def step(self, ins):
        ins.then_inc(self.sem, 1)
        self.steps += 1
        return ins

    def wait(self):
        self.eng.wait_ge(self.sem, self.start + self.steps)

    @contextmanager
    def turns(self, i, turns, per):
        before, steps = self.start, self.steps
        self.start, self.steps = before + steps + i * per, 0
        yield
        assert self.steps == per, (self.steps, per)
        self.start, self.steps = before + steps + turns * per, 0


class Ring:

    def __init__(self, nc, ctx):
        self.nc = nc
        self.buf = ctx.enter_context(nc.sbuf_tensor("ring", [P, RING, KT * P], F32))
        self.landed = [ctx.enter_context(nc.semaphore(f"ring_landed{s}")) for s in range(RING)]
        self.freed = ctx.enter_context(nc.semaphore("ring_freed"))
        self.items = 0

    def claim(self, n):
        base, self.items = self.items, self.items + n
        assert base % RING == 0 and n % RING == 0
        return base

    def load(self, sp, item, slot, src, width=KT * P):
        sp.wait_ge(self.freed, item + 1)
        sp.dma_start(self.buf[:, slot, 0:width], src).then_inc(self.landed[slot], 16)

    def arrived(self, pe, base, turn, slot):
        pe.wait_ge(self.landed[slot], turn * 16 + (base // RING + 1) * 16)

    def done(self, item):
        return item + RING + 1


class Kernel:
    def __init__(self, nc, a, ctx):
        self.nc, self.a = nc, a
        self.ring = Ring(nc, ctx)
        sb = self.resident(ctx)
        self.uT = sb("uT", [P, KT, T])
        self.cols = sb("cols", [P, N_COLS])
        self.consts = sb("consts", [P, N_CONSTS])
        self.ones = sb("ones", [P, P])
        self.mod = sb("mod", [P, 48, 2])
        self.blank = ctx.enter_context(nc.semaphore("blank"))
        self.blank_parts = SLOTS // 4
        self.ps = ctx.enter_context(nc.psum_tensor("ps", [P, 8, 512], F32))

    def resident(self, ctx):
        return lambda name, shape, dt=F32: ctx.enter_context(self.nc.sbuf_tensor(f"sb_{name}", shape, dt))

    def col(self, name, i=0, n=1):
        at = COL_AT[name][0] + i
        return self.cols[:, at:at + n]

    def const(self, name, i=0, n=None):
        at, end = CONST_AT[name]
        return self.consts[:, at + i:end if n is None else at + i + n]

    def row(self, name):
        at, end = ROW_AT[name]
        return self.a["rows"][0, at:end].partition_broadcast(P)

    @contextmanager
    def stage(self, name):
        nc, sems = self.nc, []
        with ExitStack() as ctx:
            def sb(n, shape, dt=F32):
                return ctx.enter_context(nc.sbuf_tensor(f"{name}_{n}", shape, dt))

            def sem(n):
                s = nc.alloc_semaphore(f"{name}_{n}")
                sems.append(s)
                return s

            yield sb, sem
            nc.clear_and_free_semaphores(sems)
            nc.all_engine_barrier()

    def product(self, slot, rhs, out, cols, kt=KT):
        for k in range(kt):
            last = self.nc.tensor.matmul(out, self.ring.buf[:, slot, k * P:(k + 1) * P],
                                         rhs[:, k, cols[0]:cols[1]], start=(k == 0), stop=(k == kt - 1))
        return last


def filter_stages(k):
    with ExitStack() as ctx:
        sb = k.resident(ctx)
        even, odd = sb("even", [P, TT, 2, HY_D]), sb("odd", [P, TT, 2, HY_D])
        norms = sb("norms", [P, 2, HY_D])
        stage_filter_time(k, even, odd, norms)
        stage_filter_spectrum(k, even, odd, norms)


def stage_filter_time(k, even, odd, norms):
    nc, a, ring, ps = k.nc, k.a, k.ring, k.ps
    with k.stage("ft") as (sb, sem):
        featT = sb("featT", [HY_EMB, T])
        w1, w2 = sb("w1", [HY_EMB, HY_HID]), sb("w2", [HY_HID, HY_HID])
        w3 = sb("w3", [HY_HID, 4 * HY_D])
        deltas = sb("deltas", [P, 4 * HY_D])
        cc, ccs = sb("cc", [P, KT, 2]), sb("ccs", [P, KT, 2])
        arg, whole = sb("arg", [HY_HID, T]), sb("whole", [HY_HID, T])
        hid, hid_t = sb("hid", [HY_HID, 2, T]), sb("hid_t", [HY_HID, P])
        window = sb("window", [P, 4 * HY_D])
        filt, mags = sb("filt", [P, 2, 2, HY_D]), sb("mags", [P, 2, 2, HY_D])
        mag_sum = sb("mag_sum", [P, 2, 2, HY_D])
        loaded, cc_in, silu_c = sem("loaded"), sem("cc_in"), sem("silu_c")
        pre_ready, arg_ready, hid_ready = sem("pre_ready"), sem("arg_ready"), sem("hid_ready")
        hid_t_ready, filt_mm, window_ready = sem("hid_t_ready"), sem("filt_mm"), sem("window_ready")
        filt_ready, mags_ready, summed = sem("filt_ready"), sem("mags_ready"), sem("summed")
        dve, ones_set, norm_mm = sem("dve"), sem("ones_set"), sem("norm_mm")
        mod_items = 48
        base = ring.claim(mod_items)
        loads = ((k.consts[:, :], a["consts"]), (k.cols[:, :], a["cols"]), (featT[:, :], a["featT"]),
                 (w1[:, :], a["hy_w1"]), (w2[:, :], a["hy_w2"]), (w3[:, :], a["hy_w3"]),
                 (deltas[:, :], a["neg_deltas"][0].partition_broadcast(P)))

        with nc.Block() as block:
            @block.sync
            def _(sp):
                sp.sem_inc(ring.freed, RING)
                sp.dma_start(cc[:, :, :], a["ccT"]).then_inc(cc_in, 16)
                for dst, src in loads:
                    sp.dma_start(dst, src).then_inc(loaded, 16)
                with sp.Fori(0, mod_items // RING) as j:
                    for slot in range(RING):
                        ring.load(sp, j * RING + base + slot, slot, item(a["w_mod"], j * RING + slot))

            @block.tensor
            def _(pe):
                pe.wait_ge(loaded, 16 * len(loads))
                for layer, (w, src) in enumerate(((w1[:, :], featT), (w2[:, :], hid[:, 0, :]))):
                    if layer:
                        pe.wait_ge(hid_ready, 1)
                    for h, (lo, hi) in enumerate(HALVES):
                        mm = nc.tensor.matmul(ps[0:HY_HID, h, :], w, src[:, lo:hi], start=True, stop=True)
                    mm.then_inc(pre_ready, 1)
                pe.wait_ge(silu_c, 1)

                def modulation(j, turn0):
                    for slot in range(RING):
                        ring.arrived(pe, base + turn0 * RING, j, slot)
                        for kt in range(KT):
                            mm = nc.tensor.matmul(ps[:, 6, bass.ds((j * RING + turn0 * RING + slot) * 2, 2)],
                                                  ring.buf[:, slot, kt * P:(kt + 1) * P], ccs[:, kt, :],
                                                  start=(kt == 0), stop=(kt == KT - 1))
                        mm.then_inc(ring.freed, 1)

                with pe.Fori(0, TT) as j:
                    pe.wait_ge(hid_t_ready, j + 1)
                    for q in range(4):
                        mm = nc.tensor.matmul(ps[:, q, :], hid_t[:, :], w3[:, q * HY_D:(q + 1) * HY_D],
                                              start=True, stop=True)
                    mm.then_inc(filt_mm, 1)
                    modulation(j, 0)
                pe.wait_ge(summed, TT + 1)
                pe.wait_ge(ones_set, 1)
                for o in range(2):
                    for d in range(2):
                        mm = nc.tensor.matmul(ps[:, o, :], k.ones[:, :], mag_sum[:, o, d, :],
                                              start=(d == 0), stop=(d == 1))
                mm.then_inc(norm_mm, 1)
                with pe.Fori(0, mod_items // RING - TT) as j:
                    modulation(j, TT)

            @block.scalar
            def _(act):
                act.sem_inc(mags_ready, 1)
                act.wait_ge(cc_in, 16)
                nc.scalar.activation(ccs[:, :, :], cc[:, :, :], ACT.Silu).then_inc(silu_c, 1)
                for layer in range(2):
                    act.wait_ge(arg_ready, layer + 1)
                    nc.scalar.activation(hid[:, layer, :], arg[:, :], ACT.Sin).then_inc(hid_ready, 1)
                with act.Fori(0, TT) as j:
                    act.wait_ge(filt_ready, j + 1)
                    nc.scalar.activation(window[:, :], deltas[:, :], ACT.Exp,
                                         scale=k.const("t01")[:, bass.ds(j, 1)]).then_inc(window_ready, 1)
                    act.wait_ge(filt_ready, j + 2)
                    act.wait_ge(summed, j + 1)
                    nc.scalar.activation(mags[:, :, :, :], filt[:, :, :, :], ACT.Abs).then_inc(mags_ready, 1)

            @block.gpsimd
            def _(pool):
                nc.gpsimd.memset(mag_sum[:, :, :, :], 0.0).then_inc(summed, 1)
                with pool.Fori(0, TT) as j:
                    pool.wait_ge(mags_ready, j + 2)
                    pool.wait_ge(summed, j + 1)
                    nc.gpsimd.tensor_tensor(mag_sum[:, :, :, :], mag_sum[:, :, :, :], mags[:, :, :, :],
                                            ALU.add).then_inc(summed, 1)

            @block.vector
            def _(v):
                v.sem_inc(filt_ready, 1)
                ch = Chain(v, dve)
                nc.vector.memset(k.ones[:, :], 1.0).then_inc(ones_set, 1)
                v.wait_ge(loaded, 16 * len(loads))
                for layer, (b, f) in enumerate((("hy_b1", "hy_f1"), ("hy_b2", "hy_f2"))):
                    v.wait_ge(pre_ready, layer + 1)
                    for h, (lo, hi) in enumerate(HALVES):
                        ch.step(nc.vector.tensor_scalar(arg[:, lo:hi], ps[0:HY_HID, h, :], k.col(b)[0:HY_HID],
                                                        k.col(f)[0:HY_HID], ALU.add, ALU.mult))
                    ch.wait()
                    ch.step(nc.vector.tensor_scalar(whole[:, :], arg[:, :], 1 / (2 * math.pi), ROUND,
                                                    ALU.mult, ALU.add))
                    ch.wait()
                    ch.step(nc.vector.tensor_scalar(whole[:, :], whole[:, :], ROUND, None, ALU.subtract))
                    for part in (TWO_PI_1, TWO_PI_2, TWO_PI_3):
                        ch.wait()
                        ch.step(nc.vector.scalar_tensor_tensor(out=arg[:, :], in0=whole[:, :], scalar=-part,
                                                               in1=arg[:, :], op0=ALU.mult, op1=ALU.add))
                    ch.wait()
                    nc.vector.tensor_scalar(arg[:, :], arg[:, :], 3.1415925, -3.1415925, ALU.min,
                                            ALU.max).then_inc(arg_ready, 1)
                v.wait_ge(hid_ready, 2)
                with v.Fori(0, TT) as j, ch.turns(j, TT, 3):
                    nc.vector.tensor_copy(hid_t[:, :], hid[:, 1, bass.ds(j * P, P)]).then_inc(hid_t_ready, 1)
                    v.wait_ge(filt_mm, j + 1)
                    v.wait_ge(window_ready, j + 1)
                    v.wait_ge(mags_ready, j + 1)
                    ch.step(nc.vector.tensor_tensor(filt[:, :, :, :].rearrange("p o d c -> p (o d) c"),
                                                    ps[:, 0:4, :],
                                                    window[:, :].rearrange("p (q c) -> p q c", q=4), ALU.mult))
                    ch.wait()
                    nc.vector.tensor_scalar(filt[:, :, 1, :], filt[:, :, 1, :],
                                            k.const("not_first")[:, bass.ds(j, 1)], None,
                                            ALU.mult).then_inc(filt_ready, 1)
                    v.wait_ge(filt_ready, j + 2)
                    for dst, op in ((even, ALU.add), (odd, ALU.subtract)):
                        ch.step(nc.vector.tensor_tensor(
                            dst[:, bass.ds(j, 1), :, :].rearrange("p t o c -> p (t o) c"),
                            filt[:, :, 0, :], filt[:, :, 1, :], op))
                v.wait_ge(norm_mm, 1)
                ch.step(nc.vector.reciprocal(norms[:, :, :], ps[:, 0:2, :]))
                v.wait_ge(ring.freed, ring.done(base + mod_items - 1))
                ch.step(nc.vector.tensor_tensor(k.mod[:, :, :], ps[:, 6, 0:96].rearrange("p (m r) -> p m r", r=2),
                                                k.col("b_mod", 0, 48).unsqueeze(2).broadcast_to([P, 48, 2]),
                                                ALU.add))
                ch.wait()
                for m in (8, 32):
                    ch.step(nc.vector.tensor_scalar(k.mod[:, m:m + 8, :], k.mod[:, m:m + 8, :], 1.0, None, ALU.add))


def stage_filter_spectrum(k, even, odd, norms):
    nc, a, ring, ps = k.nc, k.a, k.ring, k.ps
    with k.stage("fs") as (sb, sem):
        spec = sb("spec", [P, 2, 2, 2 * HY_D])
        last = sb("last", [1, 2, HY_D])
        evac, free, spec_free = sem("evac"), sem("free"), sem("spec_free")
        stored = [sem("stored0"), sem("stored1")]
        nyq_mm, nyq, nyq2, nyq_out = sem("nyq_mm"), sem("nyq"), sem("nyq2"), sem("nyq_out")
        base = ring.claim(2 * TT)

        with nc.Block() as block:
            @block.sync
            def _(sp):
                with sp.Fori(0, 2 * TT // RING) as j:
                    for slot in range(RING):
                        ring.load(sp, j * RING + base + slot, slot, item(a["dft"], j * RING + slot))

            @block.tensor
            def _(pe):
                with pe.Fori(0, 2 * TT // RING) as j:
                    for b in range(2):
                        pe.wait_ge(free, j * 2 + b + 1)
                        for part, src in enumerate((even, odd)):
                            slot = 2 * b + part
                            ring.arrived(pe, base, j, slot)
                            for o in range(2):
                                mm = k.product(slot, src[:, :, o, :], ps[:, 4 * b + 2 * part + o, :], (0, HY_D))
                            mm.then_inc(ring.freed, 1)
                pe.wait_ge(free, TT + 1)
                for o in range(2):
                    for t in range(TT):
                        mm = nc.tensor.matmul(ps[0:1, o, :], k.const("sign"), even[:, t, o, :],
                                              start=(t == 0), stop=(t == TT - 1))
                mm.then_inc(nyq_mm, 1)

            @block.vector
            def _(v):
                v.sem_inc(free, 2)
                with v.Fori(0, TT // 2) as j:
                    for b in range(2):
                        v.wait_ge(spec_free, j * 2 + b + 1)
                        for part, w in enumerate(("weight", "weight_s")):
                            v.wait_ge(ring.freed, j * RING + ring.done(base + 2 * b + part))
                            for o in range(2):
                                ins = nc.vector.scalar_tensor_tensor(
                                    out=spec[:, b, part, o * HY_D:(o + 1) * HY_D],
                                    in0=ps[:, 4 * b + 2 * part + o, :],
                                    scalar=k.const(w)[:, bass.ds(j * 2 + b, 1)], in1=norms[:, o, :],
                                    op0=ALU.mult, op1=ALU.mult)
                                ins.then_inc(evac, 1)
                        v.wait_ge(evac, j * 8 + 4 * b + 4)
                        v.sem_inc(free, 1)
                v.wait_ge(nyq_mm, 1)
                nc.vector.scalar_tensor_tensor(out=last[:, :, :], in0=ps[0:1, 0:2, :],
                                               scalar=1.0 / (2 * T), in1=norms[0:1, :, :],
                                               op0=ALU.mult, op1=ALU.mult).then_inc(nyq, 1)

            @block.scalar
            def _(act):
                act.sem_inc(spec_free, 2)
                with act.Fori(0, TT // 2) as j:
                    for b in range(2):
                        act.wait_ge(evac, j * 8 + 4 * b + 4)
                        dst = a["spectra"][bass.ds(j * 2 + b, 1)].rearrange("o p q n -> p (o q) n")
                        for q, part in enumerate((0, 1, 0)):
                            act.dma_start(dst[:, q, :], spec[:, b, part, :]).then_inc(stored[b], 16)
                        act.wait_ge(stored[b], j * 48 + 48)
                        act.sem_inc(spec_free, 1)
                act.wait_ge(nyq, 1)
                act.dma_start(a["spectra"][0, 0:1, 2, :], last[:, :, :].rearrange("p o n -> p (o n)")).then_inc(nyq_out, 16)
                act.wait_ge(nyq_out, 16)


def item(array, n):
    return array[bass.ds(n, 1)].rearrange("o p n -> p (o n)")


def host_arrays(x, c, ctx, c_ctx, w_mod, b_mod, ln_g, ln_b, w_in, conf_dw_w, conf_dw_b, conf_ln_g, conf_ln_b,
                ssd_conv_w, ssd_conv_b, ssd_a_log, ssd_dt_bias, ssd_d, ssd_norm_g, hy_short_w, hy_short_b,
                hy_w1, hy_b1, hy_w2, hy_b2, hy_freq, hy_w3, hy_bias, sc_conv_w, w_branch_a, w_branch_b,
                w_branch_c, w_branch_d, w_out, rt_group_w, rt_group_b, rt_expert_w, rt_expert_b,
                ex_w_gate, ex_w_up, ex_w_down):
    w = w_in[0]
    tall = {
        "b_mod": as_cols(b_mod[0]),
        "ssd_conv_w": as_cols(ssd_conv_w[0]), "ssd_conv_b": as_cols(ssd_conv_b[0]),
        "ssd_norm_g": as_cols(ssd_norm_g[0]),
        "hy_short_w": as_cols(hy_short_w[0]), "hy_short_b": as_cols(hy_short_b[0]),
        "conf_dw_w": as_cols(conf_dw_w[0]), "conf_dw_b": as_cols(conf_dw_b[0]),
        "conf_ln_g": as_cols(conf_ln_g[0]), "conf_ln_b": as_cols(conf_ln_b[0]),
        "sc_conv_w": as_cols(sc_conv_w[0]),
    }
    cols = np.zeros((P, N_COLS), np.float32)
    for name, (lo, hi) in COL_AT.items():
        if name in tall:
            cols[:, lo:hi] = tall[name]
    for name, vec in (("hy_b1", hy_b1[0]), ("hy_b2", hy_b2[0]), ("hy_f1", hy_freq[0, 0]), ("hy_f2", hy_freq[0, 1])):
        cols[0:HY_HID, COL_AT[name][0]] = vec
    rows = np.concatenate([ssd_dt_bias[0].ravel(), ssd_a_log[0].ravel(), ssd_d[0], hy_bias[0].ravel(),
                           rt_group_b[0], rt_expert_b[0], ln_g[0, 0], ln_b[0, 0], ln_g[0, 1], ln_b[0, 1]])[None, :]
    val_gate = [w[:, o + i * P:o + (i + 1) * P] for i in range(4) for o in (0, CONF_D)]
    bg_cg_xv = [w[:, OFF_D + o + i * P:OFF_D + o + (i + 1) * P] for i in range(4) for o in (SC_D, 2 * SC_D, 0)]
    out = {
        "x": x[0], "xT": x[0].T, "ctxT": ctx[0].T,
        "ccT": np.stack([c[0], c_ctx], 1).reshape(KT, P, 2).transpose(1, 0, 2),
        "cols": cols, "rows": rows,
        "w_mod": as_items(w_mod[0]),
        "w_xbc": as_items(w[:, OFF_XBC:OFF_DT]), "w_z": as_items(w[:, OFF_B:OFF_XBC]),
        "w_dt": w[:, OFF_DT:OFF_C].reshape(KT, P, 2 * HEADS).transpose(1, 0, 2),
        "w_hy": as_items(w[:, OFF_C:OFF_D]), "w_conf": as_items(np.concatenate(val_gate, 1)),
        "w_sc": as_items(np.concatenate(bg_cg_xv, 1)), "w_gate": as_items(w[:, OFF_G:]),
        "w_br_a": as_items(w_branch_a[0]), "w_br_b": as_items(w_branch_b[0]),
        "w_br_c": as_items(w_branch_c[0]), "w_br_d": as_items(w_branch_d[0]),
        "w_out": w_out[0].reshape(KT, P, D).transpose(1, 0, 2),
        "w_rt": np.concatenate([rt_group_w[0], rt_expert_w[0]], 1).reshape(KT, P, 36).transpose(1, 0, 2),
        "hy_w1": hy_w1[0], "hy_w2": hy_w2[0], "hy_w3": hy_w3[0],
        "ex_g": ex_w_gate[0], "ex_u": ex_w_up[0], "ex_d": ex_w_down[0],
    }
    out.update(shape_constants())
    return {name: np.ascontiguousarray(v) for name, v in out.items()}


SCRATCH = {
    "spectra": [TT, P, 3, 2 * HY_D],
    "xbc_chan": [14, P, T + CTX + 2],
    "xbc_tok": [CHUNKS + CTX_CHUNKS, P, 14 * P],
    "h1": [TT, P, D],
    "moe": [SLOTS * P, D],
}


def loop_items(eng, n, body):
    with eng.Fori(0, n // RING) as j:
        for q in range(RING):
            body(j, q)
    for q in range(n % RING):
        body(n // RING, q)


def stage_modulate(k):
    nc, a = k.nc, k.a
    with k.stage("um") as (sb, sem):
        x_in, done = sem("x_in"), sem("done")
        with nc.Block() as block:
            @block.scalar
            def _(act):
                for part in range(k.blank_parts):
                    act.dma_start(a["moe"].rearrange("(n p r) d -> n p (r d)", p=P, r=4)[part],
                                  a["zeros"]).then_inc(k.blank, 16)

            @block.sync
            def _(sp):
                sp.dma_start(k.uT[:, :, :], a["xT"].rearrange("(k p) t -> p k t", p=P)).then_inc(x_in, 16)

            @block.vector
            def _(v):
                v.wait_ge(x_in, 16)
                for kt in range(KT):
                    nc.vector.tensor_scalar(k.uT[:, kt, :], k.uT[:, kt, :], k.mod[:, 8 + kt, 0:1],
                                            k.mod[:, kt, 0:1], ALU.mult, ALU.add).then_inc(done, 1)
                v.wait_ge(done, KT)


def stage_project_conv(k, name, items, n, taps, bias, func, ctx=None, chan_out=None, tok_out=None, tok_sbuf=None):
    nc, a, ring, ps = k.nc, k.a, k.ring, k.ps
    width = T + (CTX + 2 if ctx is not None else 0)
    chunks = CHUNKS + (CTX_CHUNKS if ctx is not None else 0)
    full = n + -n % RING
    base = ring.claim(full)
    ctx_at = T + 2
    reads = 2 if ctx is None else 3
    with k.stage(name) as (sb, sem):
        line = sb("line", [P, 2, width + 2])
        conv = sb("conv", [P, 2, width])
        shaped = sb("shaped", [P, 2, width])
        turned = sb("turned", [P, 2, chunks, P]) if tok_sbuf is None else None
        psum_free, line_free, shaped_free, turned_free = (sem(x) for x in
                                                          ("psum_free", "line_free", "shaped_free", "turned_free"))
        lined, dve, convolved, shaped_ready = sem("lined"), sem("dve"), sem("convolved"), sem("shaped_ready")
        turned_mm, turned_ready = sem("turned_mm"), sem("turned_ready")
        stored = [[sem(f"stored{q}{b}") for b in range(2)] for q in range(2)]

        def banks(q):
            return (3 * (q % 2), 3 * (q % 2) + 1, 3 * (q % 2) + 2)

        with nc.Block() as block:
            @block.sync
            def _(sp):
                loop_items(sp, n, lambda j, q: ring.load(sp, j * RING + base + q, q, item(items, j * RING + q)))
                for q in range(n, full):
                    sp.wait_ge(ring.freed, base + q + 1)
                    sp.sem_inc(ring.landed[q % RING], 16)

            @block.tensor
            def _(pe):
                def project(j, q):
                    pe.wait_ge(psum_free, j * RING + q + 1)
                    ring.arrived(pe, base, j, q)
                    b0, b1, b2 = banks(q)
                    for bank, cols in zip((b0, b1), HALVES):
                        mm = k.product(q, k.uT, ps[:, bank, :], cols)
                    if ctx is not None:
                        pe.wait_ge(turned_ready, (j * RING + q) * reads + reads)
                        mm = k.product(q, ctx, ps[:, b2, 0:CTX], (0, CTX))
                    mm.then_inc(ring.freed, 1)

                def turn(j, q):
                    pe.wait_ge(shaped_ready, j * RING + q + 1)
                    pe.wait_ge(turned_ready, (j * RING + q) * reads + 2 * reads)
                    for c in range(CHUNKS):
                        mm = nc.tensor.transpose(ps[:, 6 + c // 4, (c % 4) * P:(c % 4 + 1) * P],
                                                 shaped[:, q % 2, c * P:(c + 1) * P], k.const("ident"))
                    if ctx is not None:
                        for c in range(CTX_CHUNKS):
                            mm = nc.tensor.transpose(ps[:, banks(q)[2], CTX + c * P:CTX + (c + 1) * P],
                                                     shaped[:, q % 2, ctx_at + c * P:ctx_at + (c + 1) * P],
                                                     k.const("ident"))
                    mm.then_inc(turned_mm, 1)

                def group(j, count):
                    for q in range(count):
                        project(j, q)
                        if q:
                            turn(j, q - 1)
                    turn(j, count - 1)

                with pe.Fori(0, n // RING) as j:
                    group(j, RING)
                if n % RING:
                    group(n // RING, n % RING)
                    pe.wait_ge(ring.freed, ring.done(base + n - 1))
                    pe.sem_inc(ring.freed, full - n)

            @block.scalar
            def _(act):
                act.sem_inc(turned_ready, 2 * reads)

                def evacuate(j, q):
                    act.wait_ge(ring.freed, j * RING + ring.done(base + q))
                    act.wait_ge(line_free, j * RING + q + 1)
                    b0, b1, b2 = banks(q)
                    ins = nc.scalar.copy(line[:, q % 2, 1:T + 1],
                                         ps[:, b0:b1 + 1, :].rearrange("p b n -> p (b n)"))
                    if ctx is not None:
                        ins.then_inc(lined, 1)
                        ins = nc.scalar.copy(line[:, q % 2, ctx_at + 1:ctx_at + 1 + CTX], ps[:, b2, 0:CTX])
                    ins.then_inc(lined, 1)

                def shape(j, q):
                    act.wait_ge(convolved, j * RING + q + 1)
                    act.wait_ge(shaped_free, j * RING + q + 1)
                    nc.scalar.activation(shaped[:, q % 2, :], conv[:, q % 2, :], func,
                                         bias=k.col(bias, 0, n)[:, bass.ds(j * RING + q, 1)]).then_inc(shaped_ready, 1)

                def evacuate_turned(j, q):
                    act.wait_ge(turned_mm, j * RING + q + 1)
                    act.wait_ge(turned_free, j * RING + q + 1)
                    for h in range(2):
                        part = slice(4 * h, 4 * h + 4)
                        if tok_sbuf is None:
                            out = turned[:, q % 2, part, :]
                        else:
                            out = tok_sbuf[:, part, bass.ds((j * RING + q) * P, P)]
                        nc.scalar.copy(out, ps[:, 6 + h, :].rearrange("p (c m) -> p c m", c=4)).then_inc(turned_ready, 1)
                    if ctx is not None:
                        nc.scalar.copy(turned[:, q % 2, CHUNKS:, :],
                                       ps[:, banks(q)[2], CTX:2 * CTX].rearrange("p (c m) -> p c m", c=CTX_CHUNKS)
                                       ).then_inc(turned_ready, 1)

                def group(j, count):
                    for q in range(count):
                        evacuate(j, q)
                        shape(j, q)
                        if q:
                            evacuate_turned(j, q - 1)
                    evacuate_turned(j, count - 1)

                with act.Fori(0, n // RING) as j:
                    group(j, RING)
                if n % RING:
                    group(n // RING, n % RING)

            @block.vector
            def _(v):
                ch = Chain(v, dve)
                ch.step(nc.vector.memset(line[:, :, :], 0.0))
                ch.wait()
                v.sem_inc(line_free, 2)
                v.sem_inc(psum_free, 2)
                copies = 1 if ctx is None else 2

                def convolve(j, q):
                    m, src, dst = j * RING + q, line[:, q % 2, :], conv[:, q % 2, :]
                    tap = [k.col(taps, 0, 3 * n)[:, bass.ds(m * 3 + i, 1)] for i in range(3)]
                    v.wait_ge(lined, m * copies + copies)
                    v.sem_inc(psum_free, 1)
                    ch.step(nc.vector.tensor_scalar(dst, src[:, 0:width], tap[0], None, ALU.mult))
                    ch.wait()
                    ch.step(nc.vector.scalar_tensor_tensor(out=dst, in0=src[:, 1:width + 1], scalar=tap[1], in1=dst,
                                                           op0=ALU.mult, op1=ALU.add))
                    ch.wait()
                    nc.vector.scalar_tensor_tensor(out=dst, in0=src[:, 2:width + 2], scalar=tap[2], in1=dst,
                                                   op0=ALU.mult, op1=ALU.add).then_inc(convolved, 1)
                    v.wait_ge(convolved, m + 1)
                    v.sem_inc(line_free, 1)

                with v.Fori(0, n // RING) as j, ch.turns(j, n // RING, 2 * RING):
                    for q in range(RING):
                        convolve(j, q)
                for q in range(n % RING):
                    convolve(n // RING, q)

            @block.gpsimd
            def _(pool):
                pool.sem_inc(shaped_free, 2)
                pool.sem_inc(turned_free, 2)

                def store(j, q):
                    b = q % 2
                    m = j * RING + q
                    pool.wait_ge(shaped_ready, m + 1)
                    if chan_out is not None:
                        pool.dma_start(item(chan_out, m), shaped[:, b, :]).then_inc(stored[0][b], 16)
                        pool.wait_ge(turned_ready, m * reads + 3 * reads)
                        pool.dma_start(tok_out[:, :, bass.ds(m * P, P)].rearrange("c p m -> p c m"),
                                       turned[:, b, :, :]).then_inc(stored[1][b], 16)
                        for which in range(2):
                            pool.wait_ge(stored[which][b], j * 32 + (q // 2) * 16 + 16)
                        pool.sem_inc(turned_free, 1)
                    else:
                        pool.wait_ge(turned_ready, m * reads + 3 * reads)
                        pool.sem_inc(turned_free, 1)
                    pool.sem_inc(shaped_free, 1)

                loop_items(pool, n, store)



def ssd_stages(k, y_bT):
    with ExitStack() as ctx:
        sb = k.resident(ctx)
        y = sb("ssd_y", [P, CHUNKS, SSD_D])
        n = CHUNKS + CTX_CHUNKS
        dt = {name: sb("dt_" + name, [P, n, 2, HEADS]) for name in
              ("dt", "log_decay", "cum", "exp_cum", "to_end", "total")}
        with ExitStack() as inner:
            uc = inner.enter_context(k.nc.sbuf_tensor("sb_uc", [P, KT, CTX], F32))
            stage_dt(k, uc, dt)
            stage_project_conv(k, "xbc", k.a["w_xbc"], 14, "ssd_conv_w", "ssd_conv_b", ACT.Silu, ctx=uc,
                               chan_out=k.a["xbc_chan"], tok_out=k.a["xbc_tok"])
        stage_scan(k, dt, y)
        stage_ssd_norm(k, y, y_bT)


def stage_dt(k, uc, dt):
    nc, a, ps = k.nc, k.a, k.ps
    n = CHUNKS + CTX_CHUNKS
    H2 = 2 * HEADS
    with k.stage("dt") as (sb, sem):
        w_dt = sb("w_dt", [P, KT, H2])
        raw = sb("raw", [H2, n * P])
        bias, a_log = sb("bias", [P, H2]), sb("a_log", [P, H2])
        tmp, neg = sb("tmp", [P, n, H2]), sb("neg", [P, n, H2])
        loaded, u_ready, raw_mm, raw_ready, turned = (sem(x) for x in
                                                      ("loaded", "u_ready", "raw_mm", "raw_ready", "turned"))
        rate_ready, abs_ready, exp_ready, ln_ready, decay_ready = (sem(x) for x in (
            "rate_ready", "abs_ready", "exp_ready", "ln_ready", "decay_ready"))
        cum_mm, diff_ready, act_done, dve = sem("cum_mm"), sem("diff_ready"), sem("act_done"), sem("dve")
        done = sem("done")

        def flat(name):
            return dt[name][:, :, :, :].rearrange("p c d h -> p c (d h)")

        def wide(row):
            return row[:, :].unsqueeze(1).broadcast_to([P, n, H2])

        with nc.Block() as block:
            @block.sync
            def _(sp):
                sp.dma_start(uc[:, :, :], a["ctxT"].rearrange("(k p) t -> p k t", p=P)).then_inc(loaded, 16)
                sp.dma_start(w_dt[:, :, :], a["w_dt"]).then_inc(loaded, 16)
                sp.dma_start(bias[:, :], k.row("dt_bias")).then_inc(loaded, 16)
                sp.dma_start(a_log[:, :], k.row("a_log")).then_inc(loaded, 16)

            @block.tensor
            def _(pe):
                pe.wait_ge(loaded, 64)
                pe.wait_ge(u_ready, KT)
                for b, (src, lo, hi) in enumerate(((k.uT, 0, 512), (k.uT, 512, 1024), (uc, 0, CTX))):
                    for kt in range(KT):
                        mm = nc.tensor.matmul(ps[0:H2, b, 0:hi - lo], w_dt[:, kt, :], src[:, kt, lo:hi],
                                              start=(kt == 0), stop=(kt == KT - 1))
                mm.then_inc(raw_mm, 1)
                pe.wait_ge(raw_ready, 2)
                for c in range(n):
                    mm = nc.tensor.transpose(ps[:, 3, c * H2:(c + 1) * H2], raw[:, c * P:(c + 1) * P],
                                             k.const("ident")[0:H2, 0:H2])
                mm.then_inc(turned, 1)
                pe.wait_ge(decay_ready, 1)
                for d, tri in enumerate(("upto", "from")):
                    nc.tensor.matmul(ps[:, 4 + d, 0:n * HEADS], k.const(tri), dt["log_decay"][:, :, d, :],
                                     start=True, stop=True)
                nc.tensor.matmul(ps[:, 6, 0:n * H2], k.ones[:, :], flat("log_decay"), start=True,
                                 stop=True).then_inc(cum_mm, 1)

            @block.vector
            def _(v):
                ch = Chain(v, dve)
                v.wait_ge(loaded, 64)
                for kt in range(KT):
                    nc.vector.tensor_scalar(uc[:, kt, :], uc[:, kt, :], k.mod[:, 8 + kt, 1:2],
                                            k.mod[:, kt, 1:2], ALU.mult, ALU.add).then_inc(u_ready, 1)
                v.wait_ge(raw_mm, 1)
                nc.vector.tensor_copy(raw[:, 0:T], ps[0:H2, 0:2, :].rearrange("p b n -> p (b n)")).then_inc(raw_ready, 1)
                nc.vector.tensor_copy(raw[:, T:T + CTX], ps[0:H2, 2, 0:CTX]).then_inc(raw_ready, 1)
                v.wait_ge(turned, 1)
                ch.step(nc.vector.tensor_tensor(tmp[:, :, :], ps[:, 3, 0:n * H2].rearrange("p (c h) -> p c h", c=n),
                                                wide(bias), ALU.add))
                ch.wait()
                nc.vector.tensor_scalar(neg[:, :, :], tmp[:, :, :], -1.0, None, ALU.mult).then_inc(abs_ready, 1)
                v.wait_ge(abs_ready, 1)
                nc.vector.tensor_tensor(neg[:, :, :], tmp[:, :, :], neg[:, :, :], ALU.min).then_inc(abs_ready, 1)
                v.wait_ge(ln_ready, 1)
                ch.step(nc.vector.scalar_tensor_tensor(out=flat("dt"), in0=tmp[:, :, :], scalar=0.0,
                                                       in1=neg[:, :, :], op0=ALU.max, op1=ALU.add))
                v.wait_ge(rate_ready, 1)
                ch.step(nc.vector.tensor_scalar(a_log[:, :], a_log[:, :], -1.0, None, ALU.mult))
                ch.wait()
                nc.vector.tensor_tensor(flat("log_decay"), flat("dt"), wide(a_log), ALU.mult).then_inc(decay_ready, 1)
                v.wait_ge(cum_mm, 1)
                for d in range(2):
                    ch.step(nc.vector.tensor_copy(dt["cum"][:, :, d, :],
                                                  ps[:, 4 + d, 0:n * HEADS].rearrange("p (c h) -> p c h", c=n)))
                ch.wait()
                nc.vector.tensor_tensor(flat("to_end"), ps[:, 6, 0:n * H2].rearrange("p (c h) -> p c h", c=n),
                                        flat("cum"), ALU.subtract).then_inc(diff_ready, 1)
                v.wait_ge(act_done, 3)
                nc.vector.tensor_copy(flat("total"), tmp[:, :, :]).then_inc(done, 1)
                v.wait_ge(done, 1)

            @block.scalar
            def _(act):
                act.wait_ge(loaded, 64)
                nc.scalar.activation(a_log[:, :], a_log[:, :], ACT.Exp).then_inc(rate_ready, 1)
                act.wait_ge(abs_ready, 2)
                nc.scalar.activation(neg[:, :, :], neg[:, :, :], ACT.Exp).then_inc(exp_ready, 1)
                act.wait_ge(exp_ready, 1)
                nc.scalar.activation(neg[:, :, :], neg[:, :, :], ACT.Ln, bias=1.0).then_inc(ln_ready, 1)
                act.wait_ge(diff_ready, 1)
                nc.scalar.activation(flat("exp_cum"), flat("cum"), ACT.Exp).then_inc(act_done, 1)
                nc.scalar.activation(flat("to_end"), flat("to_end"), ACT.Exp).then_inc(act_done, 1)
                nc.scalar.activation(tmp[:, :, :], ps[:, 6, 0:n * H2].rearrange("p (c h) -> p c h", c=n),
                                     ACT.Exp).then_inc(act_done, 1)


def stage_scan(k, dt, y):
    nc, a, ps = k.nc, k.a, k.ps
    half = SSD_D // 2
    with k.stage("scan") as (sb, sem):
        b_chan, c_chan = sb("b_chan", [P, 2, GROUPS, P]), sb("c_chan", [P, 2, GROUPS, P])
        b_tok, xs = sb("b_tok", [P, 2, GROUPS * P]), sb("xs", [P, 2, SSD_D])
        xdt, xend = sb("xdt", [P, 2, SSD_D]), sb("xend", [P, 2, SSD_D])
        decay, mix = sb("decay", [P, 2, 2, HPG, P]), sb("mix", [P, 2, 2, HPG, P])
        cb, chunk_decay = sb("cb", [P, GROUPS, P]), sb("chunk_decay", [P, HEADS])
        state, faded, out = sb("state", [P, SSD_D]), sb("faded", [P, SSD_D]), sb("out", [P, SSD_D])
        d_row = sb("d_row", [P, HEADS])
        d_in, buf_free = sem("d_in"), sem("buf_free")
        in_state, in_out = [sem("in_state0"), sem("in_state1")], [sem("in_out0"), sem("in_out1")]
        xdt_ready, xend_ready, skip_ready, faded_ready = (sem(x) for x in (
            "xdt_ready", "xend_ready", "skip_ready", "faded_ready"))
        decay_set, cb_mm, cum_mm, off_mm, diag_mm, state_mm = (sem(x) for x in (
            "decay_set", "cb_mm", "cum_mm", "off_mm", "diag_mm", "state_mm"))
        cb_ready, diff_ready, low_ready, exp_ready, mix_ready = (sem(x) for x in (
            "cb_ready", "diff_ready", "low_ready", "exp_ready", "mix_ready"))
        state_half, state_done, y_read, dve = sem("state_half"), sem("state_done"), sem("y_read"), sem("dve")
        order = (1, 0)
        steps = CTX_CHUNKS + CHUNKS

        def plan(eng, context_step, step):
            for o, d in enumerate(order):
                for i in range(CTX_CHUNKS):
                    c = CHUNKS + (i if d == 0 else CTX_CHUNKS - 1 - i)
                    context_step(o, d, c, o * steps + i, i % 2, o * (steps // 2) + i // 2)
                with eng.Fori(0, CHUNKS // 2) as j:
                    for q in range(2):
                        i = j * 2 + q
                        c = i if d == 0 else j * -2 + (CHUNKS - 1 - q)
                        step(o, d, c, j * 2 + (o * steps + CTX_CHUNKS + q), q, j + (o * steps + CTX_CHUNKS) // 2,
                             j * 2 + (o * CHUNKS + q), j + o * CHUNKS // 2, j)

        def at(name, c, d, lo=0, hi=HEADS):
            return dt[name][:, bass.ds(c, 1), d, lo:hi].rearrange("p c h -> p (c h)")

        def per_head(v, width=HD):
            return v.unsqueeze(2).broadcast_to([P, v.shape[1], width])

        def heads(v):
            return v.rearrange("p (h e) -> p h e", e=HD)

        with nc.Block() as block:
            @block.sync
            def _(sp):
                sp.dma_start(d_row[:, :], k.row("ssd_d")).then_inc(d_in, 16)

                def load_state(c, n, b):
                    sp.wait_ge(buf_free, n + 1)
                    tok = item(a["xbc_tok"], c)
                    sp.dma_start(xs[:, b, :], tok[:, 0:SSD_D]).then_inc(in_state[b], 16)
                    sp.dma_start(b_tok[:, b, :], tok[:, SSD_D:SSD_D + GROUPS * P]).then_inc(in_state[b], 16)

                def context_step(o, d, c, n, b, turn):
                    load_state(c, n, b)

                def step(o, d, c, n, b, turn, lat, lat_turn, j):
                    load_state(c, n, b)
                    for q, dst in enumerate((b_chan, c_chan)):
                        src = a["xbc_chan"][6 + GROUPS * q:6 + GROUPS * (q + 1), :, bass.ds(c * P, P)]
                        sp.dma_start(dst[:, b, :, :], src.rearrange("g p t -> p g t")).then_inc(in_out[b], 16)

                plan(sp, context_step, step)

            @block.gpsimd
            def _(pool):
                pool.wait_ge(d_in, 16)

                def inputs(o, d, c, n, b, turn):
                    pool.wait_ge(in_state[b], turn * 32 + 32)
                    nc.gpsimd.tensor_tensor(heads(xdt[:, b, :]), heads(xs[:, b, :]), per_head(at("dt", c, d)),
                                            ALU.mult).then_inc(xdt_ready, 1)
                    pool.wait_ge(xdt_ready, n + 1)
                    nc.gpsimd.tensor_tensor(heads(xend[:, b, :]), heads(xdt[:, b, :]), per_head(at("to_end", c, d)),
                                            ALU.mult).then_inc(xend_ready, 1)
                    pool.wait_ge(state_done, n + (o + 1))
                    nc.gpsimd.tensor_tensor(heads(faded[:, :]), heads(state[:, :]), per_head(at("total", c, d)),
                                            ALU.mult).then_inc(faded_ready, 1)

                def step(o, d, c, n, b, turn, lat, lat_turn, j):
                    if o == 0:
                        pool.wait_ge(in_state[b], turn * 32 + 32)
                        nc.gpsimd.tensor_tensor(
                            heads(y[:, bass.ds(c, 1), :].rearrange("p c n -> p (c n)")), heads(xs[:, b, :]),
                            per_head(d_row[:, :]), ALU.mult).then_inc(skip_ready, 1)
                    inputs(o, d, c, n, b, turn)

                plan(pool, inputs, step)

            @block.tensor
            def _(pe):
                pe.sem_inc(cum_mm, 1)
                def new_state(n, b):
                    pe.wait_ge(xend_ready, n + 1)
                    for h in range(2):
                        pe.wait_ge(state_half, n * 2 + h)
                        for g in (2 * h, 2 * h + 1):
                            mm = nc.tensor.matmul(ps[:, 7, (g % 2) * 192:(g % 2 + 1) * 192],
                                                  b_tok[:, b, g * P:(g + 1) * P],
                                                  xend[:, b, g * 192:(g + 1) * 192], start=True, stop=True)
                        mm.then_inc(state_mm, 1)

                def context_step(o, d, c, n, b, turn):
                    new_state(n, b)

                def step(o, d, c, n, b, turn, lat, lat_turn, j):
                    pe.wait_ge(in_out[b], lat_turn * 32 + 32)
                    pe.wait_ge(cb_ready, lat + 1)
                    for g in range(GROUPS):
                        mm = nc.tensor.matmul(ps[:, 2, g * P:(g + 1) * P], b_chan[:, b, g, :], c_chan[:, b, g, :],
                                              start=True, stop=True)
                    mm.then_inc(cb_mm, 1)

                    def cumulative(h):
                        pe.wait_ge(diff_ready, lat * 2 + h + 1)
                        for e in range(6):
                            col = chunk_decay[:, 6 * h + e:6 * h + e + 1].broadcast_to([P, P])
                            mm = nc.tensor.matmul(ps[:, e // 3, (e % 3) * P:(e % 3 + 1) * P], col,
                                                  k.const("from" if d else "upto"), start=True, stop=True)
                        mm.then_inc(cum_mm, 1)

                    pe.wait_ge(decay_set, lat + 1)
                    cumulative(0)
                    pe.wait_ge(state_done, n + (o + 1))
                    pe.wait_ge(y_read, lat + 1)
                    for g in range(GROUPS):
                        mm = nc.tensor.matmul(ps[:, 5 + g // 2, (g % 2) * 192:(g % 2 + 1) * 192],
                                              c_chan[:, b, g, :], state[:, g * 192:(g + 1) * 192],
                                              start=True, stop=True)
                    mm.then_inc(off_mm, 1)
                    cumulative(1)
                    new_state(n, b)
                    pe.wait_ge(xdt_ready, n + 1)
                    for h in range(2):
                        pe.wait_ge(mix_ready, lat * 2 + h + 1)
                        for e in range(6):
                            head = 6 * h + e
                            mm = nc.tensor.matmul(ps[:, 3 + h, e * HD:(e + 1) * HD], mix[:, h, e // 3, e % 3, :],
                                                  xdt[:, b, head * HD:(head + 1) * HD], start=True, stop=True)
                    mm.then_inc(diag_mm, 1)

                plan(pe, context_step, step)

            @block.scalar
            def _(act):
                def step(o, d, c, n, b, turn, lat, lat_turn, j):
                    for h in range(2):
                        act.wait_ge(low_ready, lat * 2 + h + 1)
                        nc.scalar.activation(decay[:, h, :, :, :], decay[:, h, :, :, :], ACT.Exp).then_inc(exp_ready, 1)

                plan(act, lambda *_: None, step)

            @block.vector
            def _(v):
                for first in (cb_ready, diff_ready, y_read):
                    v.sem_inc(first, 1)
                ch = Chain(v, dve)
                v.sem_inc(buf_free, 2)

                def update(o, n):
                    v.wait_ge(faded_ready, n + 1)
                    for h in range(2):
                        v.wait_ge(state_mm, n * 2 + h + 1)
                        ins = nc.vector.tensor_tensor(state[:, h * half:(h + 1) * half],
                                                      faded[:, h * half:(h + 1) * half], ps[:, 7, 0:half], ALU.add)
                        ins.then_inc(state_half, 1)
                    v.wait_ge(state_half, n * 2 + 2)
                    v.sem_inc(state_done, 1)

                def context_step(o, d, c, n, b, turn):
                    if turn == o * (steps // 2) and b == 0:
                        if o:
                            v.wait_ge(off_mm, o * CHUNKS)
                        ch.step(nc.vector.memset(state[:, :], 0.0))
                        ch.wait()
                        v.sem_inc(state_done, 1)
                    update(o, n)
                    v.sem_inc(buf_free, 1)

                def step(o, d, c, n, b, turn, lat, lat_turn, j):
                    v.wait_ge(cum_mm, lat * 2 + 1)
                    nc.vector.tensor_copy(chunk_decay[:, :], at("log_decay", c, d)).then_inc(decay_set, 1)
                    v.wait_ge(cb_mm, lat + 1)
                    nc.vector.tensor_tensor(cb[:, :, :], ps[:, 2, :].rearrange("p (g t) -> p g t", g=GROUPS),
                                            k.const("from" if d else "upto").unsqueeze(1).broadcast_to([P, GROUPS, P]),
                                            ALU.mult).then_inc(cb_ready, 1)
                    for h in range(2):
                        v.wait_ge(cum_mm, lat * 2 + h + 2)
                        mine = at("cum", c, d, 6 * h, 6 * h + 6).rearrange("p (b e) -> p b e", b=2)
                        nc.vector.tensor_tensor(decay[:, h, :, :, :],
                                                ps[:, 0:2, 0:3 * P].rearrange("p b (e t) -> p b e t", e=3),
                                                mine.unsqueeze(3).broadcast_to([P, 2, 3, P]),
                                                ALU.subtract).then_inc(diff_ready, 1)
                        v.wait_ge(diff_ready, lat * 2 + h + 2)
                        nc.vector.tensor_scalar(decay[:, h, :, :, :], decay[:, h, :, :, :], 0.0, None,
                                                ALU.min).then_inc(low_ready, 1)
                    v.wait_ge(off_mm, lat + 1)
                    update(o, n)
                    v.wait_ge(cb_ready, lat + 2)
                    for h in range(2):
                        v.wait_ge(exp_ready, lat * 2 + h + 1)
                        nc.vector.tensor_tensor(mix[:, h, :, :, :], decay[:, h, :, :, :],
                                                cb[:, 2 * h:2 * h + 2, :].unsqueeze(2).broadcast_to([P, 2, 3, P]),
                                                ALU.mult).then_inc(mix_ready, 1)
                    both = out[:, :].rearrange("p (b h e) -> p b h e", b=2, e=HD)
                    grown = at("exp_cum", c, d).rearrange("p (b h) -> p b h", b=2).unsqueeze(3)
                    ch.step(nc.vector.tensor_tensor(both, ps[:, 5:7, 0:half].rearrange("p b (h e) -> p b h e", e=HD),
                                                    grown.broadcast_to([P, 2, 6, HD]), ALU.mult))
                    ch.wait()
                    v.wait_ge(diag_mm, lat + 1)
                    nc.vector.tensor_tensor(out[:, :].rearrange("p (b n) -> p b n", b=2), ps[:, 3:5, 0:half],
                                            out[:, :].rearrange("p (b n) -> p b n", b=2), ALU.add).then_inc(y_read, 1)
                    v.wait_ge(y_read, lat + 2)
                    if o == 0:
                        v.wait_ge(skip_ready, lat + 1)
                    yc = y[:, bass.ds(c, 1), :].rearrange("p c n -> p (c n)")
                    ch.step(nc.vector.tensor_tensor(yc, yc, out[:, :], ALU.add))
                    v.sem_inc(buf_free, 1)

                for o, d in enumerate(order):
                    for i in range(CTX_CHUNKS):
                        context_step(o, d, None, o * steps + i, i % 2, o * (steps // 2) + i // 2)
                    with v.Fori(0, CHUNKS // 2) as j, ch.turns(j, CHUNKS // 2, 4):
                        for q in range(2):
                            c = j * 2 + q if d == 0 else j * -2 + (CHUNKS - 1 - q)
                            step(o, d, c, j * 2 + (o * steps + CTX_CHUNKS + q), q, None,
                                 j * 2 + (o * CHUNKS + q), None, j)
                ch.wait()


def stage_ssd_norm(k, y, y_bT):
    nc, a, ring, ps = k.nc, k.a, k.ring, k.ps
    n = SSD_D // P
    full = n + -n % RING
    base = ring.claim(full)
    with k.stage("sn") as (sb, sem):
        z = sb("z", [P, 2, T])
        square, ss = sb("square", [P, SSD_D]), sb("ss", [P, CHUNKS])
        z_ready, z_turned, gated, squared = sem("z_ready"), sem("z_turned"), sem("gated"), sem("squared")
        root, normed, turned, out_ready, dve = (sem(x) for x in ("root", "normed", "turned", "out_ready", "dve"))

        with nc.Block() as block:
            @block.sync
            def _(sp):
                loop_items(sp, n, lambda j, q: ring.load(sp, j * RING + base + q, q, item(a["w_z"], j * RING + q)))
                for q in range(n, full):
                    sp.wait_ge(ring.freed, base + q + 1)
                    sp.sem_inc(ring.landed[q % RING], 16)

            @block.tensor
            def _(pe):
                def project(m):
                    if m >= 2:
                        pe.wait_ge(z_ready, m - 1)
                    ring.arrived(pe, base, m // RING, m % RING)
                    for h, cols in enumerate(HALVES):
                        mm = k.product(m % RING, k.uT, ps[:, 2 * (m % 2) + h, :], cols)
                    mm.then_inc(ring.freed, 1)

                def turn(m):
                    pe.wait_ge(z_ready, m + 1)
                    if m >= 2:
                        pe.wait_ge(gated, m - 1)
                    for c in range(CHUNKS):
                        mm = nc.tensor.transpose(ps[:, 4 + 2 * (m % 2) + c // 4, (c % 4) * P:(c % 4 + 1) * P],
                                                 z[:, m % 2, c * P:(c + 1) * P], k.const("ident"))
                    mm.then_inc(z_turned, 1)

                for m in range(n):
                    project(m)
                    if m:
                        turn(m - 1)
                pe.wait_ge(ring.freed, ring.done(base + n - 1))
                pe.sem_inc(ring.freed, full - n)
                turn(n - 1)
                pe.wait_ge(normed, CHUNKS)
                for m in range(n):
                    if m >= 4:
                        pe.wait_ge(out_ready, m - 3)
                    for c in range(CHUNKS):
                        mm = nc.tensor.transpose(ps[:, 2 * (m % 4) + c // 4, (c % 4) * P:(c % 4 + 1) * P],
                                                 y[:, c, m * P:(m + 1) * P], k.const("ident"))
                    mm.then_inc(turned, 1)

            @block.scalar
            def _(act):
                for m in range(n):
                    act.wait_ge(ring.freed, ring.done(base + m))
                    if m >= 2:
                        act.wait_ge(z_turned, m - 1)
                    nc.scalar.activation(z[:, m % 2, :], ps[:, 2 * (m % 2):2 * (m % 2) + 2, :].rearrange("p b n -> p (b n)"),
                                         ACT.Silu).then_inc(z_ready, 1)
                act.wait_ge(gated, n)
                for c in range(CHUNKS):
                    if c:
                        act.wait_ge(squared, c)
                    nc.scalar.activation(square[:, :], y[:, c, :], ACT.Square,
                                         accum_out=ss[:, c:c + 1]).then_inc(squared, 1)
                act.wait_ge(dve, 1)
                nc.scalar.activation(ss[:, :], ss[:, :], ACT.Sqrt).then_inc(root, 1)
                for m in range(n):
                    act.wait_ge(turned, m + 1)
                    nc.scalar.activation(y_bT[:, m, :], ps[:, 2 * (m % 4):2 * (m % 4) + 2, :].rearrange("p b n -> p (b n)"),
                                         ACT.Identity, scale=k.col("ssd_norm_g", m)).then_inc(out_ready, 1)

            @block.vector
            def _(v):
                for m in range(n):
                    v.wait_ge(z_turned, m + 1)
                    part = y[:, :, m * P:(m + 1) * P]
                    nc.vector.tensor_tensor(part, part, ps[:, 4 + 2 * (m % 2):6 + 2 * (m % 2), :].rearrange(
                        "p b (c m) -> p (b c) m", m=P), ALU.mult).then_inc(gated, 1)
                v.wait_ge(squared, CHUNKS)
                ch = Chain(v, dve)
                ch.step(nc.vector.tensor_scalar(ss[:, :], ss[:, :], 1.0 / SSD_D, EPS, ALU.mult, ALU.add))
                v.wait_ge(root, 1)
                ch.step(nc.vector.reciprocal(ss[:, :], ss[:, :]))
                ch.wait()
                for c in range(CHUNKS):
                    nc.vector.tensor_scalar(y[:, c, :], y[:, c, :], ss[:, c:c + 1], None, ALU.mult).then_inc(normed, 1)


def stage_merge(k, name, branch, gate, yT, kt, merged, first):
    nc, a, ring, ps = k.nc, k.a, k.ring, k.ps
    base = ring.claim(2 * KT)
    with k.stage(name) as (sb, sem):
        gates, prod = sb("gates", [P, 2, T]), sb("prod", [P, 2, T])
        gate_ready, prod_ready, prod_free, gate_free = (sem(x) for x in (
            "gate_ready", "prod_ready", "prod_free", "gate_free"))
        added = sem("added")

        with nc.Block() as block:
            @block.sync
            def _(sp):
                with sp.Fori(0, KT // 2) as j:
                    for b in range(2):
                        at = j * RING + base + 2 * b
                        ring.load(sp, at, 2 * b, item(a["w_gate"], j * 2 + (gate * KT + b)))
                        ring.load(sp, at + 1, 2 * b + 1, item(a["w_br_" + branch], j * 2 + b), kt * P)

            @block.tensor
            def _(pe):
                with pe.Fori(0, KT // 2) as j:
                    for b in range(2):
                        ring.arrived(pe, base, j, 2 * b)
                        pe.wait_ge(gate_free, j * 2 + b + 1)
                        for h, cols in enumerate(HALVES):
                            mm = k.product(2 * b, k.uT, ps[:, 4 * b + h, :], cols)
                        mm.then_inc(ring.freed, 1)
                        ring.arrived(pe, base, j, 2 * b + 1)
                        pe.wait_ge(prod_free, j * 2 + b + 1)
                        for h, cols in enumerate(HALVES):
                            mm = k.product(2 * b + 1, yT, ps[:, 4 * b + 2 + h, :], cols, kt)
                        mm.then_inc(ring.freed, 1)

            @block.scalar
            def _(act):
                act.sem_inc(gate_free, 2)
                with act.Fori(0, KT // 2) as j:
                    for b in range(2):
                        act.wait_ge(ring.freed, j * RING + ring.done(base + 2 * b))
                        act.wait_ge(prod_free, j * 2 + b + 1)
                        nc.scalar.activation(gates[:, b, :], ps[:, 4 * b:4 * b + 2, :].rearrange("p b n -> p (b n)"),
                                             ACT.Sigmoid).then_inc(gate_ready, 1)
                        act.wait_ge(gate_ready, j * 2 + b + 1)
                        act.sem_inc(gate_free, 1)

            @block.vector
            def _(v):
                v.sem_inc(prod_free, 2)
                with v.Fori(0, KT // 2) as j:
                    for b in range(2):
                        v.wait_ge(gate_ready, j * 2 + b + 1)
                        v.wait_ge(ring.freed, j * RING + ring.done(base + 2 * b + 1))
                        mine = merged[:, bass.ds(j * 2 + b, 1), :].rearrange("p k t -> p (k t)")
                        if not first:
                            v.wait_ge(added, j * 2 + b + 1)
                        dst = mine if first else prod[:, b, :]
                        nc.vector.tensor_tensor(dst, gates[:, b, :],
                                                ps[:, 4 * b + 2:4 * b + 4, :].rearrange("p b n -> p (b n)"),
                                                ALU.mult).then_inc(prod_ready, 1)
                        v.wait_ge(prod_ready, j * 2 + b + 1)
                        v.sem_inc(prod_free, 1)

            if not first:
                @block.gpsimd
                def _(pool):
                    pool.sem_inc(added, 2)
                    with pool.Fori(0, KT // 2) as j:
                        for b in range(2):
                            pool.wait_ge(prod_ready, j * 2 + b + 1)
                            mine = merged[:, bass.ds(j * 2 + b, 1), :].rearrange("p k t -> p (k t)")
                            nc.gpsimd.tensor_tensor(mine, mine, prod[:, b, :], ALU.add).then_inc(added, 1)


def hyena_stages(k, y_cT):
    with ExitStack() as ctx:
        q_tok = k.resident(ctx)("q_tok", [P, TT, 3 * HY_D])
        stage_project_conv(k, "hp", k.a["w_hy"], 12, "hy_short_w", "hy_short_b", ACT.Identity, tok_sbuf=q_tok)
        stage_long_conv(k, q_tok, y_cT)


def stage_long_conv(k, q_tok, y_cT):
    nc, a, ring, ps = k.nc, k.a, k.ring, k.ps
    base = ring.claim(2 * 2 * 2 * TT)
    orders = 2
    with k.stage("lc") as (sb, sem):
        spec = sb("spec", [P, 2, 3, HY_D])
        prod = sb("prod", [P, 4, HY_D])
        zf = sb("zf", [P, TT, 2, HY_D])
        bias = sb("bias", [P, 2, HY_D])
        bias_in, spec_in = sem("bias_in"), [sem("spec_in0"), sem("spec_in1")]
        spec_free, freq_free, time_free = sem("spec_free"), sem("freq_free"), sem("time_free")
        dve, z_ready, zf_ready, skip_ready, turned, out_ready = (sem(x) for x in (
            "dve", "z_ready", "zf_ready", "skip_ready", "turned", "out_ready"))
        z = q_tok[:, :, 0:HY_D]

        with nc.Block() as block:
            @block.sync
            def _(sp):
                sp.dma_start(bias[:, :, :].rearrange("p o c -> p (o c)"), k.row("hy_bias")).then_inc(bias_in, 16)
                for o in range(orders):
                    for way, table in enumerate(("dft", "idft")):
                        with sp.Fori(0, 2 * TT // RING) as j:
                            for slot in range(RING):
                                at = base + (2 * o + way) * 2 * TT + slot
                                ring.load(sp, j * RING + at, slot, item(a[table], j * RING + slot))

            @block.gpsimd
            def _(pool):
                for o in range(orders):
                    with pool.Fori(0, TT // 2) as j:
                        for b in range(2):
                            pool.wait_ge(spec_free, j * 2 + (o * TT + b + 1))
                            src = a["spectra"][bass.ds(j * 2 + b, 1), :, :, o * HY_D:(o + 1) * HY_D]
                            pool.dma_start(spec[:, b, :, :], src.rearrange("o p q c -> p (o q) c")).then_inc(spec_in[b], 16)

            @block.tensor
            def _(pe):
                for o in range(orders):
                    pe.wait_ge(z_ready, o * TT)
                    at = base + 4 * o * TT
                    with pe.Fori(0, TT // 2) as j:
                        for b in range(2):
                            pe.wait_ge(freq_free, j * 2 + (o * TT + b + 1))
                            for part in range(2):
                                ring.arrived(pe, at, j, 2 * b + part)
                                k.product(2 * b + part, z, ps[:, 2 * b + part, :], (0, HY_D)).then_inc(ring.freed, 1)
                    pe.wait_ge(zf_ready, (o + 1) * TT)
                    at = base + (4 * o + 2) * TT
                    with pe.Fori(0, TT // 2) as j:
                        for b in range(2):
                            pe.wait_ge(time_free, j * 2 + (o * TT + b + 1))
                            for part in range(2):
                                ring.arrived(pe, at, j, 2 * b + part)
                                for kt in range(KT):
                                    mm = nc.tensor.matmul(ps[:, 4 + b, :], ring.buf[:, 2 * b + part, kt * P:(kt + 1) * P],
                                                          zf[:, kt, part, :], start=(part == 0 and kt == 0),
                                                          stop=(part == 1 and kt == KT - 1))
                                mm.then_inc(ring.freed, 1)
                pe.wait_ge(z_ready, orders * TT)
                for m in range(HY_D // P):
                    for t in range(TT):
                        mm = nc.tensor.transpose(ps[:, 2 * m + t // 4, (t % 4) * P:(t % 4 + 1) * P],
                                                 z[:, t, m * P:(m + 1) * P], k.const("ident"))
                    mm.then_inc(turned, 1)

            @block.scalar
            def _(act):
                for m in range(HY_D // P):
                    act.wait_ge(turned, m + 1)
                    nc.scalar.copy(y_cT[:, m, :], ps[:, 2 * m:2 * m + 2, :].rearrange("p b n -> p (b n)")
                                   ).then_inc(out_ready, 1)

            @block.vector
            def _(v):
                ch = Chain(v, dve)
                v.sem_inc(spec_free, 2)
                v.sem_inc(freq_free, 2)
                v.sem_inc(time_free, 2)
                v.wait_ge(bias_in, 16)
                for o in range(orders):
                    at = base + 4 * o * TT
                    with v.Fori(0, TT // 2) as j, ch.turns(j, TT // 2, 2 * 4):
                        for b in range(2):
                            v.wait_ge(spec_in[b], j * 16 + (o * TT // 2 + 1) * 16)
                            v.wait_ge(ring.freed, j * RING + ring.done(at + 2 * b + 1))
                            for n, (part, q) in enumerate(((0, 0), (1, 1), (0, 1), (1, 2))):
                                ch.step(nc.vector.tensor_tensor(prod[:, n, :], ps[:, 2 * b + part, :],
                                                                spec[:, b, q, :], ALU.mult))
                            ch.wait()
                            v.sem_inc(spec_free, 1)
                            v.sem_inc(freq_free, 1)
                            here = zf[:, bass.ds(j * 2 + b, 1), :, :].rearrange("p k r c -> p (k r) c")
                            for part, op in enumerate((ALU.subtract, ALU.add)):
                                ins = nc.vector.tensor_tensor(here[:, part, :], prod[:, 2 * part, :],
                                                              prod[:, 2 * part + 1, :], op)
                            ins.then_inc(zf_ready, 1)
                            v.wait_ge(zf_ready, j * 2 + (o * TT + b + 1))
                    at = base + (4 * o + 2) * TT
                    with v.Fori(0, TT // 2) as j, ch.turns(j, TT // 2, 2 * 2):
                        for b in range(2):
                            row = q_tok[:, bass.ds(j * 2 + b, 1), :].rearrange("p t c -> p (t c)")
                            zt, gate = row[:, 0:HY_D], row[:, (o + 1) * HY_D:(o + 2) * HY_D]
                            ch.step(nc.vector.tensor_tensor(prod[:, b, :], zt, bias[:, o, :], ALU.mult))
                            ch.wait()
                            v.wait_ge(ring.freed, j * RING + ring.done(at + 2 * b + 1))
                            ch.step(nc.vector.tensor_tensor(prod[:, b, :], prod[:, b, :], ps[:, 4 + b, :], ALU.add))
                            ch.wait()
                            v.sem_inc(time_free, 1)
                            nc.vector.tensor_tensor(zt, prod[:, b, :], gate, ALU.mult).then_inc(z_ready, 1)
                            v.wait_ge(z_ready, j * 2 + (o * TT + b + 1))


def stage_conformer_short(k, y_aT, y_dT):
    nc, a, ring, ps = k.nc, k.a, k.ring, k.ps
    tiles = CONF_D // P
    rows = T // GRID_W
    centre = CONF_K // 2
    base_a = ring.claim(2 * tiles)
    base_d = ring.claim(3 * tiles)
    with k.stage("cs") as (sb, sem):
        sig, val = sb("sig", [P, 2, T]), sb("val", [P, 2, T])
        mean, rstd, squares = sb("mean", [P, T]), sb("rstd", [P, T]), sb("squares", [P, tiles, T])
        cg, line, conv = sb("cg", [P, 2, T]), sb("line", [P, T + 2]), sb("conv", [P, T])
        sig_ready, val_ready, dve = sem("sig_ready"), sem("val_ready"), sem("dve")
        conf_ready, sum_mm, centred = sem("conf_ready"), sem("sum_mm"), sem("centred")
        squared, var_ready, root = sem("squared"), sem("var_ready"), sem("root")
        scaled, silu_done = sem("scaled"), sem("silu_done")
        cg_ready, xv_read, bg_read = sem("cg_ready"), sem("xv_read"), sem("bg_read")

        def banks(b):
            return ps[:, b:b + 2, :].rearrange("p b n -> p (b n)")

        with nc.Block() as block:
            @block.sync
            def _(sp):
                with sp.Fori(0, 2 * tiles // RING) as j:
                    for slot in range(RING):
                        ring.load(sp, j * RING + base_a + slot, slot, item(a["w_conf"], j * RING + slot))
                with sp.Fori(0, 3 * tiles // RING) as j:
                    for slot in range(RING):
                        ring.load(sp, j * RING + base_d + slot, slot, item(a["w_sc"], j * RING + slot))

            @block.tensor
            def _(pe):
                with pe.Fori(0, tiles // 2) as j:
                    for b in range(2):
                        pe.wait_ge(val_ready, j * 2 + b + 1)
                        for part in range(2):
                            ring.arrived(pe, base_a, j, 2 * b + part)
                            for h, cols in enumerate(HALVES):
                                mm = k.product(2 * b + part, k.uT, ps[:, 4 * b + 2 * part + h, :], cols)
                            mm.then_inc(ring.freed, 1)
                pe.wait_ge(val_ready, tiles + 2)

                def short(i):
                    for part, (read, ahead) in enumerate(((cg_ready, 0), (xv_read, 0), (bg_read, 0))):
                        m = 3 * i + part
                        if i:
                            pe.wait_ge(read, i)
                        ring.arrived(pe, base_d, m // RING, m % RING)
                        for h, cols in enumerate(HALVES):
                            mm = k.product(m % RING, k.uT, ps[:, 2 * part + h, :], cols)
                        mm.then_inc(ring.freed, 1)

                def channel_sums(src):
                    for h, (lo, hi) in enumerate(HALVES):
                        for t in range(tiles):
                            mm = nc.tensor.matmul(ps[:, 6 + h, :], k.ones[:, :], src[:, t, lo:hi],
                                                  start=(t == 0), stop=(t == tiles - 1))
                    mm.then_inc(sum_mm, 1)

                short(0)
                short(1)
                pe.wait_ge(conf_ready, tiles)
                channel_sums(y_aT)
                short(2)
                pe.wait_ge(squared, tiles)
                channel_sums(squares)
                short(3)

            @block.scalar
            def _(act):
                with act.Fori(0, tiles // 2) as j:
                    for b in range(2):
                        act.wait_ge(ring.freed, j * RING + ring.done(base_a + 2 * b + 1))
                        act.wait_ge(val_ready, j * 2 + b + 1)
                        nc.scalar.activation(sig[:, b, :], banks(4 * b + 2), ACT.Sigmoid).then_inc(sig_ready, 1)

                def copy_cg(i):
                    act.wait_ge(ring.freed, ring.done(base_d + 3 * i))
                    if i >= 2:
                        act.wait_ge(xv_read, i - 1)
                    nc.scalar.copy(cg[:, i % 2, :], banks(0)).then_inc(cg_ready, 1)

                copy_cg(0)
                copy_cg(1)
                for t in range(tiles):
                    act.wait_ge(centred, t + 1)
                    nc.scalar.activation(squares[:, t, :], y_aT[:, t, :], ACT.Square).then_inc(squared, 1)
                copy_cg(2)
                act.wait_ge(var_ready, 1)
                nc.scalar.activation(rstd[:, :], rstd[:, :], ACT.Sqrt).then_inc(root, 1)
                copy_cg(3)
                for t in range(tiles):
                    act.wait_ge(scaled, t + 1)
                    nc.scalar.activation(y_aT[:, t, :], y_aT[:, t, :], ACT.Silu, bias=k.col("conf_ln_b", t),
                                         scale=k.col("conf_ln_g", t)).then_inc(silu_done, 1)
                act.wait_ge(silu_done, tiles)

            @block.vector
            def _(v):
                ch = Chain(v, dve)
                v.sem_inc(val_ready, 2)
                ch.step(nc.vector.memset(line[:, :], 0.0))
                with v.Fori(0, tiles // 2) as j, ch.turns(j, tiles // 2, 2 * (CONF_K - 1)):
                    for b in range(2):
                        t = j * 2 + b
                        v.wait_ge(sig_ready, t + 1)
                        nc.vector.tensor_tensor(val[:, b, :], sig[:, b, :], banks(4 * b), ALU.mult).then_inc(val_ready, 1)
                        v.wait_ge(val_ready, t + 3)
                        acc = y_aT[:, bass.ds(t, 1), :].rearrange("p k t -> p (k t)")

                        def tap(i):
                            return k.col("conf_dw_w", 0, CONF_K * tiles)[:, bass.ds(t * CONF_K + i, 1)]

                        ch.step(nc.vector.tensor_scalar(acc, val[:, b, :], tap(centre),
                                                        k.col("conf_dw_b", 0, tiles)[:, bass.ds(t, 1)], ALU.mult, ALU.add))
                        others = [i for i in range(CONF_K) if i != centre]
                        for i in others:
                            s = i - centre
                            lo, hi = max(0, -s) * GRID_W, (rows - max(0, s)) * GRID_W
                            ch.wait()
                            ins = nc.vector.scalar_tensor_tensor(
                                out=acc[:, lo:hi], in0=val[:, b, lo + s * GRID_W:hi + s * GRID_W], scalar=tap(i),
                                in1=acc[:, lo:hi], op0=ALU.mult, op1=ALU.add)
                            if i == others[-1]:
                                ins.then_inc(conf_ready, 1)
                            else:
                                ch.step(ins)

                def short(i):
                    v.wait_ge(ring.freed, ring.done(base_d + 3 * i + 1))
                    v.wait_ge(cg_ready, i + 1)
                    nc.vector.tensor_tensor(line[:, 1:T + 1], cg[:, i % 2, :], banks(2), ALU.mult).then_inc(xv_read, 1)
                    v.wait_ge(xv_read, i + 1)
                    taps = [k.col("sc_conv_w", 3 * i + n) for n in range(3)]
                    ch.step(nc.vector.tensor_scalar(conv[:, :], line[:, 0:T], taps[0], None, ALU.mult))
                    for n in (1, 2):
                        ch.wait()
                        ch.step(nc.vector.scalar_tensor_tensor(out=conv[:, :], in0=line[:, n:T + n], scalar=taps[n],
                                                               in1=conv[:, :], op0=ALU.mult, op1=ALU.add))
                    ch.wait()
                    v.wait_ge(ring.freed, ring.done(base_d + 3 * i + 2))
                    nc.vector.tensor_tensor(y_dT[:, i, :], conv[:, :], banks(4), ALU.mult).then_inc(bg_read, 1)

                short(0)
                short(1)
                v.wait_ge(sum_mm, 1)
                v.wait_ge(conf_ready, tiles)
                ch.step(nc.vector.tensor_scalar(mean[:, :], banks(6), 1.0 / CONF_D, None, ALU.mult))
                ch.wait()
                for t in range(tiles):
                    nc.vector.tensor_tensor(y_aT[:, t, :], y_aT[:, t, :], mean[:, :], ALU.subtract).then_inc(centred, 1)
                short(2)
                v.wait_ge(sum_mm, 2)
                nc.vector.tensor_scalar(rstd[:, :], banks(6), 1.0 / CONF_D, EPS, ALU.mult, ALU.add).then_inc(var_ready, 1)
                v.wait_ge(root, 1)
                ch.step(nc.vector.reciprocal(rstd[:, :], rstd[:, :]))
                ch.wait()
                for t in range(tiles):
                    nc.vector.tensor_tensor(y_aT[:, t, :], y_aT[:, t, :], rstd[:, :], ALU.mult).then_inc(scaled, 1)
                short(3)
                v.wait_ge(bg_read, tiles)


class LayerNorm:

    def __init__(self, k, sb, sem, g_row, b_row):
        self.k, self.g, self.b = k, g_row, b_row
        self.stats, self.mv = sb("ln_stats", [P, 2, 6]), sb("ln_mv", [P, 2])
        self.var, self.root = sem("ln_var"), sem("ln_root")

    def scalar(self, act, n):
        act.wait_ge(self.var, n + 1)
        self.k.nc.scalar.activation(self.mv[:, 1:2], self.mv[:, 1:2], ACT.Sqrt).then_inc(self.root, 1)

    def vector(self, v, ch, s, n, out, last_sem):
        nc = self.k.nc
        for h, (lo, hi) in enumerate(HALVES):
            ch.step(nc.vector.bn_stats(self.stats[:, h, :], s[:, lo:hi]))
        ch.wait()
        ch.step(nc.vector.bn_aggr(self.mv[:, :], self.stats[:, :, :]))
        ch.wait()
        nc.vector.tensor_scalar(self.mv[:, 1:2], self.mv[:, 1:2], EPS, None, ALU.add).then_inc(self.var, 1)
        v.wait_ge(self.root, n + 1)
        ch.step(nc.vector.reciprocal(self.mv[:, 1:2], self.mv[:, 1:2]))
        ch.wait()
        ch.step(nc.vector.tensor_scalar(s, s, self.mv[:, 0:1], self.mv[:, 1:2], ALU.subtract, ALU.mult))
        ch.wait()
        ch.step(nc.vector.tensor_tensor(s, s, self.g, ALU.mult))
        ch.wait()
        nc.vector.tensor_tensor(out, s, self.b, ALU.add).then_inc(last_sem, 1)


def tail_stages(k, merged):
    with ExitStack() as ctx:
        sb = k.resident(ctx)
        rows = sb("mod_rows", [P, 4, D])
        weights, dest = sb("weights", [P, 2, TT]), sb("dest", [P, 2, TT], I32)
        plan = sb("plan", [1, SLOTS + 1], I32)
        with ExitStack() as inner:
            logits = k.resident(inner)("logits", [P, TT, 36])
            stage_output(k, merged, rows, logits)
            stage_route(k, logits, weights, dest, plan)
        stage_scatter(k, dest)
        stage_experts(k, plan, merged)
        stage_combine(k, rows, weights, dest)


def stage_output(k, merged, rows, logits):
    nc, a, ps = k.nc, k.a, k.ps
    u = k.uT
    with k.stage("out") as (sb, sem):
        w_out, w_rt = sb("w_out", [P, KT, D]), sb("w_rt", [P, KT, 36])
        ln_g, ln_b, rt_b = sb("ln_g", [P, D]), sb("ln_b", [P, D]), sb("rt_b", [P, 36])
        x, h1, s = sb("x", [P, 2, D]), sb("h1", [P, 2, D]), sb("s", [P, D])
        u_chan = sb("u_chan", [P, KT, P])
        ln = LayerNorm(k, sb, sem, ln_g[:, :], ln_b[:, :])
        w_in, small_in, x_in = sem("w_in"), sem("small_in"), [sem("x_in0"), sem("x_in1")]
        rows_mm, rows_ready, mix_mm, dve = sem("rows_mm"), sem("rows_ready"), sem("mix_mm"), sem("dve")
        mix_read, x_used, h_ready, h_out = sem("mix_read"), sem("x_used"), sem("h_ready"), [sem("h_out0"), sem("h_out1")]
        u_ready, u_turned, u_chan_ready, logit_mm, logit_ready = (sem(n) for n in (
            "u_ready", "u_turned", "u_chan_ready", "logit_mm", "logit_ready"))

        with nc.Block() as block:
            @block.sync
            def _(sp):
                small = ((w_rt[:, :, :], a["w_rt"]), (ln_g[:, :], k.row("ln_g1")), (ln_b[:, :], k.row("ln_b1")),
                         (rt_b[:, :], k.row("rt_b")))
                sp.dma_start(w_out[:, :, :], a["w_out"]).then_inc(w_in, 16)
                for dst, src in small:
                    sp.dma_start(dst, src).then_inc(small_in, 16)
                for t in range(TT):
                    if t >= 2:
                        sp.wait_ge(x_used, t - 1)
                    sp.dma_start(x[:, t % 2, :], a["x"][t * P:(t + 1) * P, :]).then_inc(x_in[t % 2], 16)

            @block.gpsimd
            def _(pool):
                for t in range(TT):
                    pool.wait_ge(h_ready, t + 1)
                    pool.dma_start(a["h1"][t], h1[:, t % 2, :]).then_inc(h_out[t % 2], 16)
                for b in range(2):
                    pool.wait_ge(h_out[b], 16 * TT // 2)

            @block.tensor
            def _(pe):
                for part in range(4):
                    for kt in range(KT):
                        m = (2 + part) * KT + kt
                        mm = nc.tensor.matmul(ps[:, 2 * part + kt // 4, (kt % 4) * P:(kt % 4 + 1) * P],
                                              k.mod[:, m, 0:1].broadcast_to([P, P]), k.const("ident"),
                                              start=True, stop=True)
                    mm.then_inc(rows_mm, 1)
                pe.wait_ge(w_in, 16)
                pe.wait_ge(small_in, 64)
                pe.wait_ge(rows_ready, 4)

                def project(t):
                    if t >= 2:
                        pe.wait_ge(mix_read, t - 1)
                    for h, (lo, hi) in enumerate(HALVES):
                        for kt in range(KT):
                            mm = nc.tensor.matmul(ps[:, 2 * (t % 2) + h, :], merged[:, kt, t * P:(t + 1) * P],
                                                  w_out[:, kt, lo:hi], start=(kt == 0), stop=(kt == KT - 1))
                    mm.then_inc(mix_mm, 1)

                def turn(t):
                    pe.wait_ge(u_ready, t + 1)
                    if t:
                        pe.wait_ge(u_chan_ready, t)
                    for kt in range(KT):
                        mm = nc.tensor.transpose(ps[:, 4 + kt // 4, (kt % 4) * P:(kt % 4 + 1) * P],
                                                 u[:, t, kt * P:(kt + 1) * P], k.const("ident"))
                    mm.then_inc(u_turned, 1)

                def route(t):
                    pe.wait_ge(u_chan_ready, t + 1)
                    if t:
                        pe.wait_ge(logit_ready, t)
                    for kt in range(KT):
                        mm = nc.tensor.matmul(ps[:, 6, 0:36], u_chan[:, kt, :], w_rt[:, kt, :],
                                              start=(kt == 0), stop=(kt == KT - 1))
                    mm.then_inc(logit_mm, 1)

                for t in range(TT + 2):
                    if t < TT:
                        project(t)
                    if t >= 2:
                        route(t - 2)
                    if 1 <= t <= TT:
                        turn(t - 1)

            @block.scalar
            def _(act):
                for part in range(4):
                    act.wait_ge(rows_mm, part + 1)
                    nc.scalar.copy(rows[:, part, :], ps[:, 2 * part:2 * part + 2, :].rearrange("p b n -> p (b n)")
                                   ).then_inc(rows_ready, 1)
                for t in range(TT):
                    ln.scalar(act, t)
                    act.wait_ge(u_turned, t + 1)
                    if t:
                        act.wait_ge(logit_mm, t)
                    nc.scalar.copy(u_chan[:, :, :], ps[:, 4:6, :].rearrange("p b (k n) -> p (b k) n", n=P)
                                   ).then_inc(u_chan_ready, 1)

            @block.vector
            def _(v):
                ch = Chain(v, dve)
                v.wait_ge(small_in, 64)
                v.wait_ge(rows_ready, 4)

                def take_logits(t):
                    v.wait_ge(logit_mm, t + 1)
                    nc.vector.tensor_tensor(logits[:, t, :], ps[:, 6, 0:36], rt_b[:, :], ALU.add).then_inc(logit_ready, 1)

                for t in range(TT):
                    b = t % 2
                    v.wait_ge(mix_mm, t + 1)
                    if t:
                        v.wait_ge(u_ready, t)
                    nc.vector.tensor_tensor(s[:, :], ps[:, 2 * b:2 * b + 2, :].rearrange("p b n -> p (b n)"),
                                            rows[:, 0, :], ALU.mult).then_inc(mix_read, 1)
                    v.wait_ge(mix_read, t + 1)
                    v.wait_ge(x_in[b], 16 * (t // 2 + 1))
                    nc.vector.scalar_tensor_tensor(out=s[:, :], in0=x[:, b, :], scalar=ALPHA, in1=s[:, :],
                                                   op0=ALU.mult, op1=ALU.add).then_inc(x_used, 1)
                    v.wait_ge(x_used, t + 1)
                    if t >= 2:
                        v.wait_ge(h_out[b], 16 * (t // 2))
                    ln.vector(v, ch, s[:, :], t, h1[:, b, :], h_ready)
                    v.wait_ge(h_ready, t + 1)
                    ch.step(nc.vector.tensor_tensor(s[:, :], h1[:, b, :], rows[:, 2, :], ALU.mult))
                    ch.wait()
                    nc.vector.tensor_tensor(u[:, t, :], s[:, :], rows[:, 1, :], ALU.add).then_inc(u_ready, 1)
                    if t >= 2:
                        take_logits(t - 2)
                take_logits(TT - 2)
                take_logits(TT - 1)
                v.wait_ge(logit_ready, TT)


def stage_route(k, logits, weights, dest, plan):
    nc, ps = k.nc, k.ps
    E, G = EXPERTS, MOE_GROUPS
    with k.stage("rt") as (sb, sem):
        top = sb("top", [P, TT])
        miss_g, cand_g = sb("miss_g", [P, TT, G]), sb("cand_g", [P, TT, G])
        group, g_exp, g_prob = sb("group", [P, TT]), sb("g_exp", [P, TT, G]), sb("g_prob", [P, TT])
        own, miss, cand = sb("own", [P, TT, E]), sb("miss", [P, TT, E]), sb("cand", [P, TT, E])
        best, which = sb("best", [P, 2, TT]), sb("which", [P, TT])
        hot = sb("hot", [P, 2, TT, E])
        chosen, before = sb("chosen", [P, TT, E]), sb("before", [P, TT, E])
        every, count = sb("every", [P, E]), sb("count", [P, E])
        blocks, scan = sb("blocks", [P, E]), sb("scan", [P, 2, E])
        first, place = sb("first", [P, E]), sb("place", [P, TT, E])
        dest_f, owner, owner_e = sb("dest_f", [P, 2, TT]), sb("owner", [1, SLOTS, E]), sb("owner_e", [1, SLOTS])
        dve, g_ready, g_exp_ready, d_ready, d_exp_ready, rank_in, rank_mm = (sem(n) for n in (
            "dve", "g_ready", "g_exp_ready", "d_ready", "d_exp_ready", "rank_in", "rank_mm"))
        iota = k.const("iota")

        def to_tiles(row, width):
            return row.unsqueeze(1).broadcast_to([P, TT, width])

        def wide(v, width):
            return v.unsqueeze(2).broadcast_to([P, TT, width])

        with nc.Block() as block:
            @block.tensor
            def _(pe):
                pe.wait_ge(rank_in, 1)
                flat = "p t e -> p (t e)"
                nc.tensor.matmul(ps[:, 0, 0:TT * E], k.ones[:, :], before[:, :, :].rearrange(flat), start=True, stop=False)
                nc.tensor.matmul(ps[:, 0, 0:TT * E], k.const("before"), chosen[:, :, :].rearrange(flat),
                                 start=False, stop=True)
                nc.tensor.matmul(ps[:, 1, 0:E], k.ones[:, :], every[:, :], start=True, stop=True).then_inc(rank_mm, 1)

            @block.scalar
            def _(act):
                act.wait_ge(g_ready, 1)
                nc.scalar.activation(g_exp[:, :, :], cand_g[:, :, :], ACT.Exp).then_inc(g_exp_ready, 1)
                act.wait_ge(d_ready, 1)
                nc.scalar.activation(which[:, :], which[:, :], ACT.Exp).then_inc(d_exp_ready, 1)

            @block.vector
            def _(v):
                ch = Chain(v, dve)

                def do(ins):
                    ch.step(ins)
                    ch.wait()

                tt, ts, stt = nc.vector.tensor_tensor, nc.vector.tensor_scalar, nc.vector.scalar_tensor_tensor
                reduce = nc.vector.tensor_reduce
                g = logits[:, :, 0:G]
                do(reduce(top[:, :], g, AX.X, ALU.max))
                do(tt(miss_g[:, :, :], g, wide(top[:, :], G), ALU.is_lt))
                tt(cand_g[:, :, :], g, wide(top[:, :], G), ALU.subtract).then_inc(g_ready, 1)
                v.wait_ge(g_exp_ready, 1)
                do(reduce(g_prob[:, :], g_exp[:, :, :], AX.X, ALU.add))
                do(nc.vector.reciprocal(g_prob[:, :], g_prob[:, :]))
                do(stt(out=cand_g[:, :, :], in0=miss_g[:, :, :], scalar=100.0, in1=to_tiles(iota[:, 0:G], G),
                       op0=ALU.mult, op1=ALU.add))
                do(reduce(group[:, :], cand_g[:, :, :], AX.X, ALU.min))
                do(tt(miss_g[:, :, :], to_tiles(iota[:, 0:G], G), wide(group[:, :], G), ALU.not_equal))
                do(ts(miss_g[:, :, :], miss_g[:, :, :], -BIG, None, ALU.mult))
                by_group = "p t (g e) -> p t g e"
                for t in range(TT):
                    ch.step(tt(own[:, t, :].rearrange("p (g e) -> p g e", g=G),
                               logits[:, t, G:G + E].rearrange("p (g e) -> p g e", g=G),
                               miss_g[:, t, :].unsqueeze(2).broadcast_to([P, G, MOE_EPG]), ALU.add))
                ch.wait()
                for r in range(2):
                    do(reduce(best[:, r, :], own[:, :, :], AX.X, ALU.max))
                    do(tt(miss[:, :, :], own[:, :, :], wide(best[:, r, :], E), ALU.is_lt))
                    do(stt(out=cand[:, :, :], in0=miss[:, :, :], scalar=100.0, in1=to_tiles(iota[:, 0:E], E),
                           op0=ALU.mult, op1=ALU.add))
                    do(reduce(which[:, :], cand[:, :, :], AX.X, ALU.min))
                    do(tt(hot[:, r, :, :], to_tiles(iota[:, 0:E], E), wide(which[:, :], E), ALU.is_equal))
                    if r == 0:
                        do(stt(out=own[:, :, :], in0=hot[:, 0, :, :], scalar=-3 * BIG, in1=own[:, :, :],
                               op0=ALU.mult, op1=ALU.add))
                tt(which[:, :], best[:, 1, :], best[:, 0, :], ALU.subtract).then_inc(d_ready, 1)
                v.wait_ge(d_exp_ready, 1)
                do(ts(top[:, :], which[:, :], 1.0, None, ALU.add))
                do(nc.vector.reciprocal(top[:, :], top[:, :]))
                do(tt(weights[:, 0, :], top[:, :], g_prob[:, :], ALU.mult))
                do(tt(weights[:, 1, :], weights[:, 0, :], which[:, :], ALU.mult))
                do(tt(chosen[:, :, :], hot[:, 0, :, :], hot[:, 1, :, :], ALU.add))
                do(nc.vector.memset(before[:, 0, :], 0.0))
                for t in range(1, TT):
                    do(tt(before[:, t, :], before[:, t - 1, :], chosen[:, t - 1, :], ALU.add))
                tt(every[:, :], before[:, TT - 1, :], chosen[:, TT - 1, :], ALU.add).then_inc(rank_in, 1)
                v.wait_ge(rank_mm, 1)
                do(nc.vector.tensor_copy(count[:, :], ps[:, 1, 0:E]))
                do(ts(blocks[:, :], count[:, :], 0.0, None, ALU.is_gt))
                for n in range(1, TT):
                    do(stt(out=blocks[:, :], in0=count[:, :], scalar=float(n * P), in1=blocks[:, :],
                           op0=ALU.is_gt, op1=ALU.add))
                for n, shift in enumerate((1, 2, 4, 8, 16)):
                    dst = scan[:, n % 2, :]
                    old = blocks[:, :] if n == 0 else scan[:, 1 - n % 2, :]
                    do(nc.vector.tensor_copy(dst[:, 0:shift], old[:, 0:shift]))
                    do(tt(dst[:, shift:E], old[:, shift:E], old[:, 0:E - shift], ALU.add))
                ends = scan[:, 0, :]
                do(tt(first[:, :], ends, blocks[:, :], ALU.subtract))
                do(stt(out=place[:, :, :], in0=to_tiles(first[:, :], E), scalar=float(P),
                       in1=ps[:, 0, 0:TT * E].rearrange("p (t e) -> p t e", e=E), op0=ALU.mult, op1=ALU.add))
                for r in range(2):
                    do(tt(cand[:, :, :], hot[:, r, :, :], place[:, :, :], ALU.mult))
                    do(reduce(dest_f[:, r, :], cand[:, :, :], AX.X, ALU.add))
                do(nc.vector.tensor_copy(dest[:, :, :], dest_f[:, :, :]))
                do(tt(owner[:, :, :], ends[0:1, :].unsqueeze(1).broadcast_to([1, SLOTS, E]),
                      iota[0:1, 0:SLOTS].unsqueeze(2).broadcast_to([1, SLOTS, E]), ALU.is_le))
                do(reduce(owner_e[:, :], owner[:, :, :], AX.X, ALU.add))
                do(ts(owner_e[:, :], owner_e[:, :], float(E - 1), None, ALU.min))
                do(nc.vector.tensor_copy(plan[:, 0:SLOTS], owner_e[:, :]))
                do(nc.vector.tensor_copy(plan[:, SLOTS:SLOTS + 1], ends[0:1, E - 1:E]))


def stage_scatter(k, dest):
    nc, a = k.nc, k.a
    with k.stage("sc") as (sb, sem):
        sent = sem("sent")
        with nc.Block() as block:
            @block.gpsimd
            def _(pool):
                pool.wait_ge(k.blank, 16 * k.blank_parts)
                for t in range(TT):
                    for r in range(2):
                        pool.indirect_dma_start(out=a["moe"], out_offset=bass.IndirectOffsetOnAxis(dest[:, r, t:t + 1], 0),
                                                in_=k.uT[:, t, :], in_offset=None).then_inc(sent, 16)
                pool.wait_ge(sent, 2 * TT * 16)


def stage_experts(k, plan, merged):
    nc, a, ps = k.nc, k.a, k.ps
    with k.stage("ex") as (sb, sem):
        w_g, w_u = sb("w_g", [P, 2, KT, FF]), sb("w_u", [P, 2, KT, FF])
        w_d = merged[:, :, :].rearrange("p (b f) d -> p b f d", b=2)
        x, y = k.uT[:, 0:2, :], k.uT[:, 4:6, :]
        x_chan = k.uT[:, 2:4, :].rearrange("p b (k n) -> p b k n", n=P)
        act_g, hid, hid_chan = sb("act_g", [P, FF]), sb("hid", [P, FF]), sb("hid_chan", [P, FF // P, P])
        g_in, u_in, d_in = ([sem(f"{n}{b}") for b in range(2)] for n in ("g_in", "u_in", "d_in"))
        x_in, y_out = [sem("x_in0"), sem("x_in1")], [sem("y_out0"), sem("y_out1")]
        gate_mm, up_mm, x_mm, hid_mm, down_mm = (sem(n) for n in ("gate_mm", "up_mm", "x_mm", "hid_mm", "down_mm"))
        y_free, x_ready, g_ready, hid_ready, hidc_ready, y_ready = (sem(n) for n in (
            "y_free", "x_ready", "g_ready", "hid_ready", "hidc_ready", "y_ready"))

        rows = a["moe"].rearrange("(s p) d -> s p d", p=P)

        def blocks(eng, body):
            n = eng.value_load(plan[0:1, SLOTS:SLOTS + 1], min_val=0, max_val=BLOCKS)
            with eng.Fori(0, SLOTS // 2) as j:
                for b in range(2):
                    with eng.If(j * 2 + b < n):
                        body(j * 2 + b, b, j)

        with nc.Block() as block:
            @block.sync
            def _(sp):
                sp.sem_inc(down_mm, 2)
                sp.dma_start(x[:, 0, :], a["moe"][0:P, :]).then_inc(x_in[0], 16)

                def body(i, b, j):
                    e = sp.value_load(plan[0:1, bass.ds(i, 1)], min_val=0, max_val=EXPERTS - 1)
                    sp.wait_ge(down_mm, i + 1)
                    sp.wait_ge(x_mm, i + 1)
                    after = nc.s_assert_within(i + 1, 1, SLOTS - 1, skip_runtime_bounds_check_because=(
                        "the body runs for i < number of blocks <= BLOCKS < SLOTS only"))
                    sp.dma_start(x[:, 1 - b, :], item(rows, after)).then_inc(x_in[1 - b], 16)
                    for dst, name, s in ((w_g, "ex_g", g_in), (w_u, "ex_u", u_in), (w_d, "ex_d", d_in)):
                        src = a[name][bass.ds(e, 1)].rearrange("o (k p) f -> p (o k) f", p=P)
                        sp.dma_start(dst[:, b, :, :], src).then_inc(s[b], 16)

                blocks(sp, body)

            @block.gpsimd
            def _(pool):
                pool.sem_inc(y_free, 2)

                def body(i, b, j):
                    pool.wait_ge(y_ready, i + 2)
                    pool.dma_start(item(rows, i), y[:, b, :]).then_inc(y_out[b], 16)
                    pool.wait_ge(y_out[b], j * 16 + 16)
                    pool.sem_inc(y_free, 1)

                blocks(pool, body)

            @block.tensor
            def _(pe):
                pe.sem_inc(x_mm, 1)
                pe.sem_inc(hid_mm, 1)
                def turn_x(b):
                    for kt in range(KT):
                        mm = nc.tensor.transpose(ps[:, 2 + kt // 4, (kt % 4) * P:(kt % 4 + 1) * P],
                                                 x[:, b, kt * P:(kt + 1) * P], k.const("ident"))
                    mm.then_inc(x_mm, 1)

                pe.wait_ge(x_in[0], 16)
                turn_x(0)

                def body(i, b, j):
                    pe.wait_ge(x_ready, i + 1)
                    pe.wait_ge(hid_ready, i + 1)
                    for w, arrived, bank, done in ((w_g, g_in, 0, gate_mm), (w_u, u_in, 1, up_mm)):
                        pe.wait_ge(arrived[b], j * 16 + 16)
                        for kt in range(KT):
                            mm = nc.tensor.matmul(ps[:, bank, :], x_chan[:, b, kt, :], w[:, b, kt, :],
                                                  start=(kt == 0), stop=(kt == KT - 1))
                        mm.then_inc(done, 1)
                    pe.wait_ge(x_in[1 - b], j * 16 + 16 + 16 * b)
                    turn_x(1 - b)
                    pe.wait_ge(hid_ready, i + 2)
                    for f in range(FF // P):
                        mm = nc.tensor.transpose(ps[:, 4, f * P:(f + 1) * P], hid[:, f * P:(f + 1) * P], k.const("ident"))
                    mm.then_inc(hid_mm, 1)
                    pe.wait_ge(hidc_ready, i + 1)
                    pe.wait_ge(d_in[b], j * 16 + 16)
                    pe.wait_ge(y_ready, i + 1)
                    for h, (lo, hi) in enumerate(HALVES):
                        for f in range(FF // P):
                            mm = nc.tensor.matmul(ps[:, 5 + h, :], hid_chan[:, f, :], w_d[:, b, f, lo:hi],
                                                  start=(f == 0), stop=(f == FF // P - 1))
                    mm.then_inc(down_mm, 1)

                blocks(pe, body)

            @block.scalar
            def _(act):
                act.sem_inc(y_ready, 1)
                def x_out(b):
                    nc.scalar.copy(x_chan[:, b, :, :], ps[:, 2:4, :].rearrange("p b (k n) -> p (b k) n", n=P)
                                   ).then_inc(x_ready, 1)

                act.wait_ge(x_mm, 2)
                x_out(0)

                def body(i, b, j):
                    act.wait_ge(gate_mm, i + 1)
                    nc.scalar.activation(act_g[:, :], ps[:, 0, :], ACT.Silu).then_inc(g_ready, 1)
                    act.wait_ge(x_mm, i + 3)
                    x_out(1 - b)
                    act.wait_ge(down_mm, i + 3)
                    act.wait_ge(y_free, i + 1)
                    nc.scalar.copy(y[:, b, :], ps[:, 5:7, :].rearrange("p b n -> p (b n)")).then_inc(y_ready, 1)

                blocks(act, body)

            @block.vector
            def _(v):
                v.sem_inc(hid_ready, 1)
                def body(i, b, j):
                    v.wait_ge(g_ready, i + 1)
                    v.wait_ge(up_mm, i + 1)
                    v.wait_ge(hid_mm, i + 1)
                    nc.vector.tensor_tensor(hid[:, :], act_g[:, :], ps[:, 1, :], ALU.mult).then_inc(hid_ready, 1)
                    v.wait_ge(hid_mm, i + 2)
                    nc.vector.tensor_copy(hid_chan[:, :, :], ps[:, 4, :].rearrange("p (f n) -> p f n", n=P)
                                          ).then_inc(hidc_ready, 1)

                blocks(v, body)


def stage_combine(k, rows, weights, dest):
    nc, a = k.nc, k.a
    with k.stage("cb") as (sb, sem):
        y, h1 = sb("y", [P, 2, 2, D]), sb("h1", [P, 2, D])
        ln_g, ln_b = sb("ln_g", [P, D]), sb("ln_b", [P, D])
        s, res = sb("s", [P, 2, D]), sb("res", [P, 2, D])
        ln = LayerNorm(k, sb, sem, ln_g[:, :], ln_b[:, :])
        small_in, y_in, h_in = sem("small_in"), [sem("y_in0"), sem("y_in1")], [sem("h_in0"), sem("h_in1")]
        dve, y_used, ready, out = sem("dve"), sem("y_used"), sem("ready"), [sem("out0"), sem("out1")]

        with nc.Block() as block:
            @block.sync
            def _(sp):
                sp.dma_start(ln_g[:, :], k.row("ln_g2")).then_inc(small_in, 16)
                sp.dma_start(ln_b[:, :], k.row("ln_b2")).then_inc(small_in, 16)
                for t in range(TT):
                    if t >= 2:
                        sp.wait_ge(y_used, t - 1)
                    sp.dma_start(h1[:, t % 2, :], a["h1"][t]).then_inc(h_in[t % 2], 16)

            @block.gpsimd
            def _(pool):
                for t in range(TT):
                    if t >= 2:
                        pool.wait_ge(y_used, t - 1)
                    for r in range(2):
                        pool.indirect_dma_start(out=y[:, t % 2, r, :], out_offset=None, in_=a["moe"],
                                                in_offset=bass.IndirectOffsetOnAxis(dest[:, r, t:t + 1], 0)
                                                ).then_inc(y_in[t % 2], 16)

            @block.scalar
            def _(act):
                for t in range(TT):
                    ln.scalar(act, t)
                    act.wait_ge(ready, t + 1)
                    act.dma_start(a["out"][t * P:(t + 1) * P, :], res[:, t % 2, :]).then_inc(out[t % 2], 16)
                for b in range(2):
                    act.wait_ge(out[b], 16 * TT // 2)

            @block.vector
            def _(v):
                ch = Chain(v, dve)
                v.wait_ge(small_in, 32)
                for t in range(TT):
                    b = t % 2
                    acc = s[:, b, :]
                    v.wait_ge(y_in[b], 32 * (t // 2 + 1))
                    ch.step(nc.vector.tensor_scalar(acc, y[:, b, 0, :], weights[:, 0, t:t + 1], None, ALU.mult))
                    ch.wait()
                    ch.step(nc.vector.scalar_tensor_tensor(out=acc, in0=y[:, b, 1, :], scalar=weights[:, 1, t:t + 1],
                                                           in1=acc, op0=ALU.mult, op1=ALU.add))
                    ch.wait()
                    ch.step(nc.vector.tensor_tensor(acc, acc, rows[:, 3, :], ALU.mult))
                    ch.wait()
                    v.wait_ge(h_in[b], 16 * (t // 2 + 1))
                    nc.vector.scalar_tensor_tensor(out=acc, in0=h1[:, b, :], scalar=ALPHA, in1=acc, op0=ALU.mult,
                                                   op1=ALU.add).then_inc(y_used, 1)
                    v.wait_ge(y_used, t + 1)
                    if t >= 2:
                        v.wait_ge(out[b], 16 * (t // 2))
                    ln.vector(v, ch, acc, t, res[:, b, :], ready)


def build_program(nc, a):
    for name, shape in SCRATCH.items():
        if name not in a:
            a[name] = nc.dram_tensor(name, shape, F32).ap()
    with ExitStack() as ctx:
        k = Kernel(nc, a, ctx)
        filter_stages(k)
        stage_modulate(k)
        merged = k.resident(ctx)("merged", [P, KT, T])
        with ExitStack() as branch:
            y_cT = k.resident(branch)("y_cT", [P, HY_D // P, T])
            hyena_stages(k, y_cT)
            stage_merge(k, "mc", "c", 2, y_cT, HY_D // P, merged, True)
        with ExitStack() as branch:
            y_bT = k.resident(branch)("y_bT", [P, SSD_D // P, T])
            ssd_stages(k, y_bT)
            stage_merge(k, "mb", "b", 1, y_bT, SSD_D // P, merged, False)
        with ExitStack() as branch:
            sb = k.resident(branch)
            y_aT, y_dT = sb("y_aT", [P, CONF_D // P, T]), sb("y_dT", [P, SC_D // P, T])
            stage_conformer_short(k, y_aT, y_dT)
            stage_merge(k, "ma", "a", 0, y_aT, CONF_D // P, merged, False)
            stage_merge(k, "md", "d", 3, y_dT, SC_D // P, merged, False)
        tail_stages(k, merged)


def kernel(**inputs):
    import concourse.bacc as bacc
    from concourse.bass_utils import run_bass_kernel_spmd

    arrays = {f"in_{name}": v for name, v in
              host_arrays(**{name: np.asarray(v) for name, v in inputs.items()}).items()}
    nc = bacc.Bacc("TRN2", target_bir_lowering=False, num_devices=1)
    a = {name[3:]: nc.dram_tensor(name, v.shape, mybir.dt.from_np(v.dtype), kind="ExternalInput").ap()
         for name, v in arrays.items()}
    a["out"] = nc.dram_tensor("out_dram", (T, D), F32, kind="ExternalOutput").ap()
    build_program(nc, a)
    r = run_bass_kernel_spmd(nc, [arrays], core_ids=[0])
    return r.results[0]["out_dram"].reshape(1, T, D)
```

```python
import math
from contextlib import ExitStack, contextmanager

import numpy as np

import concourse.bass as bass
from concourse import mybir

F32 = mybir.dt.float32
F32R = mybir.dt.float32r
I32 = mybir.dt.int32
ALU = mybir.AluOpType
ACT = mybir.ActivationFunctionType
AX = mybir.AxisListType

P = 128
D = 1024
T = 1024
KT = D // P
TT = T // P
CTX = 256
GRID_W = 64
CONF_D = 512
CONF_K = 31
SSD_D = 768
HEADS = 12
GROUPS = 4
HPG = HEADS // GROUPS
HD = SSD_D // HEADS
CHUNKS = T // P
CTX_CHUNKS = CTX // P
HY_D = 512
HY_EMB = 33
HY_HID = 64
SC_D = 512
MOE_GROUPS = 4
MOE_EPG = 8
EXPERTS = MOE_GROUPS * MOE_EPG
FF = 512
ALPHA = 2.0 ** 0.25
EPS = 1e-5
BLOCKS = (2 * T + EXPERTS * (P - 1)) // P
SLOTS = BLOCKS + 1
RING = 4
HALVES = ((0, 512), (512, 1024))
ORDER = np.concatenate([np.arange(0, T, 2), np.arange(1, T, 2)])
KTILES = TT // 2
BIG = 1e30

OFF_B = 2 * CONF_D
OFF_XBC = OFF_B + SSD_D
OFF_DT = OFF_XBC + SSD_D + 2 * GROUPS * P
OFF_C = OFF_DT + 2 * HEADS
OFF_D = OFF_C + 3 * HY_D
OFF_G = OFF_D + 3 * SC_D

TWO_PI_1 = 6.28125
TWO_PI_2 = float((np.float32(2 * math.pi - TWO_PI_1).view(np.uint32) & np.uint32(0xFFFFF000)).view(np.float32))
TWO_PI_3 = 2 * math.pi - TWO_PI_1 - TWO_PI_2
ROUND = 1.5 * 2.0 ** 23

COLS = {
    "b_mod": 48, "hy_b1": 1, "hy_b2": 1, "hy_f1": 1, "hy_f2": 1,
    "ssd_conv_w": 42, "ssd_conv_b": 14, "ssd_norm_g": 6,
    "hy_short_w": 36, "hy_short_b": 12,
    "conf_dw_w": 124, "conf_dw_b": 4, "conf_ln_g": 4, "conf_ln_b": 4, "sc_conv_w": 12,
}
ROWS = {
    "dt_bias": 24, "a_log": 24, "ssd_d": 12, "hy_bias": 1024, "rt_b": 36,
    "ln_g1": D, "ln_b1": D, "ln_g2": D, "ln_b2": D,
}
CONSTS = {
    "ident": P, "upto": P, "from": P, "before": P, "iota": 64, "sign": 1, "weight": TT,
    "t01": TT, "not_first": TT,
}


def places(sizes):
    at, out = 0, {}
    for name, n in sizes.items():
        out[name] = (at, at + n)
        at += n
    return out, at


COL_AT, N_COLS = places(COLS)
ROW_AT, N_ROWS = places(ROWS)
CONST_AT, N_CONSTS = places(CONSTS)


def shape_constants():
    q = np.arange(P)
    c = np.zeros((P, N_CONSTS), np.float32)

    def put(name, v):
        c[:, CONST_AT[name][0]:CONST_AT[name][1]] = v

    put("ident", np.eye(P))
    put("upto", q[:, None] <= q[None, :])
    put("from", q[:, None] >= q[None, :])
    put("before", q[:, None] < q[None, :])
    put("iota", np.arange(64)[None, :])
    put("sign", ((-1.0) ** q)[:, None])
    weight = np.full((P, TT), 1.0 / T)
    weight[0, 0] = 1.0 / (2 * T)
    put("weight", weight)
    not_first = np.ones((P, TT))
    not_first[0, 0] = 0.0
    put("not_first", not_first)
    t01 = np.linspace(0.0, 1.0, T, dtype=np.float32)
    put("t01", t01[ORDER].reshape(TT, P).T)

    bands_n = (HY_EMB - 1) // 2
    omega = np.float32(2.0 * math.pi / T) * np.arange(T, dtype=np.float32)[:, None]
    bands = np.linspace(1e-4, bands_n - 1, bands_n, dtype=np.float32)
    phase = (bands * omega).astype(np.float32)
    feat = np.concatenate([t01[:, None], np.cos(phase), -np.sin(phase)], axis=-1).astype(np.float32)
    deltas = np.abs(np.linspace(math.log(1e-2) / 1.5, math.log(1e-2) / 0.3, 4 * HY_D, dtype=np.float32))

    angle = (np.outer(ORDER, np.arange(T // 2)) % (2 * T)) * (2.0 * math.pi / (2 * T))
    cos, sin = np.cos(angle).astype(np.float32), np.sin(angle).astype(np.float32)
    forward = np.stack([as_items(cos), as_items(sin)], axis=1)
    back = sin.copy()
    back[:, 0] = (-1.0) ** (ORDER // 2)

    return {
        "consts": c, "featT": np.ascontiguousarray(feat[ORDER].T), "neg_deltas": -deltas[None, :],
        "zeros": np.zeros((P, 4 * D), np.float32),
        "dft": forward.reshape(TT, P, KT * P), "idft": as_items(np.concatenate([cos.T, back.T])),
    }


def as_items(w):
    kt, n = w.shape[0] // P, w.shape[1] // P
    return np.ascontiguousarray(w.reshape(kt, P, n, P).transpose(2, 1, 0, 3)).reshape(n, P, kt * P)


def as_cols(v):
    v = np.asarray(v)
    v = v.reshape(-1, v.shape[-1] // P, P)
    return v.transpose(2, 1, 0).reshape(P, -1)


class Chain:

    def __init__(self, eng, sem):
        self.eng, self.sem, self.start, self.steps = eng, sem, 0, 0

    def step(self, ins):
        ins.then_inc(self.sem, 1)
        self.steps += 1
        return ins

    def wait(self):
        self.eng.wait_ge(self.sem, self.start + self.steps)

    @contextmanager
    def turns(self, i, turns, per):
        before, steps = self.start, self.steps
        self.start, self.steps = before + steps + i * per, 0
        yield
        assert self.steps == per, (self.steps, per)
        self.start, self.steps = before + steps + turns * per, 0


def item(array, n):
    return array[bass.ds(n, 1)].rearrange("o p n -> p (o n)")


def twin(nc, name, shape):
    offset = nc.sbuf_base - 4 * math.prod(shape[1:])
    return nc.alloc_sbuf_tensor_at(f"{name}_rest", shape, F32R, offset=offset)


class Ring:

    def __init__(self, nc, ctx):
        self.nc = nc
        self.buf = ctx.enter_context(nc.sbuf_tensor("ring", [P, RING, KT * P], F32))
        self.rest = twin(nc, "ring", [P, RING, KT * P])
        self.landed = [ctx.enter_context(nc.semaphore(f"ring_landed{s}")) for s in range(RING)]
        self.freed = ctx.enter_context(nc.semaphore("ring_freed"))
        self.items = 0
        self.segments = []
        self.streamed = 0

    def plan(self, segments):
        at = 0
        for n, source in segments:
            self.segments.append((at, n, source))
            at += n + -n % RING

    def claim(self, n):
        base, self.items = self.items, self.items + n
        assert base % RING == 0 and n % RING == 0
        return base

    def load(self, sp, item, slot, src):
        sp.wait_ge(self.freed, item + 1)
        sp.dma_start(self.buf[:, slot, 0:src.shape[-1]], src).then_inc(self.landed[slot], 16)

    def stream(self, sp):
        n = self.streamed
        self.streamed += 1
        base, count, source = self.segments[n]
        if n == 0:
            sp.sem_inc(self.freed, RING)
            for slot in range(RING):
                self.load(sp, slot, slot, source(0, slot))
        if count // RING > 1:
            with sp.Fori(0, count // RING - 1) as j:
                for slot in range(RING):
                    self.load(sp, j * RING + (base + RING + slot), slot, source(j + 1, slot))
        turn = count // RING
        if count % RING:
            for slot in range(RING):
                if slot < count % RING:
                    self.load(sp, base + turn * RING + slot, slot, source(turn, slot))
                else:
                    sp.wait_ge(self.freed, base + turn * RING + slot + 1)
                    sp.sem_inc(self.landed[slot], 16)
        if n + 1 < len(self.segments):
            base, count, source = self.segments[n + 1]
            for slot in range(RING):
                self.load(sp, base + slot, slot, source(0, slot))

    def arrived(self, pe, base, turn, slot):
        pe.wait_ge(self.landed[slot], turn * 16 + (base // RING + 1) * 16)

    def done(self, item):
        return item + RING + 1


class Kernel:
    def __init__(self, nc, a, ctx):
        self.nc, self.a = nc, a
        self.ring = Ring(nc, ctx)
        sb = self.resident(ctx)
        self.uT = sb("uT", [P, KT, T])
        self.uT_rest = twin(nc, "uT", [P, KT, T])
        self.spare = sb("spare", [P, KT, T])
        self.uT_upper = twin(nc, "uT_upper", [P, KT, T])
        self.cols = sb("cols", [P, N_COLS])
        self.consts = sb("consts", [P, N_CONSTS])
        self.ones = sb("ones", [P, P])
        self.mod = sb("mod", [P, 48, 2])
        self.blank = ctx.enter_context(nc.semaphore("blank"))
        self.blank_parts = SLOTS // 4
        self.ps = ctx.enter_context(nc.psum_tensor("ps", [P, 8, 512], F32))

    def resident(self, ctx):
        return lambda name, shape, dt=F32: ctx.enter_context(self.nc.sbuf_tensor(f"sb_{name}", shape, dt))

    def col(self, name, i=0, n=1):
        at = COL_AT[name][0] + i
        return self.cols[:, at:at + n]

    def const(self, name, i=0, n=None):
        at, end = CONST_AT[name]
        return self.consts[:, at + i:end if n is None else at + i + n]

    def row(self, name):
        at, end = ROW_AT[name]
        return self.a["rows"][0, at:end].partition_broadcast(P)

    @contextmanager
    def stage(self, name):
        nc, sems = self.nc, []
        with ExitStack() as ctx:
            def sb(n, shape, dt=F32):
                return ctx.enter_context(nc.sbuf_tensor(f"{name}_{n}", shape, dt))

            def sem(n):
                s = nc.alloc_semaphore(f"{name}_{n}")
                sems.append(s)
                return s

            yield sb, sem
            nc.clear_and_free_semaphores(sems)
            nc.all_engine_barrier()

    def split_product(self, slot, upper, x_rest, x_upper, out, cols, kt=KT):
        lo, hi = cols
        for k in range(kt):
            weights = slice(k * P, (k + 1) * P)
            w = upper[:, slot % upper.shape[1], weights]
            parts = ((w, x_upper), (w, x_rest), (self.ring.rest[:, slot, weights], x_upper))
            for n, (weight, x) in enumerate(parts):
                last = self.nc.tensor.matmul(out, weight, x[:, k, lo:hi], start=(k == 0 and n == 0),
                                             stop=(k == kt - 1 and n == 2))
        return last

    def split(self, v, ch, x, upper, rest, ready):
        ch.step(self.nc.vector.tensor_copy(upper, x))
        ch.wait()
        self.nc.vector.tensor_tensor(rest, x, upper.bitcast(F32), ALU.subtract).then_inc(ready, 1)

    def product(self, slot, rhs, out, cols, kt=KT):
        for k in range(kt):
            last = self.nc.tensor.matmul(out, self.ring.buf[:, slot, k * P:(k + 1) * P],
                                         rhs[:, k, cols[0]:cols[1]], start=(k == 0), stop=(k == kt - 1))
        return last


def filter_stages(k):
    with ExitStack() as ctx:
        sb = k.resident(ctx)
        even = k.spare[:, :, :].rearrange("p t (o c) -> p t o c", o=2)
        odd = sb("odd", [P, TT, 2, HY_D])
        norms = sb("norms", [P, 2, HY_D])
        stage_filter_time(k, even, odd, norms)
        stage_filter_spectrum(k, even, odd, norms)


def stage_filter_time(k, even, odd, norms):
    nc, a, ring, ps = k.nc, k.a, k.ring, k.ps
    with k.stage("ft") as (sb, sem):
        featT = sb("featT", [HY_EMB, T])
        w1, w2 = sb("w1", [HY_EMB, HY_HID]), sb("w2", [HY_HID, HY_HID])
        w3 = sb("w3", [HY_HID, 4 * HY_D])
        deltas = sb("deltas", [P, 4 * HY_D])
        cc, ccs = sb("cc", [P, KT, 2]), sb("ccs", [P, KT, 2])
        arg, whole = sb("arg", [HY_HID, T]), sb("whole", [HY_HID, T])
        hid, hid_t = sb("hid", [HY_HID, 2, T]), sb("hid_t", [HY_HID, P])
        window = sb("window", [P, 4 * HY_D])
        filt, mags = sb("filt", [P, 2, 2, HY_D]), sb("mags", [P, 2, 2, HY_D])
        mag_sum = sb("mag_sum", [P, 2, 2, HY_D])
        loaded, cc_in, silu_c = sem("loaded"), sem("cc_in"), sem("silu_c")
        pre_ready, arg_ready, hid_ready = sem("pre_ready"), sem("arg_ready"), sem("hid_ready")
        hid_t_ready, filt_mm, window_ready = sem("hid_t_ready"), sem("filt_mm"), sem("window_ready")
        filt_ready, mags_ready, summed = sem("filt_ready"), sem("mags_ready"), sem("summed")
        dve, ones_set, norm_mm = sem("dve"), sem("ones_set"), sem("norm_mm")
        mod_items = 48
        early = mod_items // RING - TT
        mod_rows = k.uT[0:2, 0:6, :].rearrange("p k t -> p (k t)")
        mod_read, mod_turned = sem("mod_read"), sem("mod_turned")
        base = ring.claim(mod_items)
        loads = ((k.consts[:, :], a["consts"]), (k.cols[:, :], a["cols"]), (featT[:, :], a["featT"]),
                 (w1[:, :], a["hy_w1"]), (w2[:, :], a["hy_w2"]), (w3[:, :], a["hy_w3"]),
                 (deltas[:, :], a["neg_deltas"][0].partition_broadcast(P)))

        with nc.Block() as block:
            @block.sync
            def _(sp):
                sp.dma_start(cc[:, :, :], a["ccT"]).then_inc(cc_in, 16)
                for dst, src in loads:
                    sp.dma_start(dst, src).then_inc(loaded, 16)
                ring.stream(sp)

            @block.tensor
            def _(pe):
                pe.wait_ge(loaded, 16 * len(loads))
                pe.wait_ge(silu_c, 1)

                def modulation(group, j):
                    for slot in range(RING):
                        ring.arrived(pe, base + group * RING, j, slot)
                        if slot % 2 == 0:
                            pe.wait_ge(mod_read, j * 2 + (2 * group + slot // 2 + 1))
                        for kt in range(KT):
                            mm = nc.tensor.matmul(ps[0:2, 6 + slot // 2, (slot % 2) * P:(slot % 2 + 1) * P],
                                                  ccs[:, kt, :], ring.buf[:, slot, kt * P:(kt + 1) * P],
                                                  start=(kt == 0), stop=(kt == KT - 1))
                        mm.then_inc(ring.freed, 1)

                for layer, (w, src) in enumerate(((w1[:, :], featT), (w2[:, :], hid[:, 0, :]))):
                    if layer:
                        pe.wait_ge(hid_ready, 1)
                    for h, (lo, hi) in enumerate(HALVES):
                        mm = nc.tensor.matmul(ps[0:HY_HID, h, :], w, src[:, lo:hi], start=True, stop=True)
                    mm.then_inc(pre_ready, 1)
                    for group in (2 * layer, 2 * layer + 1):
                        modulation(group, 0)
                with pe.Fori(0, TT) as j:
                    pe.wait_ge(hid_t_ready, j + 1)
                    for q in range(4):
                        mm = nc.tensor.matmul(ps[:, q, :], hid_t[:, :], w3[:, q * HY_D:(q + 1) * HY_D],
                                              start=True, stop=True)
                    mm.then_inc(filt_mm, 1)
                    modulation(early, j)
                pe.wait_ge(mod_read, 2 + 2 * mod_items // RING)
                for m in range(mod_items):
                    mm = nc.tensor.transpose(ps[:, 6, 2 * m:2 * m + 2], mod_rows[:, m * P:(m + 1) * P],
                                             k.const("ident")[0:2, 0:2])
                mm.then_inc(mod_turned, 1)
                pe.wait_ge(summed, TT + 1)
                pe.wait_ge(ones_set, 1)
                for o in range(2):
                    for d in range(2):
                        mm = nc.tensor.matmul(ps[:, o, :], k.ones[:, :], mag_sum[:, o, d, :],
                                              start=(d == 0), stop=(d == 1))
                mm.then_inc(norm_mm, 1)

            @block.scalar
            def _(act):
                act.sem_inc(mags_ready, 1)
                act.wait_ge(cc_in, 16)
                nc.scalar.activation(ccs[:, :, :], cc[:, :, :], ACT.Silu).then_inc(silu_c, 1)
                act.sem_inc(mod_read, 2)

                def modulation(group, j):
                    for h in range(2):
                        act.wait_ge(ring.freed, j * RING + ring.done(base + group * RING + 2 * h + 1))
                        nc.scalar.copy(mod_rows[:, bass.ds(j * RING * P + (group * RING + 2 * h) * P, 2 * P)],
                                       ps[0:2, 6 + h, 0:2 * P]).then_inc(mod_read, 1)

                for layer in range(2):
                    modulation(2 * layer, 0)
                    act.wait_ge(arg_ready, layer + 1)
                    nc.scalar.activation(hid[:, layer, :], arg[:, :], ACT.Sin).then_inc(hid_ready, 1)
                    modulation(2 * layer + 1, 0)
                with act.Fori(0, TT) as j:
                    act.wait_ge(filt_ready, j + 1)
                    nc.scalar.activation(window[:, :], deltas[:, :], ACT.Exp,
                                         scale=k.const("t01")[:, bass.ds(j, 1)]).then_inc(window_ready, 1)
                    act.wait_ge(filt_ready, j + 2)
                    act.wait_ge(summed, j + 1)
                    nc.scalar.activation(mags[:, :, :, :], filt[:, :, :, :], ACT.Abs).then_inc(mags_ready, 1)
                    modulation(early, j)

            @block.gpsimd
            def _(pool):
                nc.gpsimd.memset(mag_sum[:, :, :, :], 0.0).then_inc(summed, 1)
                with pool.Fori(0, TT) as j:
                    pool.wait_ge(mags_ready, j + 2)
                    pool.wait_ge(summed, j + 1)
                    nc.gpsimd.tensor_tensor(mag_sum[:, :, :, :], mag_sum[:, :, :, :], mags[:, :, :, :],
                                            ALU.add).then_inc(summed, 1)

            @block.vector
            def _(v):
                v.sem_inc(filt_ready, 1)
                ch = Chain(v, dve)
                nc.vector.memset(k.ones[:, :], 1.0).then_inc(ones_set, 1)
                v.wait_ge(loaded, 16 * len(loads))
                for layer, (b, f) in enumerate((("hy_b1", "hy_f1"), ("hy_b2", "hy_f2"))):
                    v.wait_ge(pre_ready, layer + 1)
                    for h, (lo, hi) in enumerate(HALVES):
                        ch.step(nc.vector.tensor_scalar(arg[:, lo:hi], ps[0:HY_HID, h, :], k.col(b)[0:HY_HID],
                                                        k.col(f)[0:HY_HID], ALU.add, ALU.mult))
                    ch.wait()
                    ch.step(nc.vector.tensor_scalar(whole[:, :], arg[:, :], 1 / (2 * math.pi), ROUND,
                                                    ALU.mult, ALU.add))
                    ch.wait()
                    ch.step(nc.vector.tensor_scalar(whole[:, :], whole[:, :], ROUND, None, ALU.subtract))
                    for part in (TWO_PI_1, TWO_PI_2, TWO_PI_3):
                        ch.wait()
                        ch.step(nc.vector.scalar_tensor_tensor(out=arg[:, :], in0=whole[:, :], scalar=-part,
                                                               in1=arg[:, :], op0=ALU.mult, op1=ALU.add))
                    ch.wait()
                    nc.vector.tensor_scalar(arg[:, :], arg[:, :], 3.1415925, -3.1415925, ALU.min,
                                            ALU.max).then_inc(arg_ready, 1)
                v.wait_ge(hid_ready, 2)
                with v.Fori(0, TT) as j, ch.turns(j, TT, 3):
                    nc.vector.tensor_copy(hid_t[:, :], hid[:, 1, bass.ds(j * P, P)]).then_inc(hid_t_ready, 1)
                    v.wait_ge(filt_mm, j + 1)
                    v.wait_ge(window_ready, j + 1)
                    v.wait_ge(mags_ready, j + 1)
                    ch.step(nc.vector.tensor_tensor(filt[:, :, :, :].rearrange("p o d c -> p (o d) c"),
                                                    ps[:, 0:4, :],
                                                    window[:, :].rearrange("p (q c) -> p q c", q=4), ALU.mult))
                    ch.wait()
                    nc.vector.tensor_scalar(filt[:, :, 1, :], filt[:, :, 1, :],
                                            k.const("not_first")[:, bass.ds(j, 1)], None,
                                            ALU.mult).then_inc(filt_ready, 1)
                    v.wait_ge(filt_ready, j + 2)
                    for dst, op in ((even, ALU.add), (odd, ALU.subtract)):
                        ch.step(nc.vector.tensor_tensor(
                            dst[:, bass.ds(j, 1), :, :].rearrange("p t o c -> p (t o) c"),
                            filt[:, :, 0, :], filt[:, :, 1, :], op))
                v.wait_ge(norm_mm, 1)
                ch.step(nc.vector.reciprocal(norms[:, :, :], ps[:, 0:2, :]))
                v.wait_ge(mod_turned, 1)
                ch.step(nc.vector.tensor_tensor(k.mod[:, :, :], ps[:, 6, 0:96].rearrange("p (m r) -> p m r", r=2),
                                                k.col("b_mod", 0, 48).unsqueeze(2).broadcast_to([P, 48, 2]),
                                                ALU.add))
                ch.wait()
                for m in (8, 32):
                    ch.step(nc.vector.tensor_scalar(k.mod[:, m:m + 8, :], k.mod[:, m:m + 8, :], 1.0, None, ALU.add))


def stage_filter_spectrum(k, even, odd, norms):
    nc, a, ring, ps = k.nc, k.a, k.ring, k.ps
    with k.stage("fs") as (sb, sem):
        spec = sb("spec", [P, 2, 2, 2, HY_D])
        middle = sb("middle", [1, 4, HY_D])
        odds = sb("odds", [P, 2, 2, HY_D])
        odds_ready, x_in, modulated = sem("odds_ready"), sem("x_in"), sem("modulated")
        read, evac, free, spec_free = sem("read"), sem("evac"), sem("free"), sem("spec_free")
        stored = [sem("stored0"), sem("stored1")]
        middle_mm, middle_ready, middle_out = sem("middle_mm"), sem("middle_ready"), sem("middle_out")
        items = 2 * KTILES
        base = ring.claim(items)

        with nc.Block() as block:
            @block.sync
            def _(sp):
                sp.dma_start(k.uT[:, :, :], a["xT"].rearrange("(k p) t -> p k t", p=P)).then_inc(x_in, 16)
                ring.stream(sp)

            @block.tensor
            def _(pe):
                with pe.Fori(0, items // RING) as j:
                    for slot in range(RING):
                        part = slot % 2
                        src = (even, odd)[part]
                        pe.wait_ge(free, j * RING + slot + 1)
                        ring.arrived(pe, base, j, slot)
                        for o in range(2):
                            for parity in range(2):
                                for i in range(KTILES):
                                    t = KTILES * parity + i
                                    mm = nc.tensor.matmul(ps[:, 4 * part + 2 * o + parity, :],
                                                          ring.buf[:, slot, t * P:(t + 1) * P], src[:, t, o, :],
                                                          start=(i == 0), stop=(i == KTILES - 1))
                        mm.then_inc(ring.freed, 1)
                pe.wait_ge(free, items + 2)
                for n, (src, t0) in enumerate(((even, 0), (odd, KTILES))):
                    for o in range(2):
                        for i in range(KTILES):
                            mm = nc.tensor.matmul(ps[0:1, 2 * n + o, :], k.const("sign"), src[:, t0 + i, o, :],
                                                  start=(i == 0), stop=(i == KTILES - 1))
                mm.then_inc(middle_mm, 1)

            @block.vector
            def _(v):
                v.sem_inc(free, 2)
                with v.Fori(0, items // RING) as j:
                    for slot in range(RING):
                        part = slot % 2
                        sums = ps[:, 4 * part:4 * part + 4, :].rearrange("p (o e) n -> p o e n", e=2)
                        v.wait_ge(odds_ready, j * RING + slot + 1)
                        v.wait_ge(spec_free, j * RING + slot + 1)
                        for q, op in enumerate((ALU.add, ALU.subtract)):
                            nc.vector.tensor_tensor(spec[:, part, q, :, :], sums[:, :, 0, :], odds[:, part, :, :],
                                                    op).then_inc(read, 1)
                        v.wait_ge(read, j * 2 * RING + 2 * slot + 2)
                        v.sem_inc(free, 1)
                        both = spec[:, part, :, :, :]
                        nc.vector.scalar_tensor_tensor(
                            out=both, in0=both, scalar=k.const("weight")[:, bass.ds(j * 2 + slot // 2, 1)],
                            in1=norms[:, :, :].unsqueeze(1).broadcast_to([P, 2, 2, HY_D]),
                            op0=ALU.mult, op1=ALU.mult).then_inc(evac, 1)
                v.wait_ge(middle_mm, 1)
                nc.vector.scalar_tensor_tensor(
                    out=middle[:, :, :].rearrange("p (n o) c -> p n o c", o=2),
                    in0=ps[0:1, 0:4, :].rearrange("p (n o) c -> p n o c", o=2), scalar=1.0 / T,
                    in1=norms[0:1, :, :].unsqueeze(1).broadcast_to([1, 2, 2, HY_D]),
                    op0=ALU.mult, op1=ALU.mult).then_inc(middle_ready, 1)

            @block.scalar
            def _(act):
                with act.Fori(0, items // RING) as j:
                    for slot in range(RING):
                        part = slot % 2
                        act.wait_ge(ring.freed, j * RING + ring.done(base + slot))
                        act.wait_ge(free, j * RING + slot + 1)
                        sums = ps[:, 4 * part:4 * part + 4, :].rearrange("p (o e) n -> p o e n", e=2)
                        nc.scalar.copy(odds[:, part, :, :], sums[:, :, 1, :]).then_inc(odds_ready, 1)
                act.wait_ge(x_in, 16)
                for kt in range(KT):
                    nc.scalar.activation(k.uT[:, kt, :], k.uT[:, kt, :], ACT.Identity, bias=k.mod[:, kt, 0:1],
                                         scale=k.mod[:, 8 + kt, 0:1]).then_inc(modulated, 1)
                act.wait_ge(modulated, KT)

            @block.gpsimd
            def _(pool):
                pool.sem_inc(spec_free, 2)
                with pool.Fori(0, items // RING) as j:
                    for slot in range(RING):
                        part = slot % 2
                        pool.wait_ge(evac, j * RING + slot + 1)
                        dst = a["spectra"][bass.ds(j * 2 + slot // 2, 1), :, 4 * part:4 * part + 4, :]
                        pool.dma_start(dst.rearrange("t p q n -> p (t q) n"),
                                      spec[:, part, :, :, :].rearrange("p q o n -> p (q o) n")).then_inc(stored[part], 16)
                        pool.wait_ge(stored[part], j * 32 + (slot // 2) * 16 + 16)
                        pool.sem_inc(spec_free, 1)
                pool.wait_ge(middle_ready, 1)
                pool.dma_start(a["middle"], middle[:, :, :]).then_inc(middle_out, 16)
                pool.wait_ge(middle_out, 16)


def host_arrays(x, c, ctx, c_ctx, w_mod, b_mod, ln_g, ln_b, w_in, conf_dw_w, conf_dw_b, conf_ln_g, conf_ln_b,
                ssd_conv_w, ssd_conv_b, ssd_a_log, ssd_dt_bias, ssd_d, ssd_norm_g, hy_short_w, hy_short_b,
                hy_w1, hy_b1, hy_w2, hy_b2, hy_freq, hy_w3, hy_bias, sc_conv_w, w_branch_a, w_branch_b,
                w_branch_c, w_branch_d, w_out, rt_group_w, rt_group_b, rt_expert_w, rt_expert_b,
                ex_w_gate, ex_w_up, ex_w_down):
    w = w_in[0]
    tall = {
        "b_mod": as_cols(b_mod[0]),
        "ssd_conv_w": as_cols(ssd_conv_w[0]), "ssd_conv_b": as_cols(ssd_conv_b[0]),
        "ssd_norm_g": as_cols(ssd_norm_g[0]),
        "hy_short_w": as_cols(hy_short_w[0]), "hy_short_b": as_cols(hy_short_b[0]),
        "conf_dw_w": as_cols(conf_dw_w[0]), "conf_dw_b": as_cols(conf_dw_b[0]),
        "conf_ln_g": as_cols(conf_ln_g[0]), "conf_ln_b": as_cols(conf_ln_b[0]),
        "sc_conv_w": as_cols(sc_conv_w[0]),
    }
    cols = np.zeros((P, N_COLS), np.float32)
    for name, (lo, hi) in COL_AT.items():
        if name in tall:
            cols[:, lo:hi] = tall[name]
    for name, vec in (("hy_b1", hy_b1[0]), ("hy_b2", hy_b2[0]), ("hy_f1", hy_freq[0, 0]), ("hy_f2", hy_freq[0, 1])):
        cols[0:HY_HID, COL_AT[name][0]] = vec
    rows = np.concatenate([ssd_dt_bias[0].ravel(), ssd_a_log[0].ravel(), ssd_d[0], hy_bias[0].ravel(),
                           rt_group_b[0], rt_expert_b[0], ln_g[0, 0], ln_b[0, 0], ln_g[0, 1], ln_b[0, 1]])[None, :]
    val_gate = [w[:, o + i * P:o + (i + 1) * P] for i in range(4) for o in (0, CONF_D)]
    bg_cg_xv = [w[:, OFF_D + o + i * P:OFF_D + o + (i + 1) * P] for i in range(4) for o in (SC_D, 2 * SC_D, 0)]
    out = {
        "x": x[0], "xT": x[0].T, "ctxT": ctx[0].T,
        "ccT": np.stack([c[0], c_ctx], 1).reshape(KT, P, 2).transpose(1, 0, 2),
        "cols": cols, "rows": rows,
        "w_mod": as_items(w_mod[0]),
        "w_xbc": as_items(w[:, OFF_XBC:OFF_DT]), "w_z": as_items(w[:, OFF_B:OFF_XBC]),
        "w_dt": w[:, OFF_DT:OFF_C].reshape(KT, P, 2 * HEADS).transpose(1, 0, 2),
        "w_hy": as_items(w[:, OFF_C:OFF_D]), "w_conf": as_items(np.concatenate(val_gate, 1)),
        "w_sc": as_items(np.concatenate(bg_cg_xv, 1)), "w_gate": as_items(w[:, OFF_G:]),
        "w_br_a": as_items(w_branch_a[0]), "w_br_b": as_items(w_branch_b[0]),
        "w_br_c": as_items(w_branch_c[0]), "w_br_d": as_items(w_branch_d[0]),
        "w_out": w_out[0].reshape(KT, P, D).transpose(1, 0, 2),
        "w_rt": np.concatenate([rt_group_w[0], rt_expert_w[0]], 1).reshape(KT, P, 36).transpose(1, 0, 2),
        "hy_w1": hy_w1[0], "hy_w2": hy_w2[0], "hy_w3": hy_w3[0],
        "ex_g": ex_w_gate[0], "ex_u": ex_w_up[0], "ex_d": ex_w_down[0],
    }
    out.update(shape_constants())
    return {name: np.ascontiguousarray(v) for name, v in out.items()}


SCRATCH = {
    "spectra": [KTILES, P, 8, HY_D],
    "middle": [1, 4, HY_D],
    "xbc_chan": [14, P, T + CTX + 2],
    "xbc_tok": [CHUNKS + CTX_CHUNKS, P, 14 * P],
    "h1": [TT, P, D],
    "moe": [SLOTS * P, D],
}


def loop_items(eng, n, body):
    with eng.Fori(0, n // RING) as j:
        for q in range(RING):
            body(j, q)
    for q in range(n % RING):
        body(n // RING, q)


def stage_project_conv(k, name, n, taps, bias, func, ctx=None, chan_out=None, tok_out=None, tok_sbuf=None):
    nc, a, ring, ps = k.nc, k.a, k.ring, k.ps
    width = T + (CTX + 2 if ctx is not None else 0)
    chunks = CHUNKS + (CTX_CHUNKS if ctx is not None else 0)
    full = n + -n % RING
    base = ring.claim(full)
    ctx_at = T + 2
    reads = 2 if ctx is None else 3
    with k.stage(name) as (sb, sem):
        line = sb("line", [P, 2, width + 2])
        conv = sb("conv", [P, 2, width])
        shaped = sb("shaped", [P, 2, width])
        turned = sb("turned", [P, 2, chunks, P]) if tok_sbuf is None else None
        psum_free, line_free, shaped_free, turned_free = (sem(x) for x in
                                                          ("psum_free", "line_free", "shaped_free", "turned_free"))
        lined, dve, convolved, shaped_ready = sem("lined"), sem("dve"), sem("convolved"), sem("shaped_ready")
        turned_mm, turned_ready = sem("turned_mm"), sem("turned_ready")
        stored = [[sem(f"stored{q}{b}") for b in range(2)] for q in range(2)]

        def banks(q):
            return (3 * (q % 2), 3 * (q % 2) + 1, 3 * (q % 2) + 2)

        with nc.Block() as block:
            @block.sync
            def _(sp):
                ring.stream(sp)

            @block.tensor
            def _(pe):
                def project(j, q):
                    pe.wait_ge(psum_free, j * RING + q + 1)
                    ring.arrived(pe, base, j, q)
                    b0, b1, b2 = banks(q)
                    for bank, cols in zip((b0, b1), HALVES):
                        mm = k.product(q, k.uT, ps[:, bank, :], cols)
                    if ctx is not None:
                        pe.wait_ge(turned_ready, (j * RING + q) * reads + reads)
                        mm = k.product(q, ctx, ps[:, b2, 0:CTX], (0, CTX))
                    mm.then_inc(ring.freed, 1)

                def turn(j, q):
                    pe.wait_ge(shaped_ready, j * RING + q + 1)
                    pe.wait_ge(turned_ready, (j * RING + q) * reads + 2 * reads)
                    for c in range(CHUNKS):
                        if ctx is not None:
                            tokens = slice(c * P, (c + 1) * P)
                        else:
                            tokens = slice(2 * P * (c % 4) + c // 4, 2 * P * (c % 4 + 1), 2)
                        mm = nc.tensor.transpose(ps[:, 6 + c // 4, (c % 4) * P:(c % 4 + 1) * P],
                                                 shaped[:, q % 2, tokens], k.const("ident"))
                    if ctx is not None:
                        for c in range(CTX_CHUNKS):
                            mm = nc.tensor.transpose(ps[:, banks(q)[2], CTX + c * P:CTX + (c + 1) * P],
                                                     shaped[:, q % 2, ctx_at + c * P:ctx_at + (c + 1) * P],
                                                     k.const("ident"))
                    mm.then_inc(turned_mm, 1)

                def group(j, count):
                    for q in range(count):
                        project(j, q)
                        if q:
                            turn(j, q - 1)
                    turn(j, count - 1)

                with pe.Fori(0, n // RING) as j:
                    group(j, RING)
                if n % RING:
                    group(n // RING, n % RING)
                    pe.wait_ge(ring.freed, ring.done(base + n - 1))
                    pe.sem_inc(ring.freed, full - n)

            @block.scalar
            def _(act):
                act.sem_inc(turned_ready, 2 * reads)

                def evacuate(j, q):
                    act.wait_ge(ring.freed, j * RING + ring.done(base + q))
                    act.wait_ge(line_free, j * RING + q + 1)
                    b0, b1, b2 = banks(q)
                    ins = nc.scalar.copy(line[:, q % 2, 1:T + 1],
                                         ps[:, b0:b1 + 1, :].rearrange("p b n -> p (b n)"))
                    if ctx is not None:
                        ins.then_inc(lined, 1)
                        ins = nc.scalar.copy(line[:, q % 2, ctx_at + 1:ctx_at + 1 + CTX], ps[:, b2, 0:CTX])
                    ins.then_inc(lined, 1)

                def shape(j, q):
                    act.wait_ge(convolved, j * RING + q + 1)
                    act.wait_ge(shaped_free, j * RING + q + 1)
                    nc.scalar.activation(shaped[:, q % 2, :], conv[:, q % 2, :], func,
                                         bias=k.col(bias, 0, n)[:, bass.ds(j * RING + q, 1)]).then_inc(shaped_ready, 1)

                def evacuate_turned(j, q):
                    act.wait_ge(turned_mm, j * RING + q + 1)
                    act.wait_ge(turned_free, j * RING + q + 1)
                    for h in range(2):
                        part = slice(4 * h, 4 * h + 4)
                        if tok_sbuf is None:
                            out = turned[:, q % 2, part, :]
                        else:
                            out = tok_sbuf[:, part, bass.ds((j * RING + q) * P, P)]
                        nc.scalar.copy(out, ps[:, 6 + h, :].rearrange("p (c m) -> p c m", c=4)).then_inc(turned_ready, 1)
                    if ctx is not None:
                        nc.scalar.copy(turned[:, q % 2, CHUNKS:, :],
                                       ps[:, banks(q)[2], CTX:2 * CTX].rearrange("p (c m) -> p c m", c=CTX_CHUNKS)
                                       ).then_inc(turned_ready, 1)

                def group(j, count):
                    for q in range(count):
                        evacuate(j, q)
                        shape(j, q)
                        if q:
                            evacuate_turned(j, q - 1)
                    evacuate_turned(j, count - 1)

                with act.Fori(0, n // RING) as j:
                    group(j, RING)
                if n % RING:
                    group(n // RING, n % RING)

            @block.vector
            def _(v):
                ch = Chain(v, dve)
                ch.step(nc.vector.memset(line[:, :, :], 0.0))
                ch.wait()
                v.sem_inc(line_free, 2)
                v.sem_inc(psum_free, 2)
                copies = 1 if ctx is None else 2

                def convolve(j, q):
                    m, src, dst = j * RING + q, line[:, q % 2, :], conv[:, q % 2, :]
                    tap = [k.col(taps, 0, 3 * n)[:, bass.ds(m * 3 + i, 1)] for i in range(3)]
                    v.wait_ge(lined, m * copies + copies)
                    v.sem_inc(psum_free, 1)
                    ch.step(nc.vector.tensor_scalar(dst, src[:, 0:width], tap[0], None, ALU.mult))
                    ch.wait()
                    ch.step(nc.vector.scalar_tensor_tensor(out=dst, in0=src[:, 1:width + 1], scalar=tap[1], in1=dst,
                                                           op0=ALU.mult, op1=ALU.add))
                    ch.wait()
                    nc.vector.scalar_tensor_tensor(out=dst, in0=src[:, 2:width + 2], scalar=tap[2], in1=dst,
                                                   op0=ALU.mult, op1=ALU.add).then_inc(convolved, 1)
                    v.wait_ge(convolved, m + 1)
                    v.sem_inc(line_free, 1)

                with v.Fori(0, n // RING) as j, ch.turns(j, n // RING, 2 * RING):
                    for q in range(RING):
                        convolve(j, q)
                for q in range(n % RING):
                    convolve(n // RING, q)

            @block.gpsimd
            def _(pool):
                blank = a["moe"].rearrange("(n p r) d -> n p (r d)", p=P, r=4)
                assert ctx is not None or n == k.blank_parts
                pool.sem_inc(shaped_free, 2)
                pool.sem_inc(turned_free, 2)

                def store(j, q):
                    b = q % 2
                    m = j * RING + q
                    pool.wait_ge(shaped_ready, m + 1)
                    if chan_out is not None:
                        pool.dma_start(item(chan_out, m), shaped[:, b, :]).then_inc(stored[0][b], 16)
                        pool.wait_ge(turned_ready, m * reads + 3 * reads)
                        pool.dma_start(tok_out[:, :, bass.ds(m * P, P)].rearrange("c p m -> p c m"),
                                       turned[:, b, :, :]).then_inc(stored[1][b], 16)
                        for which in range(2):
                            pool.wait_ge(stored[which][b], j * 32 + (q // 2) * 16 + 16)
                        pool.sem_inc(turned_free, 1)
                    else:
                        pool.dma_start(item(blank, m), a["zeros"]).then_inc(k.blank, 16)
                        pool.wait_ge(turned_ready, m * reads + 3 * reads)
                        pool.sem_inc(turned_free, 1)
                        pool.wait_ge(k.blank, m * 16 + 16)
                    pool.sem_inc(shaped_free, 1)

                loop_items(pool, n, store)



def ssd_scan_stages(k, y):
    with ExitStack() as ctx:
        sb = k.resident(ctx)
        n = CHUNKS + CTX_CHUNKS
        dt = {name: sb("dt_" + name, [P, n, 2, HEADS]) for name in
              ("dt", "log_decay", "cum", "exp_cum", "to_end", "total")}
        with ExitStack() as inner:
            uc = inner.enter_context(k.nc.sbuf_tensor("sb_uc", [P, KT, CTX], F32))
            stage_dt(k, uc, dt)
            stage_project_conv(k, "xbc", 14, "ssd_conv_w", "ssd_conv_b", ACT.Silu, ctx=uc,
                               chan_out=k.a["xbc_chan"], tok_out=k.a["xbc_tok"])
        stage_scan(k, dt, y)


def stage_dt(k, uc, dt):
    nc, a, ps = k.nc, k.a, k.ps
    n = CHUNKS + CTX_CHUNKS
    H2 = 2 * HEADS
    with k.stage("dt") as (sb, sem):
        w_dt = sb("w_dt", [P, KT, H2])
        raw = sb("raw", [H2, n * P])
        bias, a_log = sb("bias", [P, H2]), sb("a_log", [P, H2])
        tmp, neg = sb("tmp", [P, n, H2]), sb("neg", [P, n, H2])
        loaded, u_ready, raw_mm, raw_ready, turned = (sem(x) for x in
                                                      ("loaded", "u_ready", "raw_mm", "raw_ready", "turned"))
        rate_ready, abs_ready, exp_ready, ln_ready, decay_ready = (sem(x) for x in (
            "rate_ready", "abs_ready", "exp_ready", "ln_ready", "decay_ready"))
        cum_mm, diff_ready, act_done, dve = sem("cum_mm"), sem("diff_ready"), sem("act_done"), sem("dve")
        done = sem("done")

        def flat(name):
            return dt[name][:, :, :, :].rearrange("p c d h -> p c (d h)")

        def wide(row):
            return row[:, :].unsqueeze(1).broadcast_to([P, n, H2])

        with nc.Block() as block:
            @block.sync
            def _(sp):
                sp.dma_start(uc[:, :, :], a["ctxT"].rearrange("(k p) t -> p k t", p=P)).then_inc(loaded, 16)
                sp.dma_start(w_dt[:, :, :], a["w_dt"]).then_inc(loaded, 16)
                sp.dma_start(bias[:, :], k.row("dt_bias")).then_inc(loaded, 16)
                sp.dma_start(a_log[:, :], k.row("a_log")).then_inc(loaded, 16)

            @block.tensor
            def _(pe):
                pe.wait_ge(loaded, 64)
                pe.wait_ge(u_ready, KT)
                for b, (src, lo, hi) in enumerate(((k.uT, 0, 512), (k.uT, 512, 1024), (uc, 0, CTX))):
                    for kt in range(KT):
                        mm = nc.tensor.matmul(ps[0:H2, b, 0:hi - lo], w_dt[:, kt, :], src[:, kt, lo:hi],
                                              start=(kt == 0), stop=(kt == KT - 1))
                mm.then_inc(raw_mm, 1)
                pe.wait_ge(raw_ready, 2)
                for c in range(n):
                    mm = nc.tensor.transpose(ps[:, 3, c * H2:(c + 1) * H2], raw[:, c * P:(c + 1) * P],
                                             k.const("ident")[0:H2, 0:H2])
                mm.then_inc(turned, 1)
                pe.wait_ge(decay_ready, 1)
                for d, tri in enumerate(("upto", "from")):
                    nc.tensor.matmul(ps[:, 4 + d, 0:n * HEADS], k.const(tri), dt["log_decay"][:, :, d, :],
                                     start=True, stop=True)
                nc.tensor.matmul(ps[:, 6, 0:n * H2], k.ones[:, :], flat("log_decay"), start=True,
                                 stop=True).then_inc(cum_mm, 1)

            @block.vector
            def _(v):
                ch = Chain(v, dve)
                v.wait_ge(loaded, 64)
                for kt in range(KT):
                    nc.vector.tensor_scalar(uc[:, kt, :], uc[:, kt, :], k.mod[:, 8 + kt, 1:2],
                                            k.mod[:, kt, 1:2], ALU.mult, ALU.add).then_inc(u_ready, 1)
                v.wait_ge(raw_mm, 1)
                nc.vector.tensor_copy(raw[:, 0:T], ps[0:H2, 0:2, :].rearrange("p b n -> p (b n)")).then_inc(raw_ready, 1)
                nc.vector.tensor_copy(raw[:, T:T + CTX], ps[0:H2, 2, 0:CTX]).then_inc(raw_ready, 1)
                v.wait_ge(turned, 1)
                ch.step(nc.vector.tensor_tensor(tmp[:, :, :], ps[:, 3, 0:n * H2].rearrange("p (c h) -> p c h", c=n),
                                                wide(bias), ALU.add))
                ch.wait()
                nc.vector.tensor_scalar(neg[:, :, :], tmp[:, :, :], -1.0, None, ALU.mult).then_inc(abs_ready, 1)
                v.wait_ge(abs_ready, 1)
                nc.vector.tensor_tensor(neg[:, :, :], tmp[:, :, :], neg[:, :, :], ALU.min).then_inc(abs_ready, 1)
                v.wait_ge(ln_ready, 1)
                ch.step(nc.vector.scalar_tensor_tensor(out=flat("dt"), in0=tmp[:, :, :], scalar=0.0,
                                                       in1=neg[:, :, :], op0=ALU.max, op1=ALU.add))
                v.wait_ge(rate_ready, 1)
                ch.step(nc.vector.tensor_scalar(a_log[:, :], a_log[:, :], -1.0, None, ALU.mult))
                ch.wait()
                nc.vector.tensor_tensor(flat("log_decay"), flat("dt"), wide(a_log), ALU.mult).then_inc(decay_ready, 1)
                v.wait_ge(cum_mm, 1)
                for d in range(2):
                    ch.step(nc.vector.tensor_copy(dt["cum"][:, :, d, :],
                                                  ps[:, 4 + d, 0:n * HEADS].rearrange("p (c h) -> p c h", c=n)))
                ch.wait()
                nc.vector.tensor_tensor(flat("to_end"), ps[:, 6, 0:n * H2].rearrange("p (c h) -> p c h", c=n),
                                        flat("cum"), ALU.subtract).then_inc(diff_ready, 1)
                v.wait_ge(act_done, 3)
                nc.vector.tensor_copy(flat("total"), tmp[:, :, :]).then_inc(done, 1)
                v.wait_ge(done, 1)

            @block.scalar
            def _(act):
                act.wait_ge(loaded, 64)
                nc.scalar.activation(a_log[:, :], a_log[:, :], ACT.Exp).then_inc(rate_ready, 1)
                act.wait_ge(abs_ready, 2)
                nc.scalar.activation(neg[:, :, :], neg[:, :, :], ACT.Exp).then_inc(exp_ready, 1)
                act.wait_ge(exp_ready, 1)
                nc.scalar.activation(neg[:, :, :], neg[:, :, :], ACT.Ln, bias=1.0).then_inc(ln_ready, 1)
                act.wait_ge(diff_ready, 1)
                nc.scalar.activation(flat("exp_cum"), flat("cum"), ACT.Exp).then_inc(act_done, 1)
                nc.scalar.activation(flat("to_end"), flat("to_end"), ACT.Exp).then_inc(act_done, 1)
                nc.scalar.activation(tmp[:, :, :], ps[:, 6, 0:n * H2].rearrange("p (c h) -> p c h", c=n),
                                     ACT.Exp).then_inc(act_done, 1)


def stage_scan(k, dt, y):
    nc, a, ps = k.nc, k.a, k.ps
    half = SSD_D // 2
    with k.stage("scan") as (sb, sem):
        b_chan, c_chan = sb("b_chan", [P, 2, GROUPS, P]), sb("c_chan", [P, 2, GROUPS, P])
        b_tok, xs = sb("b_tok", [P, 2, GROUPS * P]), sb("xs", [P, 2, SSD_D])
        xdt, xend = sb("xdt", [P, 2, SSD_D]), sb("xend", [P, 2, SSD_D])
        decay, mix = sb("decay", [P, 2, 2, HPG, P]), sb("mix", [P, 2, 2, HPG, P])
        cb, chunk_decay = sb("cb", [P, GROUPS, P]), sb("chunk_decay", [P, HEADS])
        state, faded, out = sb("state", [P, SSD_D]), sb("faded", [P, SSD_D]), sb("out", [P, SSD_D])
        d_row = sb("d_row", [P, HEADS])
        d_in, buf_free = sem("d_in"), sem("buf_free")
        in_state, in_out = [sem("in_state0"), sem("in_state1")], [sem("in_out0"), sem("in_out1")]
        xdt_ready, xend_ready, skip_ready, faded_ready = (sem(x) for x in (
            "xdt_ready", "xend_ready", "skip_ready", "faded_ready"))
        decay_set, cb_mm, cum_mm, off_mm, diag_mm, state_mm = (sem(x) for x in (
            "decay_set", "cb_mm", "cum_mm", "off_mm", "diag_mm", "state_mm"))
        cb_ready, diff_ready, low_ready, exp_ready, mix_ready = (sem(x) for x in (
            "cb_ready", "diff_ready", "low_ready", "exp_ready", "mix_ready"))
        state_half, state_done, y_read, dve = sem("state_half"), sem("state_done"), sem("y_read"), sem("dve")
        order = (1, 0)
        steps = CTX_CHUNKS + CHUNKS

        def plan(eng, context_step, step):
            for o, d in enumerate(order):
                for i in range(CTX_CHUNKS):
                    c = CHUNKS + (i if d == 0 else CTX_CHUNKS - 1 - i)
                    context_step(o, d, c, o * steps + i, i % 2, o * (steps // 2) + i // 2)
                with eng.Fori(0, CHUNKS // 2) as j:
                    for q in range(2):
                        i = j * 2 + q
                        c = i if d == 0 else j * -2 + (CHUNKS - 1 - q)
                        step(o, d, c, j * 2 + (o * steps + CTX_CHUNKS + q), q, j + (o * steps + CTX_CHUNKS) // 2,
                             j * 2 + (o * CHUNKS + q), j + o * CHUNKS // 2, j)

        def at(name, c, d, lo=0, hi=HEADS):
            return dt[name][:, bass.ds(c, 1), d, lo:hi].rearrange("p c h -> p (c h)")

        def per_head(v, width=HD):
            return v.unsqueeze(2).broadcast_to([P, v.shape[1], width])

        def heads(v):
            return v.rearrange("p (h e) -> p h e", e=HD)

        with nc.Block() as block:
            @block.sync
            def _(sp):
                sp.dma_start(d_row[:, :], k.row("ssd_d")).then_inc(d_in, 16)

                def load_state(c, n, b):
                    sp.wait_ge(buf_free, n + 1)
                    tok = item(a["xbc_tok"], c)
                    sp.dma_start(xs[:, b, :], tok[:, 0:SSD_D]).then_inc(in_state[b], 16)
                    sp.dma_start(b_tok[:, b, :], tok[:, SSD_D:SSD_D + GROUPS * P]).then_inc(in_state[b], 16)

                def context_step(o, d, c, n, b, turn):
                    load_state(c, n, b)

                def step(o, d, c, n, b, turn, lat, lat_turn, j):
                    load_state(c, n, b)
                    for q, dst in enumerate((b_chan, c_chan)):
                        src = a["xbc_chan"][6 + GROUPS * q:6 + GROUPS * (q + 1), :, bass.ds(c * P, P)]
                        sp.dma_start(dst[:, b, :, :], src.rearrange("g p t -> p g t")).then_inc(in_out[b], 16)

                plan(sp, context_step, step)

            @block.gpsimd
            def _(pool):
                pool.wait_ge(d_in, 16)

                def inputs(o, d, c, n, b, turn):
                    pool.wait_ge(in_state[b], turn * 32 + 32)
                    nc.gpsimd.tensor_tensor(heads(xdt[:, b, :]), heads(xs[:, b, :]), per_head(at("dt", c, d)),
                                            ALU.mult).then_inc(xdt_ready, 1)
                    pool.wait_ge(xdt_ready, n + 1)
                    nc.gpsimd.tensor_tensor(heads(xend[:, b, :]), heads(xdt[:, b, :]), per_head(at("to_end", c, d)),
                                            ALU.mult).then_inc(xend_ready, 1)
                    pool.wait_ge(state_done, n + (o + 1))
                    nc.gpsimd.tensor_tensor(heads(faded[:, :]), heads(state[:, :]), per_head(at("total", c, d)),
                                            ALU.mult).then_inc(faded_ready, 1)

                def step(o, d, c, n, b, turn, lat, lat_turn, j):
                    if o == 0:
                        pool.wait_ge(in_state[b], turn * 32 + 32)
                        nc.gpsimd.tensor_tensor(
                            heads(y[:, bass.ds(c, 1), :].rearrange("p c n -> p (c n)")), heads(xs[:, b, :]),
                            per_head(d_row[:, :]), ALU.mult).then_inc(skip_ready, 1)
                    inputs(o, d, c, n, b, turn)

                plan(pool, inputs, step)

            @block.tensor
            def _(pe):
                pe.sem_inc(cum_mm, 1)
                def new_state(n, b):
                    pe.wait_ge(xend_ready, n + 1)
                    for h in range(2):
                        pe.wait_ge(state_half, n * 2 + h)
                        for g in (2 * h, 2 * h + 1):
                            mm = nc.tensor.matmul(ps[:, 7, (g % 2) * 192:(g % 2 + 1) * 192],
                                                  b_tok[:, b, g * P:(g + 1) * P],
                                                  xend[:, b, g * 192:(g + 1) * 192], start=True, stop=True)
                        mm.then_inc(state_mm, 1)

                def context_step(o, d, c, n, b, turn):
                    new_state(n, b)

                def step(o, d, c, n, b, turn, lat, lat_turn, j):
                    pe.wait_ge(in_out[b], lat_turn * 32 + 32)
                    pe.wait_ge(cb_ready, lat + 1)
                    for g in range(GROUPS):
                        mm = nc.tensor.matmul(ps[:, 2, g * P:(g + 1) * P], b_chan[:, b, g, :], c_chan[:, b, g, :],
                                              start=True, stop=True)
                    mm.then_inc(cb_mm, 1)

                    def cumulative(h):
                        pe.wait_ge(diff_ready, lat * 2 + h + 1)
                        for e in range(6):
                            col = chunk_decay[:, 6 * h + e:6 * h + e + 1].broadcast_to([P, P])
                            mm = nc.tensor.matmul(ps[:, e // 3, (e % 3) * P:(e % 3 + 1) * P], col,
                                                  k.const("from" if d else "upto"), start=True, stop=True)
                        mm.then_inc(cum_mm, 1)

                    pe.wait_ge(decay_set, lat + 1)
                    cumulative(0)
                    pe.wait_ge(state_done, n + (o + 1))
                    pe.wait_ge(y_read, lat + 1)
                    for g in range(GROUPS):
                        mm = nc.tensor.matmul(ps[:, 5 + g // 2, (g % 2) * 192:(g % 2 + 1) * 192],
                                              c_chan[:, b, g, :], state[:, g * 192:(g + 1) * 192],
                                              start=True, stop=True)
                    mm.then_inc(off_mm, 1)
                    cumulative(1)
                    new_state(n, b)
                    pe.wait_ge(xdt_ready, n + 1)
                    for h in range(2):
                        pe.wait_ge(mix_ready, lat * 2 + h + 1)
                        for e in range(6):
                            head = 6 * h + e
                            mm = nc.tensor.matmul(ps[:, 3 + h, e * HD:(e + 1) * HD], mix[:, h, e // 3, e % 3, :],
                                                  xdt[:, b, head * HD:(head + 1) * HD], start=True, stop=True)
                    mm.then_inc(diag_mm, 1)

                plan(pe, context_step, step)

            @block.scalar
            def _(act):
                def step(o, d, c, n, b, turn, lat, lat_turn, j):
                    act.wait_ge(cum_mm, lat * 2 + 1)
                    nc.scalar.copy(chunk_decay[:, :], at("log_decay", c, d)).then_inc(decay_set, 1)
                    for h in range(2):
                        act.wait_ge(low_ready, lat * 2 + h + 1)
                        nc.scalar.activation(decay[:, h, :, :, :], decay[:, h, :, :, :], ACT.Exp).then_inc(exp_ready, 1)

                plan(act, lambda *_: None, step)

            @block.vector
            def _(v):
                for first in (cb_ready, diff_ready, y_read):
                    v.sem_inc(first, 1)
                ch = Chain(v, dve)
                v.sem_inc(buf_free, 2)

                def update(o, n):
                    v.wait_ge(faded_ready, n + 1)
                    for h in range(2):
                        v.wait_ge(state_mm, n * 2 + h + 1)
                        ins = nc.vector.tensor_tensor(state[:, h * half:(h + 1) * half],
                                                      faded[:, h * half:(h + 1) * half], ps[:, 7, 0:half], ALU.add)
                        ins.then_inc(state_half, 1)
                    v.wait_ge(state_half, n * 2 + 2)
                    v.sem_inc(state_done, 1)

                def context_step(o, d, c, n, b, turn):
                    if turn == o * (steps // 2) and b == 0:
                        if o:
                            v.wait_ge(off_mm, o * CHUNKS)
                        ch.step(nc.vector.memset(state[:, :], 0.0))
                        ch.wait()
                        v.sem_inc(state_done, 1)
                    update(o, n)
                    v.sem_inc(buf_free, 1)

                def step(o, d, c, n, b, turn, lat, lat_turn, j):
                    v.wait_ge(cb_mm, lat + 1)
                    nc.vector.tensor_tensor(cb[:, :, :], ps[:, 2, :].rearrange("p (g t) -> p g t", g=GROUPS),
                                            k.const("from" if d else "upto").unsqueeze(1).broadcast_to([P, GROUPS, P]),
                                            ALU.mult).then_inc(cb_ready, 1)
                    for h in range(2):
                        v.wait_ge(cum_mm, lat * 2 + h + 2)
                        mine = at("cum", c, d, 6 * h, 6 * h + 6).rearrange("p (b e) -> p b e", b=2)
                        nc.vector.tensor_tensor(decay[:, h, :, :, :],
                                                ps[:, 0:2, 0:3 * P].rearrange("p b (e t) -> p b e t", e=3),
                                                mine.unsqueeze(3).broadcast_to([P, 2, 3, P]),
                                                ALU.subtract).then_inc(diff_ready, 1)
                        v.wait_ge(diff_ready, lat * 2 + h + 2)
                        nc.vector.tensor_scalar(decay[:, h, :, :, :], decay[:, h, :, :, :], 0.0, None,
                                                ALU.min).then_inc(low_ready, 1)
                    v.wait_ge(off_mm, lat + 1)
                    update(o, n)
                    v.wait_ge(cb_ready, lat + 2)
                    for h in range(2):
                        v.wait_ge(exp_ready, lat * 2 + h + 1)
                        nc.vector.tensor_tensor(mix[:, h, :, :, :], decay[:, h, :, :, :],
                                                cb[:, 2 * h:2 * h + 2, :].unsqueeze(2).broadcast_to([P, 2, 3, P]),
                                                ALU.mult).then_inc(mix_ready, 1)
                    both = out[:, :].rearrange("p (b h e) -> p b h e", b=2, e=HD)
                    grown = at("exp_cum", c, d).rearrange("p (b h) -> p b h", b=2).unsqueeze(3)
                    ch.step(nc.vector.tensor_tensor(both, ps[:, 5:7, 0:half].rearrange("p b (h e) -> p b h e", e=HD),
                                                    grown.broadcast_to([P, 2, 6, HD]), ALU.mult))
                    ch.wait()
                    v.wait_ge(diag_mm, lat + 1)
                    nc.vector.tensor_tensor(out[:, :].rearrange("p (b n) -> p b n", b=2), ps[:, 3:5, 0:half],
                                            out[:, :].rearrange("p (b n) -> p b n", b=2), ALU.add).then_inc(y_read, 1)
                    v.wait_ge(y_read, lat + 2)
                    if o == 0:
                        v.wait_ge(skip_ready, lat + 1)
                    yc = y[:, bass.ds(c, 1), :].rearrange("p c n -> p (c n)")
                    ch.step(nc.vector.tensor_tensor(yc, yc, out[:, :], ALU.add))
                    v.sem_inc(buf_free, 1)

                for o, d in enumerate(order):
                    for i in range(CTX_CHUNKS):
                        context_step(o, d, None, o * steps + i, i % 2, o * (steps // 2) + i // 2)
                    with v.Fori(0, CHUNKS // 2) as j, ch.turns(j, CHUNKS // 2, 4):
                        for q in range(2):
                            c = j * 2 + q if d == 0 else j * -2 + (CHUNKS - 1 - q)
                            step(o, d, c, j * 2 + (o * steps + CTX_CHUNKS + q), q, None,
                                 j * 2 + (o * CHUNKS + q), None, j)
                ch.wait()


def stage_ssd_norm(k, y, y_bT):
    nc, ring, ps = k.nc, k.ring, k.ps
    n = SSD_D // P
    full = n + -n % RING
    base = ring.claim(full)
    with k.stage("sn") as (sb, sem):
        z = sb("z", [P, 2, T])
        square, ss = sb("square", [P, SSD_D]), sb("ss", [P, CHUNKS])
        z_ready, z_turned, gated, squared = sem("z_ready"), sem("z_turned"), sem("gated"), sem("squared")
        root, normed, turned, out_ready, dve = (sem(x) for x in ("root", "normed", "turned", "out_ready", "dve"))

        with nc.Block() as block:
            @block.sync
            def _(sp):
                ring.stream(sp)

            @block.tensor
            def _(pe):
                def project(m):
                    if m >= 2:
                        pe.wait_ge(z_ready, m - 1)
                    ring.arrived(pe, base, m // RING, m % RING)
                    for h, cols in enumerate(HALVES):
                        mm = k.product(m % RING, k.uT, ps[:, 2 * (m % 2) + h, :], cols)
                    mm.then_inc(ring.freed, 1)

                def turn(m):
                    pe.wait_ge(z_ready, m + 1)
                    if m >= 2:
                        pe.wait_ge(gated, m - 1)
                    for c in range(CHUNKS):
                        mm = nc.tensor.transpose(ps[:, 4 + 2 * (m % 2) + c // 4, (c % 4) * P:(c % 4 + 1) * P],
                                                 z[:, m % 2, c * P:(c + 1) * P], k.const("ident"))
                    mm.then_inc(z_turned, 1)

                for m in range(n):
                    project(m)
                    if m:
                        turn(m - 1)
                pe.wait_ge(ring.freed, ring.done(base + n - 1))
                pe.sem_inc(ring.freed, full - n)
                turn(n - 1)
                pe.wait_ge(normed, CHUNKS)
                for m in range(n):
                    if m >= 4:
                        pe.wait_ge(out_ready, m - 3)
                    for c in range(CHUNKS):
                        mm = nc.tensor.transpose(ps[:, 2 * (m % 4) + c // 4, (c % 4) * P:(c % 4 + 1) * P],
                                                 y[:, c, m * P:(m + 1) * P], k.const("ident"))
                    mm.then_inc(turned, 1)

            @block.scalar
            def _(act):
                for m in range(n):
                    act.wait_ge(ring.freed, ring.done(base + m))
                    if m >= 2:
                        act.wait_ge(z_turned, m - 1)
                    nc.scalar.activation(z[:, m % 2, :], ps[:, 2 * (m % 2):2 * (m % 2) + 2, :].rearrange("p b n -> p (b n)"),
                                         ACT.Silu).then_inc(z_ready, 1)
                act.wait_ge(gated, n)
                for c in range(CHUNKS):
                    if c:
                        act.wait_ge(squared, c)
                    nc.scalar.activation(square[:, :], y[:, c, :], ACT.Square,
                                         accum_out=ss[:, c:c + 1]).then_inc(squared, 1)
                act.wait_ge(dve, 1)
                nc.scalar.activation(ss[:, :], ss[:, :], ACT.Sqrt).then_inc(root, 1)
                for m in range(n):
                    act.wait_ge(turned, m + 1)
                    nc.scalar.activation(y_bT[:, m, :], ps[:, 2 * (m % 4):2 * (m % 4) + 2, :].rearrange("p b n -> p (b n)"),
                                         ACT.Identity, scale=k.col("ssd_norm_g", m)).then_inc(out_ready, 1)

            @block.vector
            def _(v):
                for m in range(n):
                    v.wait_ge(z_turned, m + 1)
                    part = y[:, :, m * P:(m + 1) * P]
                    nc.vector.tensor_tensor(part, part, ps[:, 4 + 2 * (m % 2):6 + 2 * (m % 2), :].rearrange(
                        "p b (c m) -> p (b c) m", m=P), ALU.mult).then_inc(gated, 1)
                v.wait_ge(squared, CHUNKS)
                ch = Chain(v, dve)
                ch.step(nc.vector.tensor_scalar(ss[:, :], ss[:, :], 1.0 / SSD_D, EPS, ALU.mult, ALU.add))
                v.wait_ge(root, 1)
                ch.step(nc.vector.reciprocal(ss[:, :], ss[:, :]))
                ch.wait()
                for c in range(CHUNKS):
                    nc.vector.tensor_scalar(y[:, c, :], y[:, c, :], ss[:, c:c + 1], None, ALU.mult).then_inc(normed, 1)


def stage_merge(k, name, yT, yT_rest, kt, merged, first, split_u):
    nc, ring, ps = k.nc, k.ring, k.ps
    base = ring.claim(2 * KT)
    with k.stage(name) as (sb, sem):
        upper, y_upper = sb("upper", [P, RING, KT * P], F32R), sb("y_upper", [P, kt, T], F32R)
        gates, prod = sb("gates", [P, T]), sb("prod", [P, T])
        gate_ready, prod_ready, branch_free, gate_free = (sem(x) for x in (
            "gate_ready", "prod_ready", "branch_free", "gate_free"))
        u_split, y_split, w_split, dve = sem("u_split"), sem("y_split"), sem("w_split"), sem("dve")
        widths = (KT * P, kt * P)

        with nc.Block() as block:
            @block.sync
            def _(sp):
                ring.stream(sp)

            @block.tensor
            def _(pe):
                if split_u:
                    pe.wait_ge(u_split, KT)
                with pe.Fori(0, KT // 2) as j:
                    for b in range(2):
                        pe.wait_ge(w_split, j * RING + 2 * b + 1)
                        pe.wait_ge(gate_free, j * 2 + b + 1)
                        for h, cols in enumerate(HALVES):
                            mm = k.split_product(2 * b, upper, k.uT_rest, k.uT_upper, ps[:, 4 * b + h, :], cols)
                        mm.then_inc(ring.freed, 1)
                        pe.wait_ge(w_split, j * RING + 2 * b + 2)
                        pe.wait_ge(y_split, kt)
                        pe.wait_ge(branch_free, j * 2 + b + 1)
                        for h, cols in enumerate(HALVES):
                            mm = k.split_product(2 * b + 1, upper, yT_rest, y_upper, ps[:, 4 * b + 2 + h, :], cols, kt)
                        mm.then_inc(ring.freed, 1)

            @block.scalar
            def _(act):
                act.sem_inc(gate_free, 2)
                with act.Fori(0, KT // 2) as j:
                    for b in range(2):
                        act.wait_ge(ring.freed, j * RING + ring.done(base + 2 * b))
                        act.wait_ge(branch_free, j * 2 + b + 2)
                        nc.scalar.activation(gates[:, :], ps[:, 4 * b:4 * b + 2, :].rearrange("p b n -> p (b n)"),
                                             ACT.Sigmoid).then_inc(gate_ready, 1)
                        act.wait_ge(gate_ready, j * 2 + b + 1)
                        act.sem_inc(gate_free, 1)

            @block.vector
            def _(v):
                ch = Chain(v, dve)
                v.sem_inc(branch_free, 2)

                def split_items(j, b):
                    for slot in (2 * b, 2 * b + 1):
                        ring.arrived(v, base, j, slot)
                        cols = slice(0, widths[slot % 2])
                        k.split(v, ch, ring.buf[:, slot, cols], upper[:, slot, cols], ring.rest[:, slot, cols], w_split)

                def merge(j, b):
                    v.wait_ge(gate_ready, j * 2 + b + 1)
                    v.wait_ge(ring.freed, j * RING + ring.done(base + 2 * b + 1))
                    mine = merged[:, bass.ds(j * 2 + b, 1), :].rearrange("p k t -> p (k t)")
                    nc.vector.tensor_tensor(mine if first else prod[:, :], gates[:, :],
                                            ps[:, 4 * b + 2:4 * b + 4, :].rearrange("p b n -> p (b n)"),
                                            ALU.mult).then_inc(prod_ready, 1)
                    v.wait_ge(prod_ready, j * 2 + b + 1)
                    v.sem_inc(branch_free, 1)
                    if not first:
                        ch.step(nc.vector.tensor_tensor(mine, mine, prod[:, :], ALU.add))
                        ch.wait()

                if split_u:
                    for i in range(KT):
                        k.split(v, ch, k.uT[:, i, :], k.uT_upper[:, i, :], k.uT_rest[:, i, :], u_split)
                split_items(0, 0)
                for i in range(kt):
                    k.split(v, ch, yT[:, i, :], y_upper[:, i, :], yT_rest[:, i, :], y_split)
                adds = 0 if first else 1
                with v.Fori(0, KT // 2 - 1) as j, ch.turns(j, KT // 2 - 1, 2 * (2 + adds)):
                    split_items(j, 1)
                    merge(j, 0)
                    split_items(j + 1, 0)
                    merge(j, 1)
                last = KT // 2 - 1
                split_items(last, 1)
                merge(last, 0)
                merge(last, 1)
                ch.wait()


def hyena_stages(k, y_cT, work):
    with ExitStack() as ctx:
        q_tok = k.resident(ctx)("q_tok", [P, TT, 3 * HY_D])
        stage_project_conv(k, "hp", 12, "hy_short_w", "hy_short_b", ACT.Identity, tok_sbuf=q_tok)
        stage_long_conv(k, q_tok, y_cT, work)


def stage_long_conv(k, q_tok, y_cT, work):
    nc, a, ring, ps = k.nc, k.a, k.ring, k.ps
    items = 2 * KTILES
    orders = 2
    base = ring.claim(orders * 2 * items)
    with k.stage("lc") as (sb, sem):
        spare = k.spare[:, :, :].rearrange("p (b r) (q n) -> p b r q n", r=2, q=2)
        spec = spare[:, 0:2]
        middle = sb("middle", [1, 2, HY_D])
        cs, prod = spare[:, 2], spare[:, 3]
        bias = sb("bias", [P, 2, HY_D])
        zf = work[:, :, :].rearrange("p k (h n) -> p (k h) n", n=HY_D)
        bias_in, middle_in, spec_in = sem("bias_in"), sem("middle_in"), [sem("spec_in0"), sem("spec_in1")]
        spec_free, freq_free, time_free = sem("spec_free"), sem("freq_free"), sem("time_free")
        dve, z_ready, zf_ready, middle_mm, middle_done, turned, out_ready = (sem(x) for x in (
            "dve", "z_ready", "zf_ready", "middle_mm", "middle_done", "turned", "out_ready"))
        z = q_tok[:, :, 0:HY_D]
        odds, odds_ready = sb("odds", [P, 2, 2, HY_D]), sem("odds_ready")

        with nc.Block() as block:
            @block.sync
            def _(sp):
                sp.dma_start(bias[:, :, :].rearrange("p o c -> p (o c)"), k.row("hy_bias")).then_inc(bias_in, 16)
                for _ in range(2 * orders):
                    ring.stream(sp)

            @block.gpsimd
            def _(pool):
                for o in range(orders):
                    if o:
                        pool.wait_ge(middle_done, o)
                    pool.dma_start(middle[:, :, :], a["middle"][:, o::2, :]).then_inc(middle_in, 16)
                    with pool.Fori(0, KTILES // 2) as j:
                        for b in range(2):
                            pool.wait_ge(spec_free, j * 2 + (o * KTILES + b + 1))
                            src = a["spectra"][bass.ds(j * 2 + b, 1), :, o::2, :]
                            pool.dma_start(spec[:, b, :, :, :].rearrange("p r q n -> p (r q) n"),
                                           src.rearrange("t p q n -> p (t q) n")).then_inc(spec_in[b], 16)

            @block.tensor
            def _(pe):
                for o in range(orders):
                    if o:
                        pe.wait_ge(z_ready, o * TT)
                    at = base + 2 * o * items
                    with pe.Fori(0, KTILES // 2) as j:
                        for b in range(2):
                            pe.wait_ge(freq_free, j * 2 + (o * KTILES + b + 1))
                            for part in range(2):
                                slot = 2 * b + part
                                ring.arrived(pe, at, j, slot)
                                for t in range(TT):
                                    mm = nc.tensor.matmul(ps[:, 4 * b + 2 * part + t // KTILES, :],
                                                          ring.buf[:, slot, t * P:(t + 1) * P], z[:, t, :],
                                                          start=(t % KTILES == 0), stop=(t % KTILES == KTILES - 1))
                                mm.then_inc(ring.freed, 1)
                    pe.wait_ge(freq_free, (o + 1) * KTILES + 1)
                    for t in range(TT):
                        mm = nc.tensor.matmul(ps[0:1, t // KTILES, :], k.const("sign"), z[:, t, :],
                                              start=(t % KTILES == 0), stop=(t % KTILES == KTILES - 1))
                    mm.then_inc(middle_mm, 1)
                    pe.wait_ge(zf_ready, (o + 1) * KTILES)
                    pe.wait_ge(middle_done, o + 1)
                    at = base + (2 * o + 1) * items
                    with pe.Fori(0, TT // RING) as parity:
                        for slot in range(RING):
                            pe.wait_ge(time_free, parity * RING + (o * TT + slot + 1))
                            ring.arrived(pe, at, parity, slot)
                            for kt in range(KT):
                                mm = nc.tensor.matmul(ps[:, 4 + slot, :], ring.buf[:, slot, kt * P:(kt + 1) * P],
                                                      zf[:, bass.ds(parity * KT + kt, 1), :].rearrange("p k n -> p (k n)"),
                                                      start=(kt == 0), stop=(kt == KT - 1))
                            mm.then_inc(ring.freed, 1)
                pe.wait_ge(z_ready, orders * TT)
                for m in range(HY_D // P):
                    for t in range(TT):
                        mm = nc.tensor.transpose(ps[:, 2 * m + t // 4, (t % 4) * P:(t % 4 + 1) * P],
                                                 z[:, t, m * P:(m + 1) * P], k.const("ident"))
                    mm.then_inc(turned, 1)

            @block.scalar
            def _(act):
                for o in range(orders):
                    at = base + 2 * o * items
                    with act.Fori(0, KTILES // 2) as j:
                        for b in range(2):
                            act.wait_ge(ring.freed, j * RING + ring.done(at + 2 * b + 1))
                            act.wait_ge(freq_free, j * 2 + (o * KTILES + b + 1))
                            sums = ps[:, 4 * b:4 * b + 4, :].rearrange("p (r e) n -> p r e n", e=2)
                            nc.scalar.copy(odds[:, b, :, :], sums[:, :, 1, :]).then_inc(odds_ready, 1)
                for m in range(HY_D // P):
                    act.wait_ge(turned, m + 1)
                    nc.scalar.copy(y_cT[:, m, :].rearrange("p (s e) -> p e s", e=2), ps[:, 2 * m:2 * m + 2, :]
                                   ).then_inc(out_ready, 1)

            @block.vector
            def _(v):
                ch = Chain(v, dve)
                tt = nc.vector.tensor_tensor
                v.sem_inc(spec_free, 2)
                v.sem_inc(freq_free, 2)
                v.sem_inc(time_free, RING)
                v.wait_ge(bias_in, 16)
                for o in range(orders):
                    at = base + 2 * o * items
                    with v.Fori(0, KTILES // 2) as j, ch.turns(j, KTILES // 2, 2 * 9):
                        for b in range(2):
                            v.wait_ge(odds_ready, j * 2 + (o * KTILES + b + 1))
                            sums = ps[:, 4 * b:4 * b + 4, :].rearrange("p (r e) n -> p r e n", e=2)
                            ch.step(tt(cs[:, :, 0, :], sums[:, :, 0, :], odds[:, b, :, :], ALU.add))
                            ch.step(tt(cs[:, :, 1, :], sums[:, :, 0, :], odds[:, b, :, :], ALU.subtract))
                            ch.wait()
                            v.sem_inc(freq_free, 1)
                            v.wait_ge(spec_in[b], j * 16 + (o * KTILES // 2 + 1) * 16)
                            for r in range(2):
                                ch.step(tt(prod[:, r, :, :], cs[:, 0, :, :], spec[:, b, r, :, :], ALU.mult))
                            ch.wait()
                            ch.step(tt(cs[:, 0, :, :], cs[:, 1, :, :], spec[:, b, 1, :, :], ALU.mult))
                            ch.wait()
                            ch.step(tt(cs[:, 1, :, :], cs[:, 1, :, :], spec[:, b, 0, :, :], ALU.mult))
                            ch.wait()
                            v.sem_inc(spec_free, 1)
                            ch.step(tt(prod[:, 0, :, :], prod[:, 0, :, :], cs[:, 0, :, :], ALU.subtract))
                            ch.step(tt(prod[:, 1, :, :], prod[:, 1, :, :], cs[:, 1, :, :], ALU.add))
                            ch.wait()
                            for parity, op in enumerate((ALU.add, ALU.subtract)):
                                half = zf[:, parity * KT:(parity + 1) * KT, :].rearrange("p (r t) n -> p r t n", r=2)
                                ins = tt(half[:, :, bass.ds(j * 2 + b, 1), :].rearrange("p r t n -> p r (t n)"),
                                         prod[:, :, 0, :], prod[:, :, 1, :], op)
                                if parity == 0:
                                    ch.step(ins)
                            ins.then_inc(zf_ready, 1)
                            ch.wait()
                            v.wait_ge(zf_ready, j * 2 + (o * KTILES + b + 1))
                    v.wait_ge(middle_mm, o + 1)
                    v.wait_ge(middle_in, 16 * (o + 1))
                    row = prod[0:1, :, :, :]
                    ch.step(tt(row[:, 0, :, :], ps[0:1, 0:2, :], middle[:, :, :], ALU.mult))
                    for n in range(2):
                        ch.step(tt(row[:, 1, n, :], ps[0:1, n, :], middle[:, 1 - n, :], ALU.mult))
                    ch.wait()
                    ch.step(tt(zf[0:1, KTILES, :], row[:, 0, 0, :], row[:, 0, 1, :], ALU.subtract))
                    tt(zf[0:1, KT + KTILES, :], row[:, 1, 0, :], row[:, 1, 1, :], ALU.add).then_inc(middle_done, 1)
                    ch.wait()
                    v.wait_ge(middle_done, o + 1)
                    at = base + (2 * o + 1) * items
                    with v.Fori(0, TT // RING) as j, ch.turns(j, TT // RING, RING * 2):
                        for slot in range(RING):
                            line = q_tok[:, bass.ds(j * RING + slot, 1), :].rearrange("p t c -> p (t c)")
                            zt, gate = line[:, 0:HY_D], line[:, (o + 1) * HY_D:(o + 2) * HY_D]
                            mine = prod[:, 0, slot % 2, :]
                            ch.step(tt(mine, zt, bias[:, o, :], ALU.mult))
                            ch.wait()
                            v.wait_ge(ring.freed, j * RING + ring.done(at + slot))
                            ch.step(tt(mine, mine, ps[:, 4 + slot, :], ALU.add))
                            ch.wait()
                            v.sem_inc(time_free, 1)
                            tt(zt, mine, gate, ALU.mult).then_inc(z_ready, 1)
                            v.wait_ge(z_ready, j * RING + (o * TT + slot + 1))


def stage_conformer_short(k, y_aT, y_dT):
    nc, ring, ps = k.nc, k.ring, k.ps
    tiles = CONF_D // P
    rows = T // GRID_W
    centre = CONF_K // 2
    base_a = ring.claim(2 * tiles)
    base_d = ring.claim(3 * tiles)
    with k.stage("cs") as (sb, sem):
        sig, val = sb("sig", [P, 2, T]), sb("val", [P, 2, T])
        mean, rstd, squares = sb("mean", [P, T]), sb("rstd", [P, T]), sb("squares", [P, 2, T])
        upper = sb("upper", [P, 2, KT * P], F32R)
        rounded, w_split, squares_used = sem("rounded"), sem("w_split"), sem("squares_used")
        cg, line, conv = sb("cg", [P, 2, T]), sb("line", [P, T + 2]), sb("conv", [P, T])
        sig_ready, val_ready, dve = sem("sig_ready"), sem("val_ready"), sem("dve")
        conf_ready, sum_mm, centred = sem("conf_ready"), sem("sum_mm"), sem("centred")
        squared, var_ready, root = sem("squared"), sem("var_ready"), sem("root")
        scaled, silu_done = sem("scaled"), sem("silu_done")
        cg_ready, xv_read, bg_read = sem("cg_ready"), sem("xv_read"), sem("bg_read")

        def banks(b):
            return ps[:, b:b + 2, :].rearrange("p b n -> p (b n)")

        with nc.Block() as block:
            @block.sync
            def _(sp):
                for _ in range(2):
                    ring.stream(sp)

            @block.gpsimd
            def _(pool):
                ch = Chain(pool, rounded)

                def split_items(base, items):
                    with pool.Fori(0, items // RING) as j, ch.turns(j, items // RING, RING):
                        for slot in range(RING):
                            ring.arrived(pool, base, j, slot)
                            pool.wait_ge(ring.freed, j * RING + ring.done(base + slot - 2))
                            ch.step(nc.gpsimd.tensor_tensor(upper[:, slot % 2, :], ring.buf[:, slot, :],
                                                            k.ones[:, 0:1].broadcast_to([P, KT * P]), ALU.mult))
                            ch.wait()
                            nc.gpsimd.tensor_tensor(ring.rest[:, slot, :], ring.buf[:, slot, :],
                                                    upper[:, slot % 2, :].bitcast(F32),
                                                    ALU.subtract).then_inc(w_split, 1)

                split_items(base_a, 2 * tiles)
                split_items(base_d, 3 * tiles)

            @block.tensor
            def _(pe):
                with pe.Fori(0, tiles // 2) as j:
                    for b in range(2):
                        pe.wait_ge(val_ready, j * 2 + b + 1)
                        for part in range(2):
                            pe.wait_ge(w_split, j * RING + 2 * b + part + 1)
                            for h, cols in enumerate(HALVES):
                                mm = k.split_product(2 * b + part, upper, k.uT_rest, k.uT_upper,
                                                     ps[:, 4 * b + 2 * part + h, :], cols)
                            mm.then_inc(ring.freed, 1)
                pe.wait_ge(val_ready, tiles + 2)

                def short(i):
                    for part, read in enumerate((cg_ready, xv_read, bg_read)):
                        m = 3 * i + part
                        if i:
                            pe.wait_ge(read, i)
                        pe.wait_ge(w_split, 2 * tiles + m + 1)
                        for h, cols in enumerate(HALVES):
                            mm = k.split_product(m % RING, upper, k.uT_rest, k.uT_upper, ps[:, 2 * part + h, :], cols)
                        mm.then_inc(ring.freed, 1)

                def channel_sums(t, src, done):
                    for h, (lo, hi) in enumerate(HALVES):
                        mm = nc.tensor.matmul(ps[:, 6 + h, :], k.ones[:, :], src[:, lo:hi],
                                              start=(t == 0), stop=(t == tiles - 1))
                    mm.then_inc(done, 1)

                short(0)
                short(1)
                pe.wait_ge(conf_ready, tiles)
                for t in range(tiles):
                    channel_sums(t, y_aT[:, t, :], sum_mm)
                short(2)
                for t in range(tiles):
                    pe.wait_ge(squared, t + 1)
                    channel_sums(t, squares[:, t % 2, :], squares_used)
                short(3)

            @block.scalar
            def _(act):
                with act.Fori(0, tiles // 2) as j:
                    for b in range(2):
                        act.wait_ge(ring.freed, j * RING + ring.done(base_a + 2 * b + 1))
                        act.wait_ge(val_ready, j * 2 + b + 1)
                        nc.scalar.activation(sig[:, b, :], banks(4 * b + 2), ACT.Sigmoid).then_inc(sig_ready, 1)

                def copy_cg(i):
                    act.wait_ge(ring.freed, ring.done(base_d + 3 * i))
                    if i >= 2:
                        act.wait_ge(xv_read, i - 1)
                    nc.scalar.copy(cg[:, i % 2, :], banks(0)).then_inc(cg_ready, 1)

                copy_cg(0)
                copy_cg(1)
                for t in range(tiles):
                    act.wait_ge(centred, t + 1)
                    if t >= 2:
                        act.wait_ge(squares_used, t - 1)
                    nc.scalar.activation(squares[:, t % 2, :], y_aT[:, t, :], ACT.Square).then_inc(squared, 1)
                copy_cg(2)
                act.wait_ge(var_ready, 1)
                nc.scalar.activation(rstd[:, :], rstd[:, :], ACT.Sqrt).then_inc(root, 1)
                copy_cg(3)
                for t in range(tiles):
                    act.wait_ge(scaled, t + 1)
                    nc.scalar.activation(y_aT[:, t, :], y_aT[:, t, :], ACT.Silu, bias=k.col("conf_ln_b", t),
                                         scale=k.col("conf_ln_g", t)).then_inc(silu_done, 1)
                act.wait_ge(silu_done, tiles)

            @block.vector
            def _(v):
                ch = Chain(v, dve)
                v.sem_inc(val_ready, 2)
                ch.step(nc.vector.memset(line[:, :], 0.0))
                with v.Fori(0, tiles // 2) as j, ch.turns(j, tiles // 2, 2 * (CONF_K - 1)):
                    for b in range(2):
                        t = j * 2 + b
                        v.wait_ge(sig_ready, t + 1)
                        nc.vector.tensor_tensor(val[:, b, :], sig[:, b, :], banks(4 * b), ALU.mult).then_inc(val_ready, 1)
                        v.wait_ge(val_ready, t + 3)
                        acc = y_aT[:, bass.ds(t, 1), :].rearrange("p k t -> p (k t)")

                        def tap(i):
                            return k.col("conf_dw_w", 0, CONF_K * tiles)[:, bass.ds(t * CONF_K + i, 1)]

                        ch.step(nc.vector.tensor_scalar(acc, val[:, b, :], tap(centre),
                                                        k.col("conf_dw_b", 0, tiles)[:, bass.ds(t, 1)], ALU.mult, ALU.add))
                        others = [i for i in range(CONF_K) if i != centre]
                        for i in others:
                            s = i - centre
                            lo, hi = max(0, -s) * GRID_W, (rows - max(0, s)) * GRID_W
                            ch.wait()
                            ins = nc.vector.scalar_tensor_tensor(
                                out=acc[:, lo:hi], in0=val[:, b, lo + s * GRID_W:hi + s * GRID_W], scalar=tap(i),
                                in1=acc[:, lo:hi], op0=ALU.mult, op1=ALU.add)
                            if i == others[-1]:
                                ins.then_inc(conf_ready, 1)
                            else:
                                ch.step(ins)

                def short(i):
                    v.wait_ge(ring.freed, ring.done(base_d + 3 * i + 1))
                    v.wait_ge(cg_ready, i + 1)
                    nc.vector.tensor_tensor(line[:, 1:T + 1], cg[:, i % 2, :], banks(2), ALU.mult).then_inc(xv_read, 1)
                    v.wait_ge(xv_read, i + 1)
                    taps = [k.col("sc_conv_w", 3 * i + n) for n in range(3)]
                    ch.step(nc.vector.tensor_scalar(conv[:, :], line[:, 0:T], taps[0], None, ALU.mult))
                    for n in (1, 2):
                        ch.wait()
                        ch.step(nc.vector.scalar_tensor_tensor(out=conv[:, :], in0=line[:, n:T + n], scalar=taps[n],
                                                               in1=conv[:, :], op0=ALU.mult, op1=ALU.add))
                    ch.wait()
                    v.wait_ge(ring.freed, ring.done(base_d + 3 * i + 2))
                    nc.vector.tensor_tensor(y_dT[:, i, :], conv[:, :], banks(4), ALU.mult).then_inc(bg_read, 1)

                short(0)
                short(1)
                v.wait_ge(sum_mm, tiles)
                ch.step(nc.vector.tensor_scalar(mean[:, :], banks(6), 1.0 / CONF_D, None, ALU.mult))
                ch.wait()
                for t in range(tiles):
                    nc.vector.tensor_tensor(y_aT[:, t, :], y_aT[:, t, :], mean[:, :], ALU.subtract).then_inc(centred, 1)
                short(2)
                v.wait_ge(squares_used, tiles)
                nc.vector.tensor_scalar(rstd[:, :], banks(6), 1.0 / CONF_D, EPS, ALU.mult, ALU.add).then_inc(var_ready, 1)
                v.wait_ge(root, 1)
                ch.step(nc.vector.reciprocal(rstd[:, :], rstd[:, :]))
                ch.wait()
                for t in range(tiles):
                    nc.vector.tensor_tensor(y_aT[:, t, :], y_aT[:, t, :], rstd[:, :], ALU.mult).then_inc(scaled, 1)
                short(3)
                v.wait_ge(bg_read, tiles)


class LayerNorm:

    def __init__(self, k, sb, sem, g_row, b_row):
        self.k, self.g, self.b = k, g_row, b_row
        self.stats, self.mv = sb("ln_stats", [P, 2, 6]), sb("ln_mv", [P, 2])
        self.var, self.root = sem("ln_var"), sem("ln_root")

    def scalar(self, act, n):
        act.wait_ge(self.var, n + 1)
        self.k.nc.scalar.activation(self.mv[:, 1:2], self.mv[:, 1:2], ACT.Sqrt).then_inc(self.root, 1)

    def normalise(self, v, ch, s, n):
        nc = self.k.nc
        for h, (lo, hi) in enumerate(HALVES):
            ch.step(nc.vector.bn_stats(self.stats[:, h, :], s[:, lo:hi]))
        ch.wait()
        ch.step(nc.vector.bn_aggr(self.mv[:, :], self.stats[:, :, :]))
        ch.wait()
        nc.vector.tensor_scalar(self.mv[:, 1:2], self.mv[:, 1:2], EPS, None, ALU.add).then_inc(self.var, 1)
        v.wait_ge(self.root, n + 1)
        ch.step(nc.vector.reciprocal(self.mv[:, 1:2], self.mv[:, 1:2]))
        ch.wait()
        return nc.vector.tensor_scalar(s, s, self.mv[:, 0:1], self.mv[:, 1:2], ALU.subtract, ALU.mult)

    def vector(self, v, ch, s, n, out, last_sem):
        nc = self.k.nc
        ch.step(self.normalise(v, ch, s, n))
        ch.wait()
        ch.step(nc.vector.tensor_tensor(s, s, self.g, ALU.mult))
        ch.wait()
        nc.vector.tensor_tensor(out, s, self.b, ALU.add).then_inc(last_sem, 1)


def tail_stages(k, merged):
    with ExitStack() as ctx:
        sb = k.resident(ctx)
        rows = sb("mod_rows", [P, 4, D])
        weights, dest = sb("weights", [P, 2, TT]), sb("dest", [P, 2, TT], I32)
        plan = sb("plan", [1, SLOTS + 1], I32)
        with ExitStack() as inner:
            logits = k.resident(inner)("logits", [P, TT, 36])
            stage_output(k, merged, rows, logits)
            stage_route(k, logits, weights, dest, plan)
        stage_experts(k, dest, plan, merged)
        stage_combine(k, rows, weights, dest)


def stage_output(k, merged, rows, logits):
    nc, a, ps = k.nc, k.a, k.ps
    u = k.uT
    with k.stage("out") as (sb, sem):
        w_out, w_rt = sb("w_out", [P, KT, D]), sb("w_rt", [P, KT, 36])
        ln_g, ln_b, rt_b = sb("ln_g", [P, D]), sb("ln_b", [P, D]), sb("rt_b", [P, 36])
        x, h1, s = sb("x", [P, 2, D]), sb("h1", [P, 2, D]), sb("s", [P, D])
        u_chan = sb("u_chan", [P, KT, P])
        ln = LayerNorm(k, sb, sem, ln_g[:, :], ln_b[:, :])
        w_in, small_in, x_in = sem("w_in"), sem("small_in"), [sem("x_in0"), sem("x_in1")]
        rows_mm, rows_ready, mix_mm, dve = sem("rows_mm"), sem("rows_ready"), sem("mix_mm"), sem("dve")
        mix_read, x_used, h_ready, h_out = sem("mix_read"), sem("x_used"), sem("h_ready"), [sem("h_out0"), sem("h_out1")]
        u_ready, u_turned, u_chan_ready, logit_mm, logit_ready = (sem(n) for n in (
            "u_ready", "u_turned", "u_chan_ready", "logit_mm", "logit_ready"))

        with nc.Block() as block:
            @block.sync
            def _(sp):
                small = ((w_rt[:, :, :], a["w_rt"]), (ln_g[:, :], k.row("ln_g1")), (ln_b[:, :], k.row("ln_b1")),
                         (rt_b[:, :], k.row("rt_b")))
                sp.dma_start(w_out[:, :, :], a["w_out"]).then_inc(w_in, 16)
                for dst, src in small:
                    sp.dma_start(dst, src).then_inc(small_in, 16)
                for t in range(TT):
                    if t >= 2:
                        sp.wait_ge(x_used, t - 1)
                    sp.dma_start(x[:, t % 2, :], a["x"][t * P:(t + 1) * P, :]).then_inc(x_in[t % 2], 16)

            @block.gpsimd
            def _(pool):
                for t in range(TT):
                    pool.wait_ge(h_ready, t + 1)
                    pool.dma_start(a["h1"][t], h1[:, t % 2, :]).then_inc(h_out[t % 2], 16)
                for b in range(2):
                    pool.wait_ge(h_out[b], 16 * TT // 2)

            @block.tensor
            def _(pe):
                for part in range(4):
                    for kt in range(KT):
                        m = (2 + part) * KT + kt
                        mm = nc.tensor.matmul(ps[:, 2 * part + kt // 4, (kt % 4) * P:(kt % 4 + 1) * P],
                                              k.mod[:, m, 0:1].broadcast_to([P, P]), k.const("ident"),
                                              start=True, stop=True)
                    mm.then_inc(rows_mm, 1)
                pe.wait_ge(w_in, 16)
                pe.wait_ge(small_in, 64)
                pe.wait_ge(rows_ready, 4)

                def project(t):
                    if t >= 2:
                        pe.wait_ge(mix_read, t - 1)
                    for h, (lo, hi) in enumerate(HALVES):
                        for kt in range(KT):
                            mm = nc.tensor.matmul(ps[:, 2 * (t % 2) + h, :], merged[:, kt, t * P:(t + 1) * P],
                                                  w_out[:, kt, lo:hi], start=(kt == 0), stop=(kt == KT - 1))
                    mm.then_inc(mix_mm, 1)

                def turn(t):
                    pe.wait_ge(u_ready, t + 1)
                    if t:
                        pe.wait_ge(u_chan_ready, t)
                    for kt in range(KT):
                        mm = nc.tensor.transpose(ps[:, 4 + kt // 4, (kt % 4) * P:(kt % 4 + 1) * P],
                                                 u[:, t, kt * P:(kt + 1) * P], k.const("ident"))
                    mm.then_inc(u_turned, 1)

                def route(t):
                    pe.wait_ge(u_chan_ready, t + 1)
                    if t:
                        pe.wait_ge(logit_ready, t)
                    for kt in range(KT):
                        mm = nc.tensor.matmul(ps[:, 6, 0:36], u_chan[:, kt, :], w_rt[:, kt, :],
                                              start=(kt == 0), stop=(kt == KT - 1))
                    mm.then_inc(logit_mm, 1)

                for t in range(TT + 2):
                    if t < TT:
                        project(t)
                    if t >= 2:
                        route(t - 2)
                    if 1 <= t <= TT:
                        turn(t - 1)

            @block.scalar
            def _(act):
                for part in range(4):
                    act.wait_ge(rows_mm, part + 1)
                    nc.scalar.copy(rows[:, part, :], ps[:, 2 * part:2 * part + 2, :].rearrange("p b n -> p (b n)")
                                   ).then_inc(rows_ready, 1)
                for t in range(TT):
                    ln.scalar(act, t)
                    act.wait_ge(u_turned, t + 1)
                    if t:
                        act.wait_ge(logit_mm, t)
                    nc.scalar.copy(u_chan[:, :, :], ps[:, 4:6, :].rearrange("p b (k n) -> p (b k) n", n=P)
                                   ).then_inc(u_chan_ready, 1)

            @block.vector
            def _(v):
                ch = Chain(v, dve)
                v.wait_ge(small_in, 64)
                v.wait_ge(rows_ready, 4)

                def take_logits(t):
                    v.wait_ge(logit_mm, t + 1)
                    nc.vector.tensor_tensor(logits[:, t, :], ps[:, 6, 0:36], rt_b[:, :], ALU.add).then_inc(logit_ready, 1)

                for t in range(TT):
                    b = t % 2
                    v.wait_ge(mix_mm, t + 1)
                    if t:
                        v.wait_ge(u_ready, t)
                    nc.vector.tensor_tensor(s[:, :], ps[:, 2 * b:2 * b + 2, :].rearrange("p b n -> p (b n)"),
                                            rows[:, 0, :], ALU.mult).then_inc(mix_read, 1)
                    v.wait_ge(mix_read, t + 1)
                    v.wait_ge(x_in[b], 16 * (t // 2 + 1))
                    nc.vector.scalar_tensor_tensor(out=s[:, :], in0=x[:, b, :], scalar=ALPHA, in1=s[:, :],
                                                   op0=ALU.mult, op1=ALU.add).then_inc(x_used, 1)
                    v.wait_ge(x_used, t + 1)
                    if t >= 2:
                        v.wait_ge(h_out[b], 16 * (t // 2))
                    ln.vector(v, ch, s[:, :], t, h1[:, b, :], h_ready)
                    v.wait_ge(h_ready, t + 1)
                    ch.step(nc.vector.tensor_tensor(s[:, :], h1[:, b, :], rows[:, 2, :], ALU.mult))
                    ch.wait()
                    nc.vector.tensor_tensor(u[:, t, :], s[:, :], rows[:, 1, :], ALU.add).then_inc(u_ready, 1)
                    if t >= 2:
                        take_logits(t - 2)
                take_logits(TT - 2)
                take_logits(TT - 1)
                v.wait_ge(logit_ready, TT)


def stage_route(k, logits, weights, dest, plan):
    nc, ps = k.nc, k.ps
    E, G = EXPERTS, MOE_GROUPS
    with k.stage("rt") as (sb, sem):
        top = sb("top", [P, TT])
        miss_g, cand_g = sb("miss_g", [P, TT, G]), sb("cand_g", [P, TT, G])
        group, g_exp, g_prob = sb("group", [P, TT]), sb("g_exp", [P, TT, G]), sb("g_prob", [P, TT])
        own, miss, cand = sb("own", [P, TT, E]), sb("miss", [P, TT, E]), sb("cand", [P, TT, E])
        best, which = sb("best", [P, 2, TT]), sb("which", [P, TT])
        hot = sb("hot", [P, 2, TT, E])
        chosen, before = sb("chosen", [P, TT, E]), sb("before", [P, TT, E])
        every, count = sb("every", [P, E]), sb("count", [P, E])
        blocks, scan = sb("blocks", [P, E]), sb("scan", [P, 2, E])
        first, place = sb("first", [P, E]), sb("place", [P, TT, E])
        dest_f, owner, owner_e = sb("dest_f", [P, 2, TT]), sb("owner", [1, SLOTS, E]), sb("owner_e", [1, SLOTS])
        dve, g_ready, g_exp_ready, d_ready, d_exp_ready, rank_in, rank_mm = (sem(n) for n in (
            "dve", "g_ready", "g_exp_ready", "d_ready", "d_exp_ready", "rank_in", "rank_mm"))
        iota = k.const("iota")

        def to_tiles(row, width):
            return row.unsqueeze(1).broadcast_to([P, TT, width])

        def wide(v, width):
            return v.unsqueeze(2).broadcast_to([P, TT, width])

        with nc.Block() as block:
            @block.tensor
            def _(pe):
                pe.wait_ge(rank_in, 1)
                flat = "p t e -> p (t e)"
                nc.tensor.matmul(ps[:, 0, 0:TT * E], k.ones[:, :], before[:, :, :].rearrange(flat), start=True, stop=False)
                nc.tensor.matmul(ps[:, 0, 0:TT * E], k.const("before"), chosen[:, :, :].rearrange(flat),
                                 start=False, stop=True)
                nc.tensor.matmul(ps[:, 1, 0:E], k.ones[:, :], every[:, :], start=True, stop=True).then_inc(rank_mm, 1)

            @block.scalar
            def _(act):
                act.wait_ge(g_ready, 1)
                nc.scalar.activation(g_exp[:, :, :], cand_g[:, :, :], ACT.Exp).then_inc(g_exp_ready, 1)
                act.wait_ge(d_ready, 1)
                nc.scalar.activation(which[:, :], which[:, :], ACT.Exp).then_inc(d_exp_ready, 1)

            @block.vector
            def _(v):
                ch = Chain(v, dve)

                def do(ins):
                    ch.step(ins)
                    ch.wait()

                tt, ts, stt = nc.vector.tensor_tensor, nc.vector.tensor_scalar, nc.vector.scalar_tensor_tensor
                reduce = nc.vector.tensor_reduce
                g = logits[:, :, 0:G]
                do(reduce(top[:, :], g, AX.X, ALU.max))
                do(tt(miss_g[:, :, :], g, wide(top[:, :], G), ALU.is_lt))
                tt(cand_g[:, :, :], g, wide(top[:, :], G), ALU.subtract).then_inc(g_ready, 1)
                v.wait_ge(g_exp_ready, 1)
                do(reduce(g_prob[:, :], g_exp[:, :, :], AX.X, ALU.add))
                do(nc.vector.reciprocal(g_prob[:, :], g_prob[:, :]))
                do(stt(out=cand_g[:, :, :], in0=miss_g[:, :, :], scalar=100.0, in1=to_tiles(iota[:, 0:G], G),
                       op0=ALU.mult, op1=ALU.add))
                do(reduce(group[:, :], cand_g[:, :, :], AX.X, ALU.min))
                do(tt(miss_g[:, :, :], to_tiles(iota[:, 0:G], G), wide(group[:, :], G), ALU.not_equal))
                do(ts(miss_g[:, :, :], miss_g[:, :, :], -BIG, None, ALU.mult))
                for t in range(TT):
                    ch.step(tt(own[:, t, :].rearrange("p (g e) -> p g e", g=G),
                               logits[:, t, G:G + E].rearrange("p (g e) -> p g e", g=G),
                               miss_g[:, t, :].unsqueeze(2).broadcast_to([P, G, MOE_EPG]), ALU.add))
                ch.wait()
                for r in range(2):
                    do(reduce(best[:, r, :], own[:, :, :], AX.X, ALU.max))
                    do(tt(miss[:, :, :], own[:, :, :], wide(best[:, r, :], E), ALU.is_lt))
                    do(stt(out=cand[:, :, :], in0=miss[:, :, :], scalar=100.0, in1=to_tiles(iota[:, 0:E], E),
                           op0=ALU.mult, op1=ALU.add))
                    do(reduce(which[:, :], cand[:, :, :], AX.X, ALU.min))
                    do(tt(hot[:, r, :, :], to_tiles(iota[:, 0:E], E), wide(which[:, :], E), ALU.is_equal))
                    if r == 0:
                        do(stt(out=own[:, :, :], in0=hot[:, 0, :, :], scalar=-3 * BIG, in1=own[:, :, :],
                               op0=ALU.mult, op1=ALU.add))
                tt(which[:, :], best[:, 1, :], best[:, 0, :], ALU.subtract).then_inc(d_ready, 1)
                v.wait_ge(d_exp_ready, 1)
                do(ts(top[:, :], which[:, :], 1.0, None, ALU.add))
                do(nc.vector.reciprocal(top[:, :], top[:, :]))
                do(tt(weights[:, 0, :], top[:, :], g_prob[:, :], ALU.mult))
                do(tt(weights[:, 1, :], weights[:, 0, :], which[:, :], ALU.mult))
                do(tt(chosen[:, :, :], hot[:, 0, :, :], hot[:, 1, :, :], ALU.add))
                do(nc.vector.memset(before[:, 0, :], 0.0))
                for t in range(1, TT):
                    do(tt(before[:, t, :], before[:, t - 1, :], chosen[:, t - 1, :], ALU.add))
                tt(every[:, :], before[:, TT - 1, :], chosen[:, TT - 1, :], ALU.add).then_inc(rank_in, 1)
                v.wait_ge(rank_mm, 1)
                do(nc.vector.tensor_copy(count[:, :], ps[:, 1, 0:E]))
                do(ts(blocks[:, :], count[:, :], 0.0, None, ALU.is_gt))
                for n in range(1, TT):
                    do(stt(out=blocks[:, :], in0=count[:, :], scalar=float(n * P), in1=blocks[:, :],
                           op0=ALU.is_gt, op1=ALU.add))
                for n, shift in enumerate((1, 2, 4, 8, 16)):
                    dst = scan[:, n % 2, :]
                    old = blocks[:, :] if n == 0 else scan[:, 1 - n % 2, :]
                    do(nc.vector.tensor_copy(dst[:, 0:shift], old[:, 0:shift]))
                    do(tt(dst[:, shift:E], old[:, shift:E], old[:, 0:E - shift], ALU.add))
                ends = scan[:, 0, :]
                do(tt(first[:, :], ends, blocks[:, :], ALU.subtract))
                do(stt(out=place[:, :, :], in0=to_tiles(first[:, :], E), scalar=float(P),
                       in1=ps[:, 0, 0:TT * E].rearrange("p (t e) -> p t e", e=E), op0=ALU.mult, op1=ALU.add))
                for r in range(2):
                    do(tt(cand[:, :, :], hot[:, r, :, :], place[:, :, :], ALU.mult))
                    do(reduce(dest_f[:, r, :], cand[:, :, :], AX.X, ALU.add))
                do(nc.vector.tensor_copy(dest[:, :, :], dest_f[:, :, :]))
                do(tt(owner[:, :, :], ends[0:1, :].unsqueeze(1).broadcast_to([1, SLOTS, E]),
                      iota[0:1, 0:SLOTS].unsqueeze(2).broadcast_to([1, SLOTS, E]), ALU.is_le))
                do(reduce(owner_e[:, :], owner[:, :, :], AX.X, ALU.add))
                do(ts(owner_e[:, :], owner_e[:, :], float(E - 1), None, ALU.min))
                do(nc.vector.tensor_copy(plan[:, 0:SLOTS], owner_e[:, :]))
                do(nc.vector.tensor_copy(plan[:, SLOTS:SLOTS + 1], ends[0:1, E - 1:E]))


def stage_experts(k, dest, plan, merged):
    nc, a, ps = k.nc, k.a, k.ps
    with k.stage("ex") as (sb, sem):
        w_g, w_u = sb("w_g", [P, 2, KT, FF]), sb("w_u", [P, 2, KT, FF])
        w_d = merged[:, :, :].rearrange("p (b f) d -> p b f d", b=2)
        x, y = k.uT[:, 0:2, :], k.uT[:, 4:6, :]
        x_chan = k.uT[:, 2:4, :].rearrange("p b (k n) -> p b k n", n=P)
        act_g, hid, hid_chan = sb("act_g", [P, FF]), sb("hid", [P, FF]), sb("hid_chan", [P, FF // P, P])
        g_in, u_in, d_in = ([sem(f"{n}{b}") for b in range(2)] for n in ("g_in", "u_in", "d_in"))
        x_in, y_out = [sem("x_in0"), sem("x_in1")], [sem("y_out0"), sem("y_out1")]
        gate_mm, up_mm, x_mm, hid_mm, down_mm = (sem(n) for n in ("gate_mm", "up_mm", "x_mm", "hid_mm", "down_mm"))
        sent, x_first = sem("sent"), sem("x_first")
        y_free, x_ready, g_ready, hid_ready, hidc_ready, y_ready = (sem(n) for n in (
            "y_free", "x_ready", "g_ready", "hid_ready", "hidc_ready", "y_ready"))

        rows = a["moe"].rearrange("(s p) d -> s p d", p=P)

        def blocks(eng, body):
            n = eng.value_load(plan[0:1, SLOTS:SLOTS + 1], min_val=0, max_val=BLOCKS)
            with eng.Fori(0, SLOTS // 2) as j:
                for b in range(2):
                    with eng.If(j * 2 + b < n):
                        body(j * 2 + b, b, j)

        with nc.Block() as block:
            @block.sync
            def _(sp):
                for use in (up_mm, down_mm):
                    sp.sem_inc(use, 2)

                def body(i, b, j):
                    e = sp.value_load(plan[0:1, bass.ds(i, 1)], min_val=0, max_val=EXPERTS - 1)
                    sp.wait_ge(sent, 2 * TT * 16)
                    sp.wait_ge(x_mm, i + 1)
                    after = nc.s_assert_within(i + 1, 1, SLOTS - 1, skip_runtime_bounds_check_because=(
                        "the body runs for i < number of blocks <= BLOCKS < SLOTS only"))
                    sp.dma_start(x[:, 1 - b, :], item(rows, after)).then_inc(x_in[1 - b], 16)
                    sp.wait_ge(up_mm, i + 1)
                    for dst, name, s in ((w_g, "ex_g", g_in), (w_u, "ex_u", u_in), (w_d, "ex_d", d_in)):
                        if dst is w_d:
                            sp.wait_ge(down_mm, i + 1)
                        src = a[name][bass.ds(e, 1)].rearrange("o (k p) f -> p (o k) f", p=P)
                        sp.dma_start(dst[:, b, :, :], src).then_inc(s[b], 16)

                blocks(sp, body)

            @block.gpsimd
            def _(pool):
                pool.sem_inc(y_free, 2)
                pool.wait_ge(k.blank, 16 * k.blank_parts)
                for t in range(TT):
                    for r in range(2):
                        pool.indirect_dma_start(out=a["moe"], out_offset=bass.IndirectOffsetOnAxis(dest[:, r, t:t + 1], 0),
                                                in_=k.uT[:, t, :], in_offset=None).then_inc(sent, 16)
                pool.wait_ge(sent, 2 * TT * 16)
                pool.dma_start(x[:, 0, :], a["moe"][0:P, :]).then_inc(x_first, 16)

                def body(i, b, j):
                    pool.wait_ge(y_ready, i + 2)
                    pool.dma_start(item(rows, i), y[:, b, :]).then_inc(y_out[b], 16)
                    pool.wait_ge(y_out[b], j * 16 + 16)
                    pool.sem_inc(y_free, 1)

                blocks(pool, body)

            @block.tensor
            def _(pe):
                pe.sem_inc(x_mm, 1)
                pe.sem_inc(hid_mm, 1)

                def turn_x(b, kts):
                    for kt in kts:
                        mm = nc.tensor.transpose(ps[:, 2 + kt // 4, (kt % 4) * P:(kt % 4 + 1) * P],
                                                 x[:, b, kt * P:(kt + 1) * P], k.const("ident"))
                    if KT - 1 in kts:
                        mm.then_inc(x_mm, 1)

                pe.wait_ge(x_first, 16)
                turn_x(0, range(KT))

                def body(i, b, j):
                    pe.wait_ge(x_ready, i + 1)
                    pe.wait_ge(hid_ready, i + 1)
                    for w, arrived, bank, done in ((w_g, g_in, 0, gate_mm), (w_u, u_in, 1, up_mm)):
                        pe.wait_ge(arrived[b], j * 16 + 16)
                        for kt in range(KT):
                            mm = nc.tensor.matmul(ps[:, bank, :], x_chan[:, b, kt, :], w[:, b, kt, :],
                                                  start=(kt == 0), stop=(kt == KT - 1))
                        mm.then_inc(done, 1)
                    pe.wait_ge(x_in[1 - b], j * 16 + 16)
                    turn_x(1 - b, range(KT // 2))
                    pe.wait_ge(hid_ready, i + 2)
                    for f in range(FF // P):
                        mm = nc.tensor.transpose(ps[:, 4, f * P:(f + 1) * P], hid[:, f * P:(f + 1) * P], k.const("ident"))
                    mm.then_inc(hid_mm, 1)
                    turn_x(1 - b, range(KT // 2, KT))
                    pe.wait_ge(hidc_ready, i + 1)
                    pe.wait_ge(d_in[b], j * 16 + 16)
                    pe.wait_ge(y_ready, i + 1)
                    for h, (lo, hi) in enumerate(HALVES):
                        for f in range(FF // P):
                            mm = nc.tensor.matmul(ps[:, 5 + h, :], hid_chan[:, f, :], w_d[:, b, f, lo:hi],
                                                  start=(f == 0), stop=(f == FF // P - 1))
                    mm.then_inc(down_mm, 1)

                blocks(pe, body)

            @block.scalar
            def _(act):
                act.sem_inc(y_ready, 1)
                def x_out(b):
                    nc.scalar.copy(x_chan[:, b, :, :], ps[:, 2:4, :].rearrange("p b (k n) -> p (b k) n", n=P)
                                   ).then_inc(x_ready, 1)

                act.wait_ge(x_mm, 2)
                x_out(0)

                def body(i, b, j):
                    act.wait_ge(gate_mm, i + 1)
                    nc.scalar.activation(act_g[:, :], ps[:, 0, :], ACT.Silu).then_inc(g_ready, 1)
                    act.wait_ge(x_mm, i + 3)
                    x_out(1 - b)
                    act.wait_ge(down_mm, i + 3)
                    act.wait_ge(y_free, i + 1)
                    nc.scalar.copy(y[:, b, :], ps[:, 5:7, :].rearrange("p b n -> p (b n)")).then_inc(y_ready, 1)

                blocks(act, body)

            @block.vector
            def _(v):
                v.sem_inc(hid_ready, 1)
                def body(i, b, j):
                    v.wait_ge(g_ready, i + 1)
                    v.wait_ge(up_mm, i + 3)
                    v.wait_ge(hid_mm, i + 1)
                    nc.vector.tensor_tensor(hid[:, :], act_g[:, :], ps[:, 1, :], ALU.mult).then_inc(hid_ready, 1)
                    v.wait_ge(hid_mm, i + 2)
                    nc.vector.tensor_copy(hid_chan[:, :, :], ps[:, 4, :].rearrange("p (f n) -> p f n", n=P)
                                          ).then_inc(hidc_ready, 1)

                blocks(v, body)


def stage_combine(k, rows, weights, dest):
    nc, a = k.nc, k.a
    with k.stage("cb") as (sb, sem):
        y, h1 = sb("y", [P, 2, 2, D]), sb("h1", [P, 2, D])
        ln_g, ln_b = sb("ln_g", [P, D]), sb("ln_b", [P, D])
        s, res = sb("s", [P, 3, D]), sb("res", [P, 2, D])
        ln = LayerNorm(k, sb, sem, ln_g[:, :], ln_b[:, :])
        small_in, y_in, h_in = sem("small_in"), [sem("y_in0"), sem("y_in1")], [sem("h_in0"), sem("h_in1")]
        out = [sem("out0"), sem("out1")]
        dve, started, y_used, normed, weighted, ready = (sem(n) for n in (
            "dve", "started", "y_used", "normed", "weighted", "ready"))

        with nc.Block() as block:
            @block.sync
            def _(sp):
                sp.dma_start(ln_g[:, :], k.row("ln_g2")).then_inc(small_in, 16)
                sp.dma_start(ln_b[:, :], k.row("ln_b2")).then_inc(small_in, 16)
                for t in range(TT + 2):
                    if t < TT:
                        if t >= 2:
                            sp.wait_ge(y_used, t - 1)
                        sp.dma_start(h1[:, t % 2, :], a["h1"][t]).then_inc(h_in[t % 2], 16)
                    if t >= 2:
                        sp.wait_ge(ready, t - 1)
                        sp.dma_start(a["out"][(t - 2) * P:(t - 1) * P, :], res[:, t % 2, :]).then_inc(out[t % 2], 16)
                for b in range(2):
                    sp.wait_ge(out[b], 16 * TT // 2)

            @block.gpsimd
            def _(pool):
                def gather(t):
                    for r in range(2):
                        pool.indirect_dma_start(out=y[:, t % 2, r, :], out_offset=None, in_=a["moe"],
                                                in_offset=bass.IndirectOffsetOnAxis(dest[:, r, t:t + 1], 0)
                                                ).then_inc(y_in[t % 2], 16)

                gather(0)
                gather(1)
                pool.wait_ge(small_in, 32)
                for t in range(TT):
                    if t + 2 < TT:
                        pool.wait_ge(y_used, t + 1)
                        gather(t + 2)
                    acc = s[:, t % 3, :]
                    pool.wait_ge(normed, t + 1)
                    nc.gpsimd.tensor_tensor(acc, acc, ln_g[:, :], ALU.mult).then_inc(weighted, 1)
                    pool.wait_ge(weighted, t + 1)
                    if t >= 2:
                        pool.wait_ge(out[t % 2], 16 * (t // 2))
                    nc.gpsimd.tensor_tensor(res[:, t % 2, :], acc, ln_b[:, :], ALU.add).then_inc(ready, 1)

            @block.scalar
            def _(act):
                def start(t):
                    act.wait_ge(y_in[t % 2], 32 * (t // 2 + 1))
                    if t >= 3:
                        act.wait_ge(ready, t - 2)
                    nc.scalar.activation(s[:, t % 3, :], y[:, t % 2, 0, :], ACT.Copy,
                                         scale=weights[:, 0, t:t + 1]).then_inc(started, 1)

                start(0)
                for t in range(TT):
                    if t + 1 < TT:
                        start(t + 1)
                    ln.scalar(act, t)

            @block.vector
            def _(v):
                ch = Chain(v, dve)
                for t in range(TT):
                    b = t % 2
                    acc = s[:, t % 3, :]
                    v.wait_ge(started, t + 1)
                    ch.step(nc.vector.scalar_tensor_tensor(out=acc, in0=y[:, b, 1, :], scalar=weights[:, 1, t:t + 1],
                                                           in1=acc, op0=ALU.mult, op1=ALU.add))
                    ch.wait()
                    ch.step(nc.vector.tensor_tensor(acc, acc, rows[:, 3, :], ALU.mult))
                    ch.wait()
                    v.wait_ge(h_in[b], 16 * (t // 2 + 1))
                    nc.vector.scalar_tensor_tensor(out=acc, in0=h1[:, b, :], scalar=ALPHA, in1=acc, op0=ALU.mult,
                                                   op1=ALU.add).then_inc(y_used, 1)
                    v.wait_ge(y_used, t + 1)
                    if t:
                        v.wait_ge(normed, t)
                    ln.normalise(v, ch, acc, t).then_inc(normed, 1)


def weight_segments(a):
    def whole(name, n):
        return name, n, lambda j, slot: item(a[name], j * RING + slot)

    def merge(branch, gate):
        def source(j, slot):
            if slot % 2 == 0:
                return item(a["w_gate"], j * 2 + (gate * KT + slot // 2))
            return item(a["w_br_" + branch], j * 2 + slot // 2)

        return "merge_" + branch, 2 * KT, source

    tables = [whole("dft", TT), whole("idft", TT)]
    return [whole("w_mod", 48), whole("dft", TT), whole("w_hy", 3 * HY_D // P), *tables, *tables,
            whole("w_xbc", (SSD_D + 2 * GROUPS * P) // P), whole("w_z", SSD_D // P), merge("c", 2), merge("b", 1),
            whole("w_conf", 2 * CONF_D // P), whole("w_sc", 3 * SC_D // P), merge("a", 0), merge("d", 3)]


def build_program(nc, a):
    for name, shape in SCRATCH.items():
        if name not in a:
            a[name] = nc.dram_tensor(name, shape, F32).ap()
    with ExitStack() as ctx:
        k = Kernel(nc, a, ctx)
        k.ring.plan([(n, source) for _, n, source in weight_segments(a)])
        filter_stages(k)
        merged = k.resident(ctx)("merged", [P, KT, T])
        with ExitStack() as branches:
            y_cT = k.resident(branches)("y_cT", [P, HY_D // P, T])
            y_cT_rest = twin(nc, "y_cT", [P, HY_D // P, T])
            hyena_stages(k, y_cT, merged)
            y = k.spare[:, :, 0:SSD_D]
            ssd_scan_stages(k, y)
            y_bT = k.resident(branches)("y_bT", [P, SSD_D // P, T])
            y_bT_rest = twin(nc, "y_bT", [P, SSD_D // P, T])
            stage_ssd_norm(k, y, y_bT)
            stage_merge(k, "mc", y_cT, y_cT_rest, HY_D // P, merged, first=True, split_u=True)
            stage_merge(k, "mb", y_bT, y_bT_rest, SSD_D // P, merged, first=False, split_u=False)
        with ExitStack() as branches:
            sb = k.resident(branches)
            y_aT = sb("y_aT", [P, CONF_D // P, T])
            y_aT_rest = twin(nc, "y_aT", [P, CONF_D // P, T])
            y_dT = sb("y_dT", [P, SC_D // P, T])
            y_dT_rest = twin(nc, "y_dT", [P, SC_D // P, T])
            stage_conformer_short(k, y_aT, y_dT)
            stage_merge(k, "ma", y_aT, y_aT_rest, CONF_D // P, merged, first=False, split_u=False)
            stage_merge(k, "md", y_dT, y_dT_rest, SC_D // P, merged, first=False, split_u=False)
        tail_stages(k, merged)


def kernel(**inputs):
    import concourse.bacc as bacc
    from concourse.bass_utils import run_bass_kernel_spmd

    arrays = {f"in_{name}": v for name, v in
              host_arrays(**{name: np.asarray(v) for name, v in inputs.items()}).items()}
    nc = bacc.Bacc("TRN2", target_bir_lowering=False, num_devices=1)
    a = {name[3:]: nc.dram_tensor(name, v.shape, mybir.dt.from_np(v.dtype), kind="ExternalInput").ap()
         for name, v in arrays.items()}
    a["out"] = nc.dram_tensor("out_dram", (T, D), F32, kind="ExternalOutput").ap()
    build_program(nc, a)
    r = run_bass_kernel_spmd(nc, [arrays], core_ids=[0])
    return r.results[0]["out_dram"].reshape(1, T, D)
```
